# Optimizing a Trainium2 kernel written in Bass

```python
import math
import jax, jax.numpy as jnp
from jax import lax
import numpy as np

D_MODEL = 1024
BATCH = 1
SEQ = 512
DEPTH = 2
DEC_BATCH = 8
DEC_SEQ = 1
PAST_LEN = 2048
PAGE_SIZE = 128

N_A_LAYERS = DEPTH // 2
N_B_LAYERS = DEPTH - N_A_LAYERS
GLA_HEADS = 4
GLA_DK = D_MODEL // 2 // GLA_HEADS
GLA_DV = D_MODEL // GLA_HEADS
GLA_GATE_RANK = 16
GLA_GATE_NORM = 16.0
GLA_CHUNK = 64
MLA_HEADS = 8
MLA_Q_RANK = 3 * D_MODEL // 8
MLA_KV_RANK = D_MODEL // 4
MLA_NOPE = 64
MLA_ROPE = 32
MLA_QK = MLA_NOPE + MLA_ROPE
MLA_V = 64
ROPE_THETA = 10000.0
Q_BLOCK = 128
MOE_GROUPS = 4
MOE_EXP_PER_GROUP = 4
MOE_EXPERTS = MOE_GROUPS * MOE_EXP_PER_GROUP
MOE_TOP_K = 2
MOE_D_FF = D_MODEL // 4
NORM_EPS = 1e-6

kernel_name = 'yoco_gla_mla_hmoe_step'

F32 = jnp.float32

def rms_norm(x, g):
    xf = x.astype(F32)
    y = xf * lax.rsqrt(jnp.mean(xf * xf, axis=-1, keepdims=True) + NORM_EPS)
    return (y * g.astype(F32)).astype(x.dtype)

def rope_tables(pos):
    inv = ROPE_THETA ** (-jnp.arange(0, MLA_ROPE, 2, dtype=F32) / MLA_ROPE)
    ang = pos.astype(F32)[:, None] * inv[None, :]
    ang = jnp.concatenate([ang, ang], axis=-1)
    return jnp.cos(ang), jnp.sin(ang)

def apply_rope(x, cos, sin):
    half = x.shape[-1] // 2
    xf = x.astype(F32)
    rot = jnp.concatenate([-xf[..., half:], xf[..., :half]], axis=-1)
    return (xf * cos + rot * sin).astype(x.dtype)

def gla_recurrence(q, k, v, gk, s0):
    bsz, L, H, dk = q.shape
    dv = v.shape[-1]
    C = math.gcd(L, GLA_CHUNK)
    n = L // C

    def chunks(t):
        return t.astype(F32).reshape(bsz, n, C, H, t.shape[-1]).transpose(1, 0, 3, 2, 4)

    causal = jnp.tril(jnp.ones((C, C), dtype=bool))[:, :, None]

    def step(S, inp):
        qc, kc, vc, gc = inp
        b = jnp.cumsum(gc, axis=2)
        diff = b[:, :, :, None, :] - b[:, :, None, :, :]
        decay = jnp.exp(jnp.where(causal, diff, -jnp.inf))
        attn = jnp.einsum('bhtd,bhsd,bhtsd->bhts', qc, kc, decay)
        o = (jnp.einsum('bhts,bhsv->bhtv', attn, vc)
             + jnp.einsum('bhtd,bhdv->bhtv', qc * jnp.exp(b), S))
        b_last = b[:, :, -1:, :]
        S_new = (S * jnp.exp(b_last[:, :, 0, :])[..., None]
                 + jnp.einsum('bhsd,bhsv->bhdv', kc * jnp.exp(b_last - b), vc))
        return S_new, o

    s_fin, o = lax.scan(step, s0.astype(F32), (chunks(q), chunks(k), chunks(v), chunks(gk)))
    o = o.transpose(1, 0, 3, 2, 4).reshape(bsz, L, H, dv)
    return o, s_fin

def gla_mix(h, w_in, w_gate_up, b_gate, out_norm, w_out, s0):
    bsz, L, _ = h.shape
    hk = GLA_HEADS * GLA_DK
    hv = GLA_HEADS * GLA_DV
    proj = h @ w_in
    q, k, v, r, g_low = jnp.split(proj, [hk, 2 * hk, 2 * hk + hv, 2 * hk + 2 * hv], axis=-1)
    gk = jax.nn.log_sigmoid((g_low @ w_gate_up + b_gate).astype(F32)) / GLA_GATE_NORM

    def heads(t, d):
        return t.reshape(bsz, L, GLA_HEADS, d)

    o, s_fin = gla_recurrence(heads(q, GLA_DK) * (GLA_DK ** -0.5), heads(k, GLA_DK),
                              heads(v, GLA_DV), heads(gk, GLA_DK), s0)
    o = rms_norm(o, out_norm) * jax.nn.silu(heads(r, GLA_DV).astype(F32))
    return o.reshape(bsz, L, hv).astype(h.dtype) @ w_out, s_fin.astype(s0.dtype)

def mla_queries(h, w_dq, q_lat_norm, w_uq, q_norm, cos, sin):
    bsz, L, _ = h.shape
    cq = rms_norm(h @ w_dq, q_lat_norm)
    q = (cq @ w_uq).reshape(bsz, L, MLA_HEADS, MLA_QK)
    q = jnp.concatenate([q[..., :MLA_NOPE], apply_rope(q[..., MLA_NOPE:], cos[:, None, :], sin[:, None, :])], axis=-1)
    return rms_norm(q, q_norm)

def mla_shared_kv(s, kv_in_norm, w_dkv, kv_lat_norm, cos, sin):
    kv = rms_norm(s, kv_in_norm) @ w_dkv
    ckv = rms_norm(kv[..., :MLA_KV_RANK], kv_lat_norm)
    kr = apply_rope(kv[..., MLA_KV_RANK:], cos, sin)
    return ckv, kr

def mla_keys(ckv, kr, w_uk, k_norm):
    kn = jnp.einsum('...pr,rhd->...phd', ckv, w_uk)
    krb = jnp.broadcast_to(kr[..., None, :], kn.shape[:-1] + (MLA_ROPE,))
    return rms_norm(jnp.concatenate([kn, krb], axis=-1), k_norm)

def mla_attend_prompt(q, ckv, kr, w_uk, w_uv, k_norm):
    bsz, S, H, _ = q.shape
    k = mla_keys(ckv, kr, w_uk, k_norm)
    v = jnp.einsum('bsr,rhd->bshd', ckv, w_uv)
    nb = S // Q_BLOCK
    qb = q.reshape(bsz, nb, Q_BLOCK, H, MLA_QK).transpose(1, 0, 2, 3, 4)
    key_pos = jnp.arange(S)
    scale = MLA_QK ** -0.5

    def block(args):
        qi, i = args
        s = jnp.einsum('bqhd,bkhd->bhqk', qi, k).astype(F32) * scale
        qpos = i * Q_BLOCK + jnp.arange(Q_BLOCK)
        s = jnp.where(key_pos[None, :] <= qpos[:, None], s, -jnp.inf)
        p = jax.nn.softmax(s, axis=-1)
        return jnp.einsum('bhqk,bkhd->bqhd', p.astype(v.dtype), v)

    o = lax.map(block, (qb, jnp.arange(nb)))
    return o.transpose(1, 0, 2, 3, 4).reshape(bsz, S, H, MLA_V)

def mla_attend_sample(q, ckv_new, kr_new, cache_ckv, cache_krope, page_table, w_uk, w_uv, k_norm):
    db, L, H, _ = q.shape
    qf = q.astype(F32)
    scale = MLA_QK ** -0.5

    def page_step(carry, page_ids):
        m, l, acc = carry
        c = cache_ckv[page_ids]
        kr = cache_krope[page_ids]
        k = mla_keys(c, kr, w_uk, k_norm)
        s = jnp.einsum('bqhd,bphd->bqhp', qf, k.astype(F32)) * scale
        m_new = jnp.maximum(m, jnp.max(s, axis=-1))
        corr = jnp.exp(m - m_new)
        p = jnp.exp(s - m_new[..., None])
        l = l * corr + jnp.sum(p, axis=-1)
        acc = acc * corr[..., None] + jnp.einsum('bqhp,bpr->bqhr', p, c.astype(F32))
        return (m_new, l, acc), None

    init = (jnp.full((db, L, H), -jnp.inf, F32), jnp.zeros((db, L, H), F32),
            jnp.zeros((db, L, H, MLA_KV_RANK), F32))
    (m, l, acc), _ = lax.scan(page_step, init, page_table.T)
    k_new = mla_keys(ckv_new, kr_new, w_uk, k_norm)
    s = jnp.einsum('bqhd,bkhd->bqhk', qf, k_new.astype(F32)) * scale
    causal = jnp.tril(jnp.ones((L, L), dtype=bool))[None, :, None, :]
    s = jnp.where(causal, s, -jnp.inf)
    m_new = jnp.maximum(m, jnp.max(s, axis=-1))
    corr = jnp.exp(m - m_new)
    p = jnp.exp(s - m_new[..., None])
    l = l * corr + jnp.sum(p, axis=-1)
    acc = acc * corr[..., None] + jnp.einsum('bqhk,bkr->bqhr', p, ckv_new.astype(F32))
    o_lat = acc / l[..., None]
    return jnp.einsum('bqhr,rhd->bqhd', o_lat, w_uv.astype(F32)).astype(q.dtype)

def hier_moe(h, w_group, b_group, w_router, b_router, w_gate, w_up, w_down):
    bsz, L, D = h.shape
    t = h.reshape(bsz * L, D)
    p_group = jax.nn.softmax((t @ w_group + b_group).astype(F32), axis=-1)
    g_val, g_idx = lax.top_k(p_group, 1)
    g_onehot = jax.nn.one_hot(g_idx[:, 0], MOE_GROUPS, dtype=F32)
    logits_e = (t @ w_router + b_router).astype(F32).reshape(-1, MOE_GROUPS, MOE_EXP_PER_GROUP)
    p_e = jax.nn.softmax(jnp.einsum('tg,tge->te', g_onehot, logits_e), axis=-1)
    e_val, e_idx = lax.top_k(p_e, MOE_TOP_K)
    w_sel = g_val * e_val / jnp.sum(e_val, axis=-1, keepdims=True)
    expert_id = g_idx * MOE_EXP_PER_GROUP + e_idx
    gates = jnp.einsum('tk,tke->te', w_sel, jax.nn.one_hot(expert_id, MOE_EXPERTS, dtype=F32))
    hid = jax.nn.silu(jnp.einsum('td,edf->tef', t, w_gate)) * jnp.einsum('td,edf->tef', t, w_up)
    y = jnp.einsum('tef,efd->td', hid * gates[..., None].astype(hid.dtype), w_down)
    return y.reshape(bsz, L, D)

def trunk(x, c, pos, gla_state_in, paged, w):
    bsz, L, _ = x.shape
    cos, sin = rope_tables(pos)
    ckv = kr = None
    new_gla = []
    for l in range(DEPTH):
        mod = (jax.nn.silu(c) @ w['ada_w'][l] + w['ada_b'][l])[:, None, :]
        sh_a, sc_a, g_a, sh_f, sc_f, g_f = jnp.split(mod, 6, axis=-1)
        hm = rms_norm(x, w['mix_norm'][l]) * (1.0 + sc_a) + sh_a
        if l < N_A_LAYERS:
            a = l
            m, st = gla_mix(hm, w['gla_w_in'][a], w['gla_w_gate_up'][a], w['gla_b_gate'][a],
                            w['gla_out_norm'][a], w['gla_w_out'][a], gla_state_in[a])
            new_gla.append(st)
        else:
            b = l - N_A_LAYERS
            q = mla_queries(hm, w['mla_w_dq'][b], w['mla_q_lat_norm'][b], w['mla_w_uq'][b],
                            w['mla_q_norm'][b], cos, sin)
            if paged is None:
                o = mla_attend_prompt(q, ckv, kr, w['kv_w_uk'], w['kv_w_uv'], w['kv_k_norm'])
            else:
                o = mla_attend_sample(q, ckv, kr, paged[0], paged[1], paged[2],
                                      w['kv_w_uk'], w['kv_w_uv'], w['kv_k_norm'])
            m = o.reshape(bsz, L, MLA_HEADS * MLA_V) @ w['mla_w_out'][b]
        x = x + g_a * m
        hf = rms_norm(x, w['ffn_norm'][l]) * (1.0 + sc_f) + sh_f
        x = x + g_f * hier_moe(hf, w['moe_w_group'][l], w['moe_b_group'][l], w['moe_w_router'][l],
                               w['moe_b_router'][l], w['moe_w_gate'][l], w['moe_w_up'][l], w['moe_w_down'][l])
        if l == N_A_LAYERS - 1:
            ckv, kr = mla_shared_kv(x, w['kv_in_norm'], w['kv_w_dkv'], w['kv_lat_norm'], cos, sin)
    return x, jnp.stack(new_gla, axis=0), ckv, kr

def setup_inputs(seed: int = 0) -> dict:
    key = jax.random.key(seed)
    ks = iter(jax.random.split(key, 64))

    def nrm(shape, scale):
        return jax.random.normal(next(ks), shape, F32) * scale

    def gain(shape):
        return 1.0 + nrm(shape, 0.02)

    n_pages = PAST_LEN // PAGE_SIZE
    n_used = DEC_BATCH * n_pages
    n_pool = n_used + max(1, n_used // 4)
    page_table = jax.random.permutation(next(ks), n_pool)[:n_used].reshape(DEC_BATCH, n_pages).astype(jnp.int32)
    D = D_MODEL
    gla_in = 2 * GLA_HEADS * GLA_DK + 2 * GLA_HEADS * GLA_DV + GLA_GATE_RANK
    return {
        'x_prompt': nrm((BATCH, SEQ, D), 1.0),
        'x_sample': nrm((DEC_BATCH, DEC_SEQ, D), 1.0),
        'c_prompt': nrm((BATCH, D), 1.0),
        'c_sample': nrm((DEC_BATCH, D), 1.0),
        'state_gla': nrm((N_A_LAYERS, DEC_BATCH, GLA_HEADS, GLA_DK, GLA_DV), 0.5),
        'cache_ckv': nrm((n_pool, PAGE_SIZE, MLA_KV_RANK), 1.0),
        'cache_krope': nrm((n_pool, PAGE_SIZE, MLA_ROPE), 1.0),
        'page_table': page_table,
        'ada_w': nrm((DEPTH, D, 6 * D), 0.5 * D ** -0.5),
        'ada_b': nrm((DEPTH, 6 * D), 0.02),
        'mix_norm': gain((DEPTH, D)),
        'ffn_norm': gain((DEPTH, D)),
        'gla_w_in': nrm((N_A_LAYERS, D, gla_in), D ** -0.5),
        'gla_w_gate_up': nrm((N_A_LAYERS, GLA_GATE_RANK, GLA_HEADS * GLA_DK), GLA_GATE_RANK ** -0.5),
        'gla_b_gate': nrm((N_A_LAYERS, GLA_HEADS * GLA_DK), 0.1),
        'gla_out_norm': gain((N_A_LAYERS, GLA_DV)),
        'gla_w_out': nrm((N_A_LAYERS, GLA_HEADS * GLA_DV, D), (GLA_HEADS * GLA_DV) ** -0.5),
        'mla_w_dq': nrm((N_B_LAYERS, D, MLA_Q_RANK), D ** -0.5),
        'mla_q_lat_norm': gain((N_B_LAYERS, MLA_Q_RANK)),
        'mla_w_uq': nrm((N_B_LAYERS, MLA_Q_RANK, MLA_HEADS * MLA_QK), MLA_Q_RANK ** -0.5),
        'mla_q_norm': gain((N_B_LAYERS, MLA_QK)),
        'mla_w_out': nrm((N_B_LAYERS, MLA_HEADS * MLA_V, D), (MLA_HEADS * MLA_V) ** -0.5),
        'kv_in_norm': gain((D,)),
        'kv_w_dkv': nrm((D, MLA_KV_RANK + MLA_ROPE), D ** -0.5),
        'kv_lat_norm': gain((MLA_KV_RANK,)),
        'kv_w_uk': nrm((MLA_KV_RANK, MLA_HEADS, MLA_NOPE), MLA_KV_RANK ** -0.5),
        'kv_w_uv': nrm((MLA_KV_RANK, MLA_HEADS, MLA_V), MLA_KV_RANK ** -0.5),
        'kv_k_norm': gain((MLA_QK,)),
        'moe_w_group': nrm((DEPTH, D, MOE_GROUPS), D ** -0.5),
        'moe_b_group': nrm((DEPTH, MOE_GROUPS), 0.01),
        'moe_w_router': nrm((DEPTH, D, MOE_EXPERTS), D ** -0.5),
        'moe_b_router': nrm((DEPTH, MOE_EXPERTS), 0.01),
        'moe_w_gate': nrm((DEPTH, MOE_EXPERTS, D, MOE_D_FF), D ** -0.5),
        'moe_w_up': nrm((DEPTH, MOE_EXPERTS, D, MOE_D_FF), D ** -0.5),
        'moe_w_down': nrm((DEPTH, MOE_EXPERTS, MOE_D_FF, D), MOE_D_FF ** -0.5),
    }

def reference(x_prompt, x_sample, c_prompt, c_sample, state_gla, cache_ckv, cache_krope, page_table,
              ada_w, ada_b, mix_norm, ffn_norm,
              gla_w_in, gla_w_gate_up, gla_b_gate, gla_out_norm, gla_w_out,
              mla_w_dq, mla_q_lat_norm, mla_w_uq, mla_q_norm, mla_w_out,
              kv_in_norm, kv_w_dkv, kv_lat_norm, kv_w_uk, kv_w_uv, kv_k_norm,
              moe_w_group, moe_b_group, moe_w_router, moe_b_router, moe_w_gate, moe_w_up, moe_w_down):
    w = dict(ada_w=ada_w, ada_b=ada_b, mix_norm=mix_norm, ffn_norm=ffn_norm,
             gla_w_in=gla_w_in, gla_w_gate_up=gla_w_gate_up, gla_b_gate=gla_b_gate,
             gla_out_norm=gla_out_norm, gla_w_out=gla_w_out,
             mla_w_dq=mla_w_dq, mla_q_lat_norm=mla_q_lat_norm, mla_w_uq=mla_w_uq,
             mla_q_norm=mla_q_norm, mla_w_out=mla_w_out,
             kv_in_norm=kv_in_norm, kv_w_dkv=kv_w_dkv, kv_lat_norm=kv_lat_norm,
             kv_w_uk=kv_w_uk, kv_w_uv=kv_w_uv, kv_k_norm=kv_k_norm,
             moe_w_group=moe_w_group, moe_b_group=moe_b_group, moe_w_router=moe_w_router,
             moe_b_router=moe_b_router, moe_w_gate=moe_w_gate, moe_w_up=moe_w_up, moe_w_down=moe_w_down)
    gla_zero = jnp.zeros((N_A_LAYERS, x_prompt.shape[0], GLA_HEADS, GLA_DK, GLA_DV), state_gla.dtype)
    y_prompt, state_gla_prompt, ckv_prompt, krope_prompt = trunk(
        x_prompt, c_prompt, jnp.arange(SEQ), gla_zero, None, w)
    y_sample, state_gla_sample, ckv_sample, krope_sample = trunk(
        x_sample, c_sample, PAST_LEN + jnp.arange(DEC_SEQ), state_gla,
        (cache_ckv, cache_krope, page_table), w)
    return (y_prompt, y_sample, state_gla_prompt, state_gla_sample, ckv_prompt, krope_prompt, ckv_sample, krope_sample)


_drawn_inputs = setup_inputs


def setup_inputs(seed=0):
    import zlib

    import numpy as np

    out = dict(_drawn_inputs(seed))
    spreads = {}
    factors = {'cache_ckv': 3.994,
     'cache_krope': 8.0,
     'ffn_norm': 4.653,
     'gla_out_norm': 8.0,
     'mla_q_lat_norm': 8.0,
     'mla_q_norm': 8.0,
     'kv_k_norm': 8.0,
     'moe_b_group': 8.0,
     'moe_b_router': 6.054}
    for name, (base, spread) in spreads.items():
        noise = np.random.default_rng([zlib.crc32(name.encode()), seed]).standard_normal(out[name].shape)
        drawn = base * np.exp(spread * noise) if base else spread * noise
        out[name] = __import__('jax').numpy.asarray(drawn.astype(out[name].dtype))
    for name, factor in factors.items():
        out[name] = (out[name] * factor).astype(out[name].dtype)
    return out
```

```python
from contextlib import ExitStack, contextmanager

import numpy as np
import concourse.bass as bass
from concourse import mybir

F32 = mybir.dt.float32
I32 = mybir.dt.int32
ALU = mybir.AluOpType
ACT = mybir.ActivationFunctionType
AX = mybir.AxisListType

P = 128
D = 1024
KD = D // P
NP, NS = 512, 8
T = NP + NS
HT = T // 2
QT = NP // P
EPS = 1e-6
GH, DK, DV, GR = 4, 128, 256, 16
C = 64
NC = NP // C
MH, NOPE, ROPE, MV = 8, 64, 32, 64
QK = NOPE + ROPE
QR, KVR = 384, 256
PAST, PAGE = 2048, 128
NPG = PAST // PAGE
PSL = 8
PROW = KVR + ROPE
NE, NG, NEG, FF = 16, 4, 4, 256
BIG = 1.0e30
SLOTS = 4

ID, ONE, O1024, O256, O384, TRI, SCAN, RANK = 0, 128, 256, 384, 512, 640, 704, 1216
NCONST = 1220
B64, B32, E0, F0, K1, ROT, CAUS, COS, SIN = 0, 128, 256, 512, 768, 896, 1024, 1152, 1672
NCONST2 = 2192
MIXN, FFNN, ADAB, GBIAS, ONORM, KVIN, QLAT, KVLAT, QNN, QNR, KNN, KNR = 0, 16, 32, 128, 132, 134, 142, 145, 147, 148, 149, 150
NVEC = 151


def constant_tables():
    c = np.zeros((P, NCONST), np.float32)
    c[:, ID:ID + P] = np.eye(P)
    c[:, ONE:ONE + P] = 1.0
    c[:, O1024:O1024 + P] = 1.0 / D
    c[:, O256:O256 + P] = 1.0 / 256
    c[:, O384:O384 + P] = 1.0 / QR
    p = np.arange(P)
    c[:, TRI:TRI + C] = np.arange(C)[None, :] >= (p % C)[:, None]
    c[:, SCAN:SCAN + NP] = (np.arange(NP) % C != 0)[None, :]
    c[:, RANK:RANK + 4] = np.array([4.0, 3.0, 2.0, 1.0])
    m = np.zeros((P, NCONST2), np.float32)
    one = np.float32(1.0 / QK)
    half, quarter = p // NOPE, p // ROPE
    m[:, B64:B64 + P] = (half[:, None] == half[None, :]) * one
    m[:, B32:B32 + P] = (quarter[:, None] == quarter[None, :]) * one
    for u in range(2):
        m[:, E0 + u * P:E0 + (u + 1) * P] = (half[:, None] + 2 * u == quarter[None, :]) * one
        m[:, F0 + u * P:F0 + (u + 1) * P] = (quarter[:, None] == half[None, :] + 2 * u) * one
    m[:, K1:K1 + P] = (p < ROPE)[:, None] * one
    for i in range(P):
        j = i + ROPE // 2 if i % ROPE < ROPE // 2 else i - ROPE // 2
        m[j, ROT + i] = -1.0 if i % ROPE < ROPE // 2 else 1.0
    m[:, CAUS:CAUS + P] = np.where(p[None, :] <= p[:, None], 0.0, -BIG)
    inv = (np.float32(10000.0) ** (-np.arange(0, ROPE, 2, dtype=np.float32) / np.float32(ROPE))).astype(np.float32)
    pos = np.concatenate([np.arange(NP), np.full(NS, PAST)]).astype(np.float32)
    ang = (pos[:, None] * inv[None, :]).astype(np.float32)
    ang = np.tile(np.concatenate([ang, ang], axis=1), (1, P // ROPE)).T
    m[:, COS:COS + T] = np.cos(ang)
    m[:, SIN:SIN + T] = np.sin(ang)
    return c, m


STAGES = [("ada", 24), ("norm0", 1), ("qk", 8), ("glow", 1), ("gup", 4), ("v", 5), ("onorm", 4), ("r", 8), ("gout", 8)]
for _l in (0, 1):
    if _l:
        STAGES += [("kvnorm", 1), ("dkv", 3), ("ckvnorm", 1), ("krot", 1), ("norm2", 1), ("dq", 3), ("cqnorm", 1),
                   ("uq", 6), ("qrot", 2), ("qss", 6), ("uk", 4), ("kss", 6), ("uv", 4), ("mout", 8)]
    STAGES += [(f"fnorm{_l}", 1), (f"route{_l}", 1), (f"gt{_l}", 1), (f"moe{_l}", NE * 12)]
FIRST = {}
_n = 0
for _s, _k in STAGES:
    FIRST[_s] = _n
    _n += _k

RING = {f"ada{j}": (j % SLOTS, j // SLOTS + 1) for j in range(24)}
_use = [6] * SLOTS
for _name, _slot in (("wq", 0), ("wk", 1), ("wv0", 2), ("wv1", 3), ("wr0", 0), ("wr1", 1), ("wo0", 2), ("wo1", 3),
                     ("moe0", None), ("dkv", 0), ("dq", 1), ("uq", 2), ("ukv", 3), ("mwo", 0), ("moe1", None)):
    if _slot is None:
        for _s in range(SLOTS):
            RING[f"{_name}_{_s}"] = (_s, _use[_s] + 1)
            _use[_s] += NE // 2
        continue
    _use[_slot] += 1
    RING[_name] = (_slot, _use[_slot])


class Turn:

    def __init__(self, stage):
        self.n, self.off = FIRST[stage], 0

    def count(self):
        return self.n + 1 + self.off

    def slot(self):
        return self.n % SLOTS


class Order:

    def __init__(self, eng, own):
        self.eng, self.own, self.c, self.open = eng, own, {}, []
        self.i, self.per = None, {}

    def value(self, sem):
        v = self.c[sem.name]
        return v if self.i is None else v + self.i * self.per.get(sem.name, 0)

    def __call__(self, ins, sem=None, hold=True):
        sem = sem or self.own
        self.c[sem.name] = self.c.get(sem.name, 0) + 1
        ins.then_inc(sem, 1)
        if sem not in self.open:
            self.open.append(sem)
        if hold:
            self.settle()

    def settle(self):
        for sem in self.open:
            self.eng.wait_ge(sem, self.value(sem))
        self.open = []

    @contextmanager
    def loop(self, trips, per):
        per = {s.name: k for s, k in per}
        start = dict(self.c)
        with self.eng.Fori(0, trips) as i:
            self.i, self.per = i, per
            yield i
            self.settle()
        self.i = None
        for name in set(self.c) | set(per):
            got = self.c.get(name, 0) - start.get(name, 0)
            assert got == per.get(name, 0), (name, got, per)
            self.c[name] = start.get(name, 0) + trips * got


def trunk_program(nc, io):
    with ExitStack() as ctx:
        def sb(name, shape, dt=F32):
            return ctx.enter_context(nc.sbuf_tensor(name, shape, dt))

        def sem(name):
            return ctx.enter_context(nc.semaphore(name))

        PS = ctx.enter_context(nc.psum_tensor("PS", [P, 8, 512], F32))
        CONST = sb("CONST", [P, NCONST])
        VEC = sb("VEC", [P, NVEC])
        WRT = sb("WRT", [P, 2, KD, NG + NE])
        BRT = sb("BRT", [P, 2, NG + NE])
        PTB = sb("PTB", [1, NS * NPG], I32)
        EPST = sb("EPST", [P, 1])
        CT = sb("CT", [P, KD, 1 + NS])
        MOD = sb("MOD", [P, 2 * 6 * KD, 1 + NS])
        AM = sb("AM", [P, KD, 1 + NS])
        TS = sb("TS", [P, 2 * NS])
        RS = sb("RS", [P, 2, T])
        X = sb("X", [P, KD, T])
        H = sb("H", [P, KD, T])
        QB = sb("QB", [P, KD, T])
        O = sb("O", [P, KD, T])
        BE = sb("BE", [P, KD, T])
        VV = sb("VV", [P, 4096])
        VS = sb("VS", [NS, GH * DV])
        AT = sb("AT", [P, 1024])
        SST = sb("SST", [P, 3072])
        WB = sb("WB", [P, SLOTS, 4096])

        def ident(a=P, b=P, p=0, c=0):
            return CONST[p:p + a, ID + c:ID + c + b]

        def const(col, n=P, lo=0, hi=P):
            return CONST[lo:hi, col:col + n]

        def const2(col, n=P, lo=0, hi=P):
            return SST[lo:hi, col:col + n]

        B = BE[:, 0:4, :]
        E = BE[:, 4:8, :]
        EF = E.rearrange("p a b -> p (a b)")
        HF = H[:, :, :].rearrange("p a b -> p (a b)")
        V = VV[:, :].rearrange("p (t n) -> p t n", t=4)
        CKV = VV[:, 0:3 * T].rearrange("p (k t) -> p k t", k=3)
        VP = VV[:, 3 * T:3 * T + 2048].rearrange("p (k n) -> p k n", k=4)
        KRT = VV[0:ROPE, 3 * T:3 * T + PSL * PAGE].rearrange("p (k n) -> p k n", k=PSL)
        S = SST[:, 0:1024]
        ST = SST[:, 1024:3072].rearrange("p (b n) -> p b n", b=2)
        PG = SST[:, 0:PSL * PROW].rearrange("p (k n) -> p k n", k=PSL)
        CN = SST[:, 0:PSL * KVR].rearrange("p (k n) -> p k n", k=PSL)

        def two(ap):
            return ap.rearrange("p (a b) -> p a b", a=2)

        def halves(s, m=P):
            return PS[0:m, 2 * s:2 * s + 2, 0:HT]

        psum_full, psum_free = sem("psum_full"), sem("psum_free")
        ring_full = [sem(f"ring_full{s}") for s in range(SLOTS)]
        ring_free = [sem(f"ring_free{s}") for s in range(SLOTS)]
        consts_in, x_in, mla_consts_in = sem("consts_in"), sem("x_in"), sem("mla_consts_in")
        gate_up_in, pages_in = sem("gate_up_in"), sem("page_table_in")
        vec_order, act_order = sem("vec_order"), sem("act_order")
        cond_silu, attn_ready = sem("cond_silu"), sem("attn_ready")
        sq_ready, rms_ready, h_ready = sem("sq_ready"), sem("rms_ready"), sem("h_ready")
        glow_ready, softplus_ready, decay_ready, exp_ready = (sem("glow_ready"), sem("softplus_ready"),
                                                              sem("decay_ready"), sem("exp_ready"))
        decayed, prep_full, prep_done = sem("decayed"), sem("prep_full"), sem("prep_done")
        o_full, o_taken, state_ready = sem("gla_o_full"), sem("gla_o_taken"), sem("state_ready")
        ks_full, km_ready, outer_full, snew_ready, os_full = (sem("ks_full"), sem("km_ready"), sem("outer_full"),
                                                              sem("snew_ready"), sem("os_full"))
        st_in = [sem(f"st_in{b}") for b in range(2)]
        st_out = [sem(f"st_out{b}") for b in range(2)]
        y_stored = sem("y_stored")
        stored, silu_ready = sem("stored"), sem("silu_ready")
        route_exp_in, route_exp = sem("route_exp_in"), sem("route_exp")
        gates_ready, gt_ready, gt_stored = sem("gates_ready"), sem("gt_ready"), sem("gt_stored")
        row_in = [sem(f"gate_row_in{b}") for b in range(2)]
        lat_ready, kr_ready, rope_ready = sem("lat_ready"), sem("kr_ready"), sem("rope_ready")
        sc_full, negmax_ready, exp_done, p_ready = sem("sc_full"), sem("negmax_ready"), sem("exp_done"), sem("p_ready")
        pt_full, pt_ready, pv_full, pv_done = sem("pt_full"), sem("pt_ready"), sem("pv_full"), sem("pv_done")
        qp_ready, ql_full, ql_ready = sem("qp_ready"), sem("ql_full"), sem("ql_ready")
        page_in = [sem(f"page_in{s}") for s in range(PSL)]
        page_used, scores_taken, kn_full, page_sq = (sem("page_used"), sem("scores_taken"), sem("kn_full"),
                                                     sem("page_sq"))
        ssq_ready, krstd_ready, max_ready, max_full, shifted, p_exp = (sem("ssq_ready"), sem("krstd_ready"),
                                                                      sem("max_ready"), sem("max_full"),
                                                                      sem("shifted"), sem("p_exp"))
        sum_ready, sum_full, cpage_used, acc_full, acc_taken = (sem("sum_ready"), sem("sum_full"),
                                                                sem("cpage_used"), sem("acc_full"),
                                                                sem("acc_taken"))
        olat_ready, osam_full, y_ready = sem("olat_ready"), sem("osam_full"), sem("y_ready")

        SQ = {s: n + 1 for n, s in enumerate(["norm0", "onorm", "fnorm0", "kvnorm", "ckvnorm", "norm2", "cqnorm",
                                              "qss", "kss", "fnorm1"])}
        RMS, n = {}, 0
        for s, k in (("norm0", 1), ("onorm", 4), ("fnorm0", 1), ("kvnorm", 1), ("ckvnorm", 1), ("norm2", 1),
                     ("cqnorm", 1), ("qss", 6), ("kss", 6), ("fnorm1", 1)):
            RMS[s] = n
            n += k
        HR = {"norm0": 9, "fnorm0": 18, "kvnorm": 26, "norm2": 35, "fnorm1": 44}
        SCALE = float(QK) ** -0.5
        LAYERS = ("moe0", "moe1")

        WGU, WG = AT[0:GR, 0:512], AT[:, 512:640].rearrange("p (k n) -> p k n", k=KD)
        BM, BL, FE = (SST[:, 1024 + 32 * i:1056 + 32 * i].rearrange("p (h c) -> p h c", h=GH) for i in range(3))
        QP, PR = (AT[:, 48 * i:48 * i + 48].rearrange("p (k s) -> p k s", k=6) for i in range(2))
        QL = AT[:, 96:224].rearrange("p (r s h) -> p r s h", r=2, s=NS)
        QRS = AT[0:ROPE, 224:288].rearrange("p (s h) -> p s h", s=NS)
        NEW, KRS, MX, LS, DG = AT[:, 288:352], AT[:, 352:480], AT[:, 480:544], AT[:, 544:608], AT[0:64, 608:672]
        OL = AT[:, 688:816].rearrange("p (r s h) -> p r s h", r=2, s=NS)
        RLS, PNB, MC = AT[:, 816:880], AT[:, 880:944], AT[0:64, 672:673]
        SC, SSQ = HF[:, 0:1024], HF[:, 1024:2048]
        SQP = HF[:, 2048:4096].rearrange("p (b n) -> p b n", b=4)
        LOG = AT[:, 0:100].rearrange("p (q n) -> p q n", q=5)
        GX, OHG, OH1, OH2, LE, TMP = (AT[:, 100 + 20 * i:120 + 20 * i].rearrange("p (q n) -> p q n", q=5)
                                      for i in range(6))
        M1, M2, M3, X2 = (AT[:, 220 + 5 * i:225 + 5 * i] for i in range(4))
        GATES = AT[:, 256:336].rearrange("p (q g e) -> p q g e", q=5, g=NG)
        SEL = AT[:, 336:416].rearrange("p (q g e) -> p q g e", q=5, g=NG)
        NM, LN = TS[:, 0:2], TS[:, 2:4]

        block = ctx.enter_context(nc.Block())

        @block.sync
        def _(sp):
            sp.dma_start(CT[:, :, :], io["c"]).then_inc(consts_in, 16)
            sp.dma_start(VEC[:, :], io["vec"]).then_inc(consts_in, 16)

            def load(name, src, part=None, last=True):
                slot, use = RING[name]
                dst = WB[:, slot, :] if part is None else WB[:, slot, part[0]:part[1]]
                if use > 1:
                    sp.wait_ge(ring_free[slot], use - 1)
                sp.dma_start(dst, src).then_inc(ring_full[slot], 16)

            for j in range(SLOTS):
                load(f"ada{j}", io["ada"][0, j])
            sp.dma_start(X[:, :, :], io["x"]).then_inc(x_in, 16)
            sp.dma_start(CONST[:, :], io["const"]).then_inc(x_in, 16)
            sp.dma_start(WRT[:, :, :, :], io["router"]).then_inc(x_in, 16)
            sp.dma_start(BRT[:, :, :], io["router_b"].partition_broadcast(P)).then_inc(x_in, 16)
            sp.dma_start(WGU, io["gate_up"]).then_inc(gate_up_in, 16)
            sp.dma_start(WG, io["gate_low"]).then_inc(gate_up_in, 16)
            with sp.Fori(1, 6) as i:
                for s in range(SLOTS):
                    sp.wait_ge(ring_free[s], i)
                    sp.dma_start(WB[:, s, :], io["ada"][bass.ds(i, 1), s].rearrange("a p n -> p (a n)"))\
                        .then_inc(ring_full[s], 16)
            for j, name in enumerate(("wq", "wk", "wv0", "wv1", "wr0", "wr1", "wo0", "wo1")):
                load(name, io["gla"][j])

            def moe(l):
                gu, dn = io["moe_gu"][l], io["moe_dn"][l]
                name = LAYERS[l]
                with sp.Fori(0, NE // 2) as i:
                    for e in range(2):
                        sp.wait_ge(ring_free[e], i + (RING[f"{name}_{e}"][1] - 1))
                        sp.dma_start(WB[:, e, :], gu[bass.ds(i, 1), e].rearrange("a p n -> p (a n)"))\
                            .then_inc(ring_full[e], 16)
                        sp.wait_ge(ring_free[2 + e], i + (RING[f"{name}_{2 + e}"][1] - 1))
                        sp.dma_start(WB[:, 2 + e, 0:2048], dn[bass.ds(i, 1), e].rearrange("a p n -> p (a n)"))\
                            .then_inc(ring_full[2 + e], 16)

            moe(0)
            load("dkv", io["dkv"], (0, KD * QR))
            load("dq", io["dq"], (0, KD * QR))
            load("uq", io["uq"], (0, 3 * MH * QK))
            load("ukv", io["ukv"], (0, 3072))
            load("mwo", io["mwo"])
            moe(1)
            sp.wait_ge(y_ready, 1)
            sp.dma_start(io["y"], X[:, :, :]).then_inc(y_stored, 16)
            sp.wait_ge(y_stored, 16)
            sp.wait_ge(stored, 16 * 3)
            for b in range(2):
                sp.wait_ge(st_out[b], 16 * NS // 2)
            sp.wait_ge(gt_stored, 32)

        @block.gpsimd
        def _(pool):
            pool.dma_start(PTB[:, :], io["pages"]).then_inc(pages_in, 16)
            pool.wait_ge(exp_ready, 1)
            pool.wait_ge(state_ready, NC)
            for b in range(NS):
                if b >= 2:
                    pool.wait_ge(os_full, b - 1)
                    pool.wait_ge(st_out[b % 2], 16 * (b // 2))
                pool.dma_start(ST[:, b % 2, :], io["state_in"][b]).then_inc(st_in[b % 2], 16)
                if b == 0:
                    pool.dma_start(io["state_p"], S).then_inc(stored, 16)
                if b >= 1:
                    pool.wait_ge(snew_ready, GH * b)
                    pool.dma_start(io["state_s"][b - 1], ST[:, (b - 1) % 2, :]).then_inc(st_out[(b - 1) % 2], 16)
            pool.wait_ge(snew_ready, GH * NS)
            pool.dma_start(io["state_s"][NS - 1], ST[:, 1, :]).then_inc(st_out[1], 16)
            pool.wait_ge(stored, 16)
            for b in range(2):
                pool.wait_ge(st_out[b], 16 * NS // 2)
            pool.wait_ge(os_full, NS)
            pool.dma_start(SST[:, 0:NCONST2], io["const2"]).then_inc(mla_consts_in, 16)

            def gate_rows(l):
                pool.wait_ge(gt_ready, l + 1)
                pool.dma_start(io["gates"][l], EF[0:NE, 0:T]).then_inc(gt_stored, 16)
                pool.wait_ge(gt_stored, 16 * (l + 1))
                rows = io["gates"][l].rearrange("(i e) t -> i e t", e=2)
                used = SLOTS + FIRST[LAYERS[l]]
                with pool.Fori(0, NE // 2) as i:
                    for e in range(2):
                        pool.wait_ge(psum_free, i * 24 + (used + 12 * e - 24 + 4))
                        pool.dma_start(QB[:, 2 + e, :], rows[bass.ds(i, 1), e].rearrange("a t -> (a t)")
                                       .partition_broadcast(P)).then_inc(row_in[e], 16)

            gate_rows(0)
            pool.wait_ge(lat_ready, 1)
            pool.dma_start(io["ckv"], CKV[:, 0:2, :]).then_inc(stored, 16)
            pool.wait_ge(kr_ready, 1)
            pool.dma_start(io["kr"], CKV[0:ROPE, 2, :]).then_inc(stored, 16)

            pool.wait_ge(pages_in, 16)
            with pool.Fori(0, NS * NPG // PSL) as g:
                for j in range(PSL):
                    page = pool.value_load(PTB[0:1, bass.ds(g * PSL + j, 1)], min_val=0, max_val=io["npool"] - 1)
                    pool.wait_ge(page_used, g * PSL + (j + 1))
                    pool.dma_start(PG[:, j, :], io["cache_t"][bass.ds(page, 1)].rearrange("a p n -> p (a n)"))\
                        .then_inc(page_in[j], 16)
                    pool.dma_start(KRT[:, j, :], io["cache_kr"][bass.ds(page, 1)].rearrange("a p n -> p (a n)"))\
                        .then_inc(page_in[j], 16)
            pool.wait_ge(page_used, NS * NPG + PSL)
            for j in range(PSL):
                page = pool.value_load(PTB[0:1, j:j + 1], min_val=0, max_val=io["npool"] - 1)
                pool.dma_start(CN[:, j, :], io["cache"][bass.ds(page, 1)].rearrange("a p n -> p (a n)"))\
                    .then_inc(page_in[j], 16)
            with pool.Fori(1, NS * NPG // PSL) as g:
                for j in range(PSL):
                    page = pool.value_load(PTB[0:1, bass.ds(g * PSL + j, 1)], min_val=0, max_val=io["npool"] - 1)
                    pool.wait_ge(cpage_used, g * PSL + (j + 1 - PSL))
                    pool.dma_start(CN[:, j, :], io["cache"][bass.ds(page, 1)].rearrange("a p n -> p (a n)"))\
                        .then_inc(page_in[j], 16)
            gate_rows(1)

        @block.tensor
        def _(pe):
            mm = nc.tensor.matmul

            def slot_for(t):
                pe.wait_ge(psum_free, t.count())
                s = t.slot()
                t.n += 1
                return s

            def product(t, pairs, m=P, done=True):
                s = slot_for(t)
                for a in range(2):
                    for k, (w, x) in enumerate(pairs):
                        last = mm(PS[0:m, 2 * s + a, 0:HT], w, x[:, a * HT:(a + 1) * HT],
                                  start=(k == 0), stop=(k == len(pairs) - 1))
                last.then_inc(psum_full, 1)

            def chunk(name):
                slot, use = RING[name]
                pe.wait_ge(ring_full[slot], 16 * use)
                return slot

            pe.wait_ge(cond_silu, 1)
            t = Turn("ada")
            with pe.Fori(0, 6) as i:
                for s in range(SLOTS):
                    pe.wait_ge(psum_free, i * SLOTS + (s + 1))
                    pe.wait_ge(ring_full[s], i * 16 + 16)
                    w = WB[:, s, :].rearrange("p (k n) -> p k n", k=KD)
                    for n in range(4):
                        for k in range(KD):
                            last = mm(PS[:, 2 * s, 9 * n:9 * n + 9], w[:, k, n * P:(n + 1) * P], CT[:, k, :],
                                      start=(k == 0), stop=(k == KD - 1))
                    last.then_inc(psum_full, 1)
                    pe.wait_ge(psum_full, i * SLOTS + (s + 1))
                    pe.sem_inc(ring_free[s], 1)

            def release(name, count):
                pe.wait_ge(psum_full, count)
                pe.sem_inc(ring_free[RING[name][0]], 1)

            def mean_square(stage, rows, avg):
                pe.wait_ge(sq_ready, SQ[stage])
                t = Turn(stage)
                product(t, [(avg, r) for r in rows])

            pe.wait_ge(x_in, 64)
            mean_square("norm0", [H[:, k, :] for k in range(KD)], const(O1024))

            pe.wait_ge(h_ready, HR["norm0"])
            t = Turn("qk")
            for name in ("wq", "wk"):
                w = WB[:, chunk(name), :].rearrange("p (k n) -> p k n", k=KD)
                for n in range(4):
                    product(t, [(w[:, k, n * P:(n + 1) * P], H[:, k, :]) for k in range(KD)])
                release(name, t.n)
            pe.wait_ge(gate_up_in, 32)
            product(Turn("glow"), [(WG[:, k, :], H[:, k, :]) for k in range(KD)], m=GR)
            pe.wait_ge(glow_ready, 1)
            t = Turn("gup")
            for n in range(4):
                product(t, [(WGU[:, n * P:(n + 1) * P], EF[0:GR, 0:T])])
            t = Turn("v")
            w = [WB[:, chunk(f"wv{a}"), :].rearrange("p (k n) -> p k n", k=KD) for a in range(2)]
            for q in range(5):
                m = P if q < QT else NS
                s = slot_for(t)
                for a in range(2):
                    for k in range(KD):
                        last = mm(PS[0:m, 2 * s + a, :], H[:, k, q * P:q * P + m], w[a][:, k, :],
                                  start=(k == 0), stop=(k == KD - 1))
                last.then_inc(psum_full, 1)
            release("wv0", t.n)
            pe.sem_inc(ring_free[RING["wv1"][0]], 1)

            pe.wait_ge(decayed, 2)
            for q in range(QT):
                if q >= 2:
                    pe.wait_ge(prep_done, 2 * (q - 1))
                for h in range(GH):
                    nc.tensor.transpose(PS[:, q % 2, h * P:(h + 1) * P], QB[:, 4 + h, q * P:(q + 1) * P], ident())
                    for a in range(2):
                        sl = slice(q * P + a * C, q * P + (a + 1) * C)
                        last = mm(PS[a * C:(a + 1) * C, 2 + q % 2, h * C:(h + 1) * C], QB[:, 4 + h, sl], QB[:, h, sl],
                                  start=True, stop=True)
                last.then_inc(prep_full, 1)
            for c in range(NC):
                q, lo = c // 2, C * (c % 2)
                if c == 0:
                    pe.wait_ge(prep_done, 2 * QT)
                if c >= 2:
                    pe.wait_ge(state_ready, c - 1)
                    pe.wait_ge(o_taken, c - 1)
                for h in range(GH):
                    mm(PS[:, 2 * (c % 2) + h // 2, (h % 2) * DV:(h % 2 + 1) * DV],
                       EF[lo:lo + C, q * 512 + h * DK:q * 512 + (h + 1) * DK],
                       V[lo:lo + C, q, h * DV:(h + 1) * DV], start=True, stop=True)
                if c >= 1:
                    pe.wait_ge(state_ready, c)
                for n in range(2 * GH):
                    h = n // 2
                    out = PS[:, 4 + c % 2, n * C:(n + 1) * C]
                    last = mm(out, V[lo:lo + C, q, n * P:(n + 1) * P],
                              AT[lo:lo + C, q * 256 + h * C:q * 256 + (h + 1) * C], start=True, stop=(c == 0))
                    if c >= 1:
                        last = mm(out, S[:, n * P:(n + 1) * P], QB[:, h, c * C:(c + 1) * C], start=False, stop=True)
                last.then_inc(o_full, 1)
            for h in range(GH):
                last = nc.tensor.transpose(PS[0:NS, 6, h * P:(h + 1) * P], QB[:, 4 + h, NP:T], ident())
            last.then_inc(ks_full, 1)

            def outer(b):
                pe.wait_ge(km_ready, b + 1)
                if b >= 2:
                    pe.wait_ge(snew_ready, GH * (b - 1))
                if b == 0:
                    pe.wait_ge(state_ready, NC)
                for h in range(GH):
                    last = mm(PS[:, 2 * (b % 2) + h // 2, (h % 2) * DV:(h % 2 + 1) * DV],
                              EF[0:NS, 512 * (1 + b % 2) + h * DK:512 * (1 + b % 2) + (h + 1) * DK],
                              VS[:, h * DV:(h + 1) * DV], start=True, stop=True)
                last.then_inc(outer_full, 1)

            outer(0)
            for b in range(NS):
                if b + 1 < NS:
                    outer(b + 1)
                pe.wait_ge(snew_ready, GH * (b + 1))
                for n in range(2 * GH):
                    last = mm(PS[:, 7, b * 8 + n:b * 8 + n + 1], ST[:, b % 2, n * P:(n + 1) * P],
                              QB[:, n // 2, NP + b:NP + b + 1], start=True, stop=True)
                last.then_inc(os_full, 1)

            pe.wait_ge(sq_ready, SQ["onorm"])
            t = Turn("onorm")
            for h in range(GH):
                product(t, [(const(O256), BE[:, 2 * h + a, :]) for a in range(2)])
            t = Turn("r")
            for name in ("wr0", "wr1"):
                w = WB[:, chunk(name), :].rearrange("p (k n) -> p k n", k=KD)
                for n in range(4):
                    product(t, [(w[:, k, n * P:(n + 1) * P], H[:, k, :]) for k in range(KD)])
                release(name, t.n)
            pe.wait_ge(psum_free, SLOTS + FIRST["r"] + 8)
            t = Turn("gout")
            for name in ("wo0", "wo1"):
                w = WB[:, chunk(name), :].rearrange("p (k n) -> p k n", k=KD)
                for n in range(4):
                    product(t, [(w[:, k, n * P:(n + 1) * P], O[:, k, :]) for k in range(KD)])
                release(name, t.n)

            def experts(l):
                mean_square(f"fnorm{l}", [H[:, k, :] for k in range(KD)], const(O1024))
                pe.wait_ge(h_ready, HR[f"fnorm{l}"])
                t = Turn(f"route{l}")
                s = slot_for(t)
                for q in range(5):
                    m = P if q < QT else NS
                    for k in range(KD):
                        last = mm(PS[0:m, 2 * s, q * 20:q * 20 + 20], H[:, k, q * P:q * P + m], WRT[:, l, k, :],
                                  start=(k == 0), stop=(k == KD - 1))
                last.then_inc(psum_full, 1)
                pe.wait_ge(gates_ready, l + 1)
                s = slot_for(Turn(f"gt{l}"))
                for q in range(5):
                    m = P if q < QT else NS
                    last = nc.tensor.transpose(PS[0:NE, 2 * s + q // QT, (q % QT) * P:(q % QT) * P + m],
                                               AT[0:m, 256 + q * NE:256 + (q + 1) * NE], ident(m, m))
                last.then_inc(psum_full, 1)
                name = LAYERS[l]
                t = Turn(name)
                base = t.n
                with pe.Fori(0, NE // 2) as i:
                    t.off = i * 24
                    for e in range(2):
                        pe.wait_ge(ring_full[e], i * 16 + 16 * RING[f"{name}_{e}"][1])
                        wgu = WB[:, e, :].rearrange("p (k n) -> p k n", k=KD)
                        for f in range(2):
                            for g in range(2):
                                lo = g * FF + f * P
                                product(t, [(wgu[:, k, lo:lo + P], H[:, k, :]) for k in range(KD)])
                        pe.wait_ge(psum_full, i * 24 + t.n)
                        pe.sem_inc(ring_free[e], 1)
                        pe.wait_ge(ring_full[2 + e], i * 16 + 16 * RING[f"{name}_{2 + e}"][1])
                        pe.wait_ge(psum_free, i * 24 + (SLOTS + t.n))
                        wd = WB[:, 2 + e, 0:2048].rearrange("p (f n) -> p f n", f=2)
                        for d in range(KD):
                            product(t, [(wd[:, f, d * P:(d + 1) * P], QB[:, 4 + 2 * e + f, :]) for f in range(2)])
                        pe.wait_ge(psum_full, i * 24 + t.n)
                        pe.sem_inc(ring_free[2 + e], 1)

            experts(0)

            mean_square("kvnorm", [H[:, k, :] for k in range(KD)], const(O1024))
            pe.wait_ge(h_ready, HR["kvnorm"])
            t = Turn("dkv")
            w = WB[:, chunk("dkv"), 0:KD * QR].rearrange("p (k n) -> p k n", k=KD)
            for n in range(3):
                product(t, [(w[:, k, n * P:(n + 1) * P], H[:, k, :]) for k in range(KD)])
            release("dkv", t.n)
            mean_square("ckvnorm", [E[:, k, :] for k in range(2)], const(O256))
            pe.wait_ge(mla_consts_in, 16)
            product(Turn("krot"), [(const2(ROT), CKV[:, 2, :])])

            mean_square("norm2", [H[:, k, :] for k in range(KD)], const(O1024))
            pe.wait_ge(h_ready, HR["norm2"])
            t = Turn("dq")
            w = WB[:, chunk("dq"), 0:KD * QR].rearrange("p (k n) -> p k n", k=KD)
            for n in range(3):
                product(t, [(w[:, k, n * P:(n + 1) * P], H[:, k, :]) for k in range(KD)])
            release("dq", t.n)
            mean_square("cqnorm", [E[:, k, :] for k in range(3)], const(O384))
            pe.wait_ge(lat_ready, 2)
            t = Turn("uq")
            w = WB[:, chunk("uq"), 0:3 * MH * QK].rearrange("p (k n) -> p k n", k=3)
            for n in range(6):
                product(t, [(w[:, k, n * P:(n + 1) * P], B[:, k, :]) for k in range(3)])
            release("uq", t.n)
            pe.wait_ge(psum_free, SLOTS + t.n)
            t = Turn("qrot")
            for j in range(2):
                product(t, [(const2(ROT), QB[:, 4 + j, :])])
            pe.wait_ge(sq_ready, SQ["qss"])
            t = Turn("qss")
            for m in range(4):
                product(t, [(const2(B64), H[:, m, :]), (const2(F0 + (m % 2) * P), H[:, 4 + m // 2, :])])
            for j in range(2):
                product(t, [(const2(B32), H[:, 4 + j, :])]
                        + [(const2(E0 + u * P), H[:, 2 * j + u, :]) for u in range(2)])
            chunk("ukv")
            wukv = WB[:, RING["ukv"][0], :]
            t = Turn("uk")
            for n in range(4):
                product(t, [(wukv[:, k * 512 + n * P:k * 512 + (n + 1) * P], CKV[:, k, :]) for k in range(2)])
            pe.wait_ge(sq_ready, SQ["kss"])
            t = Turn("kss")
            for m in range(4):
                product(t, [(const2(B64), H[:, m, :]), (const2(K1), H[:, 4, :])])
            for j in range(2):
                product(t, [(const2(K1), H[:, 4, :])]
                        + [(const2(E0 + u * P), H[:, 2 * j + u, :]) for u in range(2)])
            t = Turn("uv")
            for q in range(QT):
                s = slot_for(t)
                for k in range(2):
                    last = mm(PS[:, 2 * s, :], CKV[:, k, q * P:(q + 1) * P],
                              wukv[:, 1024 + k * 512:1536 + k * 512], start=(k == 0), stop=(k == 1))
                last.then_inc(psum_full, 1)

            def scores(n):
                q, h = n // MH, n % MH
                nk = (q + 1) * P
                if n == 0:
                    pe.wait_ge(psum_free, SLOTS + FIRST["uv"] + 4)
                if n >= 2:
                    pe.wait_ge(exp_done, n - 1)
                lo, lr = NOPE * (h % 2), ROPE * (h % 4)
                mm(PS[:, n % 2, 0:nk], QB[lo:lo + NOPE, h // 2, q * P:(q + 1) * P], O[lo:lo + NOPE, h // 2, 0:nk],
                   start=True, stop=False)
                mm(PS[:, n % 2, 0:nk], QB[lr:lr + ROPE, 4 + h // 4, q * P:(q + 1) * P],
                   O[lr:lr + ROPE, 4 + h // 4, 0:nk], start=False, stop=True).then_inc(sc_full, 1)

            scores(0)
            for n in range(QT * MH):
                q, h = n // MH, n % MH
                if n + 1 < QT * MH:
                    scores(n + 1)
                pe.wait_ge(p_ready, n + 1)
                if n >= 2:
                    pe.wait_ge(pt_ready, n - 1)
                for k in range(q + 1):
                    last = nc.tensor.transpose(PS[:, 2 + n % 2, k * P:(k + 1) * P],
                                               EF[:, 512 * (n % 2) + k * P:512 * (n % 2) + (k + 1) * P], ident())
                last.then_inc(pt_full, 1)
                pe.wait_ge(pt_ready, n + 1)
                if n >= 2:
                    pe.wait_ge(pv_done, n - 1)
                lo = MV * (h % 2)
                for k in range(q + 1):
                    last = mm(PS[lo:lo + MV, 4 + n % 2, 0:P], VP[:, k, h * MV:(h + 1) * MV],
                              EF[:, 1024 + 512 * (n % 2) + k * P:1024 + 512 * (n % 2) + (k + 1) * P],
                              start=(k == 0), stop=(k == q))
                last.then_inc(pv_full, 1)

            pe.wait_ge(qp_ready, 2)
            for r in range(2):
                for h in range(MH):
                    lo = NOPE * (h % 2)
                    mm(PS[:, 3 * (h % 2), (r * 4 + h // 2) * 8:(r * 4 + h // 2) * 8 + 8],
                       wukv[lo:lo + NOPE, 2048 + (h // 2) * 256 + r * P:2048 + (h // 2) * 256 + (r + 1) * P],
                       QP[lo:lo + NOPE, h // 2, :], start=True, stop=True)
            for h in range(MH):
                mm(PS[0:ROPE, 1, h * 8:h * 8 + 8], ident(P, ROPE, 0, ROPE * (h % 4)), QP[:, 4 + h // 4, :],
                   start=True, stop=True)
            for h in range(MH):
                mm(PS[0:1, 2, h * 8:h * 8 + 8], const2(B64 + NOPE * (h % 2), 1), PR[:, h // 2, :],
                   start=True, stop=False)
                last = mm(PS[0:1, 2, h * 8:h * 8 + 8], const2(B32 + ROPE * (h % 4), 1), PR[:, 4 + h // 4, :],
                          start=False, stop=True)
            last.then_inc(ql_full, 1)
            pe.wait_ge(ql_ready, 5)
            with pe.Fori(0, NS) as i:
                for j in range(NPG):
                    g, sl = j // PSL, j % PSL
                    pe.wait_ge(page_in[sl], i * 64 + (32 * g + 32))
                    if sl == 0:
                        pe.wait_ge(scores_taken, i * 2 + (g + 1))
                    pe.wait_ge(page_used, i * NPG + (j + 5))
                    out = PS[:, 4 + g, sl * 8:sl * 8 + 8]
                    for r in range(2):
                        mm(out, PG[:, sl, r * P:(r + 1) * P],
                           QL[:, r, bass.ds(i, 1), :].rearrange("p a h -> p (a h)"), start=(r == 0), stop=False)
                    mm(out, KRT[:, sl, :], QRS[:, bass.ds(i, 1), :].rearrange("p a h -> p (a h)"),
                       start=False, stop=True)
                    for r in range(2):
                        last = mm(PS[:, j % 4, :], PG[:, sl, r * P:(r + 1) * P], wukv[:, r * 512:(r + 1) * 512],
                                  start=(r == 0), stop=(r == 1))
                    last.then_inc(kn_full, 1)
            pe.wait_ge(max_ready, 1)
            nc.tensor.transpose(PS[0:64, 6, 0:P], MX, ident()).then_inc(max_full, 1)
            pe.wait_ge(max_ready, 2)
            mm(PS[:, 7, 0:64], const(ONE, P, 0, 64), DG, start=True, stop=True).then_inc(max_full, 1)
            pe.wait_ge(sum_ready, 1)
            mm(PS[:, 6, 0:64], const(ONE), LS, start=True, stop=True)
            mm(PS[:, 6, 64:128], const(ONE, P, 0, 1), NEW[0:1, :], start=True, stop=True).then_inc(sum_full, 1)
            with pe.Fori(0, NS) as i:
                pe.wait_ge(acc_taken, i + 1)
                for j in range(NPG):
                    g, sl = j // PSL, j % PSL
                    pe.wait_ge(page_in[sl], i * 32 + (16 * g + 16 + 32 * NS * NPG // PSL))
                    for r in range(2):
                        last = mm(PS[:, r, 0:8], CN[:, sl, r * P:(r + 1) * P], HF[:, bass.ds(i * 128 + j * 8, 8)],
                                  start=(j == 0), stop=(j == NPG - 1), skip_group_check=True)
                    last.then_inc(cpage_used, 1)
                pe.wait_ge(cpage_used, i * NPG + NPG)
                pe.sem_inc(acc_full, 1)
            pe.wait_ge(olat_ready, 1)
            for h in range(MH):
                lo = MV * (h % 2)
                for r in range(2):
                    last = mm(PS[lo:lo + MV, 4, (h // 2) * 8:(h // 2) * 8 + 8],
                              wukv[:, 1024 + r * 512 + h * MV:1024 + r * 512 + (h + 1) * MV], OL[:, r, :, h],
                              start=(r == 0), stop=(r == 1))
            last.then_inc(osam_full, 1)
            pe.wait_ge(osam_full, 1)
            pe.sem_inc(ring_free[RING["ukv"][0]], 1)
            pe.wait_ge(attn_ready, 1)
            t = Turn("mout")
            w = WB[:, chunk("mwo"), :].rearrange("p (k n) -> p k n", k=4)
            for n in range(KD):
                product(t, [(w[:, k, n * P:(n + 1) * P], B[:, k, :]) for k in range(4)])
            release("mwo", t.n)
            experts(1)

        @block.scalar
        def _(act):
            a = Order(act, act_order)
            f = nc.scalar.activation
            act.wait_ge(consts_in, 32)
            a(f(CT[:, :, :], CT[:, :, :], ACT.Silu), cond_silu)

            def rms(stage, n=1):
                t = Turn(stage)
                for j in range(n):
                    act.wait_ge(psum_full, t.count())
                    if j >= 2:
                        act.wait_ge(psum_free, SLOTS + t.n - 1)
                    r = two(RS[:, (RMS[stage] + j) % 2, :])
                    a(f(r, halves(t.slot()), ACT.Ln, bias=EPST[:, 0:1]))
                    a(f(r, r, ACT.Exp, scale=-0.5), rms_ready)
                    t.n += 1

            rms("norm0")
            act.wait_ge(psum_free, SLOTS + FIRST["gup"] + 4)
            a(f(E, B, ACT.Abs))
            a(f(E, E, ACT.Exp, scale=-1.0))
            a(f(E, E, ACT.Ln, bias=CONST[:, ONE:ONE + 1]), softplus_ready)
            act.wait_ge(decay_ready, 1)
            a(f(B[:, :, NP:T], B[:, :, NP:T], ACT.Exp))
            a(f(FE, FE, ACT.Exp))
            a(f(B[:, :, 0:NP], E[:, :, 0:NP], ACT.Exp), exp_ready)
            a(f(E[:, :, 0:NP], E[:, :, 0:NP], ACT.Exp, scale=-1.0), exp_ready)
            rms("onorm", 4)
            t = Turn("r")
            for n in range(8):
                act.wait_ge(psum_full, t.count())
                a(f(two(QB[:, n, :]), halves(t.slot()), ACT.Silu), silu_ready)
                t.n += 1

            def experts(l):
                rms(f"fnorm{l}")
                act.wait_ge(route_exp_in, 2 * l + 1)
                a(f(GX, GX, ACT.Exp), route_exp)
                act.wait_ge(route_exp_in, 2 * l + 2)
                a(f(X2, X2, ACT.Exp), route_exp)
                base = FIRST[LAYERS[l]]
                with a.loop(NE // 2, [(silu_ready, 4)]) as i:
                    for e in range(2):
                        for h in range(2):
                            r = base + 12 * e + 2 * h
                            act.wait_ge(psum_full, i * 24 + (r + 1))
                            act.wait_ge(psum_free, i * 24 + (SLOTS + r - 11))
                            a(f(two(QB[:, h, :]), halves(r % SLOTS), ACT.Silu), silu_ready)

            experts(0)
            for stage, n in (("kvnorm", 1), ("ckvnorm", 1), ("norm2", 1), ("cqnorm", 1), ("qss", 6), ("kss", 6)):
                rms(stage, n)
            for n in range(QT * MH):
                nk = (n // MH + 1) * P
                act.wait_ge(negmax_ready, n + 1)
                if n >= 2:
                    act.wait_ge(pt_full, n - 1)
                a(f(EF[:, 512 * (n % 2):512 * (n % 2) + nk], PS[:, n % 2, 0:nk], ACT.Exp, bias=NM[:, n % 2:n % 2 + 1],
                    scale=SCALE, accum_out=LN[:, n % 2:n % 2 + 1]), exp_done)
            with a.loop(NS, [(act_order, NPG), (page_sq, NPG)]) as i:
                for j in range(NPG):
                    act.wait_ge(kn_full, i * NPG + (j + 1))
                    act.wait_ge(page_used, i * NPG + (j + 5))
                    a(f(SQP[:, j % 4, :], PS[:, j % 4, :], ACT.Square), hold=False)
                    a(f(RS[:, 0, 0:ROPE], PG[:, j % PSL, KVR:PROW], ACT.Square,
                        accum_out=KRS[:, bass.ds(i * NPG + j, 1)]), page_sq)
            act.wait_ge(ssq_ready, 1)
            a(f(SSQ, SSQ, ACT.Ln, bias=EPST[:, 0:1], scale=1.0 / QK))
            a(f(SSQ, SSQ, ACT.Exp, scale=-0.5), krstd_ready)
            act.wait_ge(shifted, 1)
            a(f(NEW, NEW, ACT.Exp))
            a(f(SC, SC, ACT.Exp), p_exp)
            experts(1)

        @block.vector
        def _(dve):
            v = Order(dve, vec_order)
            nv = nc.vector
            tt, ts, stt, cp, red = (nv.tensor_tensor, nv.tensor_scalar, nv.scalar_tensor_tensor, nv.tensor_copy,
                                    nv.tensor_reduce)

            def full(t):
                dve.wait_ge(psum_full, t.count())
                s = t.slot()
                t.n += 1
                return s

            def rows(ap, n):
                return ap.unsqueeze(1).to_broadcast([P, n, T])

            v(nv.memset(EPST[:, :], EPS), psum_free)
            v(nv.memset(AT[:, 672:688], 0.0), psum_free)
            v(nv.memset(TS[:, 0:NS], 0.0), psum_free)
            v(nv.memset(TS[:, NS:2 * NS], 0.0), psum_free)
            dve.wait_ge(consts_in, 32)
            with v.loop(6, [(psum_free, SLOTS)]) as i:
                for s in range(SLOTS):
                    dve.wait_ge(psum_full, i * SLOTS + (s + 1))
                    v(tt(MOD[:, bass.ds(i * 16 + 4 * s, 4), :],
                         PS[:, 2 * s, 0:36].rearrange("p (n c) -> p n c", n=4),
                         VEC[:, bass.ds(i * 16 + (ADAB + 4 * s), 4)].unsqueeze(2).to_broadcast([P, 4, 1 + NS]),
                         ALU.add), psum_free)

            rms_used = [0]

            def normed():
                rms_used[0] += 1
                dve.wait_ge(rms_ready, rms_used[0])
                return RS[:, (rms_used[0] - 1) % 2, :]

            def squares(dst, src):
                v(tt(dst, src, src, ALU.mult), sq_ready)

            def norm_modulate(stage, mod, gain):
                squares(H[:, :, :], X[:, :, :])
                v(stt(AM[:, :, :], MOD[:, mod + 8:mod + 16, :], 1.0,
                      VEC[:, gain:gain + KD].unsqueeze(2).to_broadcast([P, KD, 1 + NS]), ALU.add, ALU.mult))
                r = normed()
                full(Turn(stage))
                v(tt(H[:, :, :], X[:, :, :], rows(r, KD), ALU.mult), psum_free)
                v(tt(H[:, :, NP:T], H[:, :, NP:T], AM[:, :, 1:], ALU.mult))
                for k in range(KD):
                    v(ts(H[:, k, 0:NP], H[:, k, 0:NP], AM[:, k, 0:1], MOD[:, mod + k, 0:1], ALU.mult, ALU.add),
                      h_ready, hold=False)
                v(tt(H[:, :, NP:T], H[:, :, NP:T], MOD[:, mod:mod + KD, 1:], ALU.add), h_ready)

            def residual(stage, mod):
                t = Turn(stage)
                for n in range(KD):
                    s = full(t)
                    g = MOD[:, mod + n, 0:1]
                    v(stt(X[:, n, 0:HT], PS[:, 2 * s, 0:HT], g, X[:, n, 0:HT], ALU.mult, ALU.add), hold=False)
                    v(stt(X[:, n, HT:NP], PS[:, 2 * s + 1, 0:NP - HT], g, X[:, n, HT:NP], ALU.mult, ALU.add),
                      hold=False)
                    v(tt(TS[:, 0:NS], PS[:, 2 * s + 1, NP - HT:HT], MOD[:, mod + n, 1:], ALU.mult))
                    v(tt(X[:, n, NP:T], X[:, n, NP:T], TS[:, 0:NS], ALU.add), psum_free)

            dve.wait_ge(x_in, 64)
            norm_modulate("norm0", 0, MIXN)
            t = Turn("qk")
            for n in range(8):
                s = full(t)
                v(ts(two(QB[:, n, :]), halves(s), float(DK) ** -0.5 if n < 4 else 1.0, None, ALU.mult), psum_free)
            s = full(Turn("glow"))
            v(cp(two(EF[0:GR, 0:T]), halves(s, GR)), psum_free)
            v(cp(TS[:, 0:1], EPST[:, :]), glow_ready)
            t = Turn("gup")
            for n in range(4):
                s = full(t)
                v(ts(two(B[:, n, :]), halves(s), VEC[:, GBIAS + n:GBIAS + n + 1], None, ALU.add), psum_free)
            t = Turn("v")
            for q in range(5):
                s = full(t)
                src = PS[:, 2 * s:2 * s + 2, :] if q < QT else PS[0:NS, 2 * s:2 * s + 2, :]
                dst = V[:, q, :] if q < QT else VS[:, :]
                v(cp(dst.rearrange("p (a b) -> p a b", a=2), src), psum_free)
            dve.wait_ge(softplus_ready, 1)
            v(stt(B, B, 0.0, E, ALU.min, ALU.subtract))
            v(ts(B, B, 1.0 / 16.0, None, ALU.mult))
            for h in range(GH):
                v(nv.tensor_tensor_scan(E[:, h, 0:NP], const(SCAN, NP), B[:, h, 0:NP], 0.0, ALU.mult, ALU.add),
                  hold=False)
            v.settle()
            EC = E[:, :, 0:NP].rearrange("p h (c t) -> p h c t", c=NC)
            v(cp(BM, EC[:, :, :, C // 2 - 1]), hold=False)
            v(cp(BL, EC[:, :, :, C - 1]))
            v(tt(FE, BL, BM, ALU.subtract))
            v(tt(FE[:, :, 0:NC - 1], FE[:, :, 0:NC - 1], BM[:, :, 1:NC], ALU.add))
            v(tt(EC, EC, BM.unsqueeze(3).to_broadcast([P, GH, NC, C]), ALU.subtract), decay_ready)
            dve.wait_ge(exp_ready, 1)
            v(tt(QB[:, 0:4, 0:NP], QB[:, 0:4, 0:NP], B[:, :, 0:NP], ALU.mult), decayed)
            dve.wait_ge(exp_ready, 2)
            v(tt(QB[:, 4:8, 0:NP], QB[:, 4:8, 0:NP], E[:, :, 0:NP], ALU.mult), decayed)
            for q in range(QT):
                dve.wait_ge(prep_full, q + 1)
                v(cp(EF[:, q * 512:(q + 1) * 512], PS[:, q % 2, :]), prep_done, hold=False)
                v(tt(AT[:, q * 256:(q + 1) * 256].rearrange("p (h t) -> p h t", h=GH),
                     PS[:, 2 + q % 2, 0:256].rearrange("p (h t) -> p h t", h=GH),
                     const(TRI, C).unsqueeze(1).to_broadcast([P, GH, C]), ALU.mult), prep_done)
            S4 = S.rearrange("p (h n) -> p h n", h=GH)
            for c in range(NC):
                dve.wait_ge(o_full, c + 1)
                v(cp(O[:, :, c * C:(c + 1) * C], PS[:, 4 + c % 2, :].rearrange("p (n t) -> p n t", n=8)), o_taken)
                kv = PS[:, 2 * (c % 2):2 * (c % 2) + 2, :].rearrange("p a (h n) -> p (a h) n", h=2)
                fe = FE[:, :, c:c + 1].to_broadcast([P, GH, DV])
                if c == 0:
                    v(tt(S4, kv, fe, ALU.mult), state_ready)
                else:
                    v(tt(S4, kv, S4, ALU.add))
                    v(tt(S4, S4, fe, ALU.mult), state_ready)
            dve.wait_ge(ks_full, 1)
            v(cp(EF[0:NS, 0:512], PS[0:NS, 6, :]))

            def key_row(b):
                if b >= 2:
                    dve.wait_ge(outer_full, b - 1)
                v(ts(EF[0:NS, 512 * (1 + b % 2):512 * (2 + b % 2)], EF[0:NS, 0:512], CONST[0:NS, ID + b:ID + b + 1],
                     None, ALU.mult), km_ready)

            key_row(0)
            for b in range(NS):
                if b + 1 < NS:
                    key_row(b + 1)
                dve.wait_ge(outer_full, b + 1)
                dve.wait_ge(st_in[b % 2], 16 * (b // 2 + 1))
                for h in range(GH):
                    st = ST[:, b % 2, h * DV:(h + 1) * DV]
                    v(stt(st, st, B[:, h, NP + b:NP + b + 1],
                          PS[:, 2 * (b % 2) + h // 2, (h % 2) * DV:(h % 2 + 1) * DV], ALU.mult, ALU.add),
                      snew_ready, hold=False)
                v.settle()
            dve.wait_ge(os_full, NS)
            v(cp(O[:, :, NP:T], PS[:, 7, 0:64].rearrange("p (b n) -> p n b", b=NS)))
            squares(BE[:, :, :], O[:, :, :])
            t = Turn("onorm")
            for h in range(GH):
                r = normed()
                full(t)
                v(tt(O[:, 2 * h:2 * h + 2, :], O[:, 2 * h:2 * h + 2, :], rows(r, 2), ALU.mult), psum_free)
            t = Turn("r")
            for n in range(8):
                full(t)
                dve.wait_ge(silu_ready, n + 1)
                v(stt(O[:, n, :], O[:, n, :], VEC[:, ONORM + n % 2:ONORM + n % 2 + 1], QB[:, n, :], ALU.mult,
                      ALU.mult), psum_free)
            residual("gout", 16)

            def first_max(dst, src, top, tmp, top2):
                b = [P, 5, 4]
                v(red(top, src, AX.X, ALU.max))
                v(tt(tmp, src, top.unsqueeze(2).to_broadcast(b), ALU.is_ge))
                v(tt(tmp, tmp, CONST[:, RANK:RANK + 4].unsqueeze(1).to_broadcast(b), ALU.mult))
                v(red(top2, tmp, AX.X, ALU.max))
                v(tt(dst, tmp, top2.unsqueeze(2).to_broadcast(b), ALU.is_equal))

            def experts(l):
                norm_modulate(f"fnorm{l}", l * 48 + 24, FFNN + 8 * l)
                v(nv.memset(LOG, 0.0))
                s = full(Turn(f"route{l}"))
                bias = BRT[:, l, :]
                v(tt(LOG[:, 0:QT, :], PS[:, 2 * s, 0:80].rearrange("p (q n) -> p q n", q=QT),
                     bias.unsqueeze(1).to_broadcast([P, QT, 20]), ALU.add))
                v(tt(LOG[0:NS, QT, :], PS[0:NS, 2 * s, 80:100], bias[0:NS, :], ALU.add), psum_free)
                b = [P, 5, 4]
                first_max(OHG, LOG[:, :, 0:4], M1, TMP, M2)
                v(tt(GX, LOG[:, :, 0:4], M1.unsqueeze(2).to_broadcast(b), ALU.subtract), route_exp_in)
                le = LOG[:, :, 4:20].rearrange("p q (g e) -> p q g e", g=NG)
                v(tt(SEL, le, OHG.unsqueeze(3).to_broadcast([P, 5, 4, 4]), ALU.mult))
                v(red(LE, SEL.rearrange("p q g e -> p q e g"), AX.X, ALU.add))
                first_max(OH1, LE, M1, TMP, M2)
                v(stt(LE, OH1, -BIG, LE, ALU.mult, ALU.add))
                first_max(OH2, LE, M3, TMP, M2)
                v(tt(X2, M3, M1, ALU.subtract), route_exp_in)
                dve.wait_ge(route_exp, 2 * l + 2)
                v(red(M1, GX, AX.X, ALU.add))
                v(stt(M2, X2, 1.0, M1, ALU.add, ALU.mult))
                v(nv.reciprocal(M1, M2))
                v(tt(M2, M1, X2, ALU.mult))
                v(tt(OH1, OH1, M1.unsqueeze(2).to_broadcast(b), ALU.mult))
                v(tt(OH2, OH2, M2.unsqueeze(2).to_broadcast(b), ALU.mult))
                v(tt(OH1, OH1, OH2, ALU.add))
                v(tt(GATES, OH1.unsqueeze(2).to_broadcast([P, 5, 4, 4]), OHG.unsqueeze(3).to_broadcast([P, 5, 4, 4]),
                     ALU.mult), gates_ready)
                s = full(Turn(f"gt{l}"))
                v(cp(EF[0:NE, 0:NP], PS[0:NE, 2 * s, :]))
                v(cp(EF[0:NE, NP:T], PS[0:NE, 2 * s + 1, 0:NS]), psum_free)
                v(nv.memset(O[:, :, :], 0.0), gt_ready)
                t = Turn(LAYERS[l])
                silus = 8 + 32 * l
                with v.loop(NE // 2, [(psum_free, 24)]) as i:
                    t.off = i * 24
                    for e in range(2):
                        dve.wait_ge(row_in[e], i * 16 + (16 + 128 * l))
                        for f in range(2):
                            s = full(t)
                            dve.wait_ge(silu_ready, i * 4 + (silus + 2 * e + f + 1))
                            v(tt(QB[:, f, :], QB[:, f, :], QB[:, 2 + e, :], ALU.mult), psum_free)
                            s = full(t)
                            v(tt(two(QB[:, 4 + 2 * e + f, :]), two(QB[:, f, :]), halves(s), ALU.mult), psum_free)
                        for d in range(KD):
                            s = full(t)
                            v(tt(two(O[:, d, :]), two(O[:, d, :]), halves(s), ALU.add), psum_free)
                mod = l * 48 + 40
                for n in range(KD):
                    v(stt(X[:, n, 0:NP], O[:, n, 0:NP], MOD[:, mod + n, 0:1], X[:, n, 0:NP], ALU.mult, ALU.add),
                      hold=False)
                v(tt(O[:, :, NP:T], O[:, :, NP:T], MOD[:, mod:mod + KD, 1:], ALU.mult))
                v(tt(X[:, :, NP:T], X[:, :, NP:T], O[:, :, NP:T], ALU.add), y_ready if l else None)

            experts(0)

            squares(H[:, :, :], X[:, :, :])
            r = normed()
            full(Turn("kvnorm"))
            v(tt(H[:, :, :], X[:, :, :], rows(r, KD), ALU.mult), psum_free)
            for k in range(KD):
                v(ts(H[:, k, :], H[:, k, :], VEC[:, KVIN + k:KVIN + k + 1], None, ALU.mult), h_ready, hold=False)
            v.settle()
            t = Turn("dkv")
            for n in range(3):
                s = full(t)
                v(cp(two(CKV[:, n, :]), halves(s)), psum_free)
            squares(E[:, 0:2, :], CKV[:, 0:2, :])
            r = normed()
            full(Turn("ckvnorm"))
            v(tt(CKV[:, 0:2, :], CKV[:, 0:2, :], rows(r, 2), ALU.mult), psum_free)
            v(ts(CKV[:, 0, :], CKV[:, 0, :], VEC[:, KVLAT:KVLAT + 1], None, ALU.mult))
            v(ts(CKV[:, 1, :], CKV[:, 1, :], VEC[:, KVLAT + 1:KVLAT + 2], None, ALU.mult), lat_ready)
            s = full(Turn("krot"))
            v(tt(two(E[:, 3, :]), halves(s), two(const2(SIN, T)), ALU.mult), psum_free)
            v(tt(CKV[:, 2, :], CKV[:, 2, :], const2(COS, T), ALU.mult))
            v(tt(CKV[:, 2, :], CKV[:, 2, :], E[:, 3, :], ALU.add), kr_ready)

            norm_modulate("norm2", 48, MIXN + 8)
            t = Turn("dq")
            for n in range(3):
                s = full(t)
                v(cp(two(B[:, n, :]), halves(s)), psum_free)
            squares(E[:, 0:3, :], B[:, 0:3, :])
            r = normed()
            full(Turn("cqnorm"))
            v(tt(B[:, 0:3, :], B[:, 0:3, :], rows(r, 3), ALU.mult), psum_free)
            for k in range(2):
                v(ts(B[:, k, :], B[:, k, :], VEC[:, QLAT + k:QLAT + k + 1], None, ALU.mult))
            v(ts(B[:, 2, :], B[:, 2, :], VEC[:, QLAT + 2:QLAT + 3], None, ALU.mult), lat_ready)
            t = Turn("uq")
            for n in range(6):
                s = full(t)
                v(cp(two(QB[:, n, :]), halves(s)), psum_free)
            t = Turn("qrot")
            for j in range(2):
                s = full(t)
                v(tt(two(E[:, j, :]), halves(s), two(const2(SIN, T)), ALU.mult), psum_free)
            v(tt(QB[:, 4:6, :], QB[:, 4:6, :], rows(const2(COS, T), 2), ALU.mult))
            v(tt(QB[:, 4:6, :], QB[:, 4:6, :], E[:, 0:2, :], ALU.add))
            squares(H[:, 0:6, :], QB[:, 0:6, :])
            t = Turn("qss")
            for n in range(6):
                r = normed()
                full(t)
                g = QNN if n < 4 else QNR
                v(stt(QB[:, n, :], QB[:, n, :], VEC[:, g:g + 1], r, ALU.mult, ALU.mult), psum_free)
            t = Turn("uk")
            for n in range(4):
                s = full(t)
                v(cp(two(O[:, n, :]), halves(s)), psum_free)
            v(tt(H[:, 0:4, :], O[:, 0:4, :], O[:, 0:4, :], ALU.mult))
            squares(H[:, 4, :], CKV[:, 2, :])
            t = Turn("kss")
            for n in range(6):
                r = normed()
                full(t)
                g, src = (KNN, O[:, n, :]) if n < 4 else (KNR, CKV[:, 2, :])
                v(stt(O[:, n, :], src, VEC[:, g:g + 1], r, ALU.mult, ALU.mult), psum_free)
            t = Turn("uv")
            for q in range(QT):
                s = full(t)
                v(cp(VP[:, q, :], PS[:, 2 * s, :]), psum_free)

            def mask_max(n):
                q, b = n // MH, n % 2
                dve.wait_ge(sc_full, n + 1)
                diag = PS[:, b, q * P:(q + 1) * P]
                v(tt(diag, diag, const2(CAUS), ALU.add))
                v(red(NM[:, b:b + 1], PS[:, b, 0:(q + 1) * P], AX.X, ALU.max))
                v(ts(NM[:, b:b + 1], NM[:, b:b + 1], -SCALE, None, ALU.mult), negmax_ready)

            mask_max(0)
            for n in range(QT * MH):
                q, h, b = n // MH, n % MH, n % 2
                nk = (q + 1) * P
                if n + 1 < QT * MH:
                    if n >= 1:
                        dve.wait_ge(exp_done, n)
                    mask_max(n + 1)
                dve.wait_ge(exp_done, n + 1)
                v(nv.reciprocal(LN[:, b:b + 1], LN[:, b:b + 1]))
                pb = EF[:, 512 * b:512 * b + nk]
                v(ts(pb, pb, LN[:, b:b + 1], None, ALU.mult), p_ready)
                dve.wait_ge(pt_full, n + 1)
                if n >= 2:
                    dve.wait_ge(pv_full, n - 1)
                v(cp(EF[:, 1024 + 512 * b:1024 + 512 * b + nk], PS[:, 2 + b, 0:nk]), pt_ready)
                dve.wait_ge(pv_full, n + 1)
                lo = MV * (h % 2)
                v(cp(B[lo:lo + MV, h // 2, q * P:(q + 1) * P], PS[lo:lo + MV, 4 + b, 0:P]), pv_done)

            v(ts(QP[:, 0:4, :], QB[:, 0:4, NP:T], VEC[:, KNN:KNN + 1], None, ALU.mult), hold=False)
            v(ts(QP[:, 4:6, :], QB[:, 4:6, NP:T], VEC[:, KNR:KNR + 1], None, ALU.mult), qp_ready)
            v(stt(PR, QB[:, 0:6, NP:T], SCALE * QK, O[:, 0:6, NP:T], ALU.mult, ALU.mult), qp_ready)
            v(nv.memset(NEW, -BIG))
            dve.wait_ge(ql_full, 1)
            for r in range(2):
                for u in range(2):
                    v(ts(QL[:, r, :, u:MH:2], PS[:, 3 * u, r * 32:(r + 1) * 32].rearrange("p (h s) -> p s h", h=4),
                         SCALE, None, ALU.mult), ql_ready)
            v(ts(QRS, PS[0:ROPE, 1, 0:64].rearrange("p (h s) -> p s h", h=MH), SCALE, None, ALU.mult), ql_ready)
            v(cp(NEW[0:1, :].rearrange("p (s h) -> p s h", s=NS), PS[0:1, 2, 0:64].rearrange("p (h s) -> p s h", h=MH)))
            for n in range(2):
                v(cp(TS[:, n:n + 1], EPST[:, :]), scores_taken)
            for n in range(PSL):
                v(cp(TS[:, n:n + 1], EPST[:, :]), page_used)
            with v.loop(NS, [(page_used, NPG), (scores_taken, 2)]) as i:
                for j in range(NPG):
                    dve.wait_ge(page_sq, i * NPG + (j + 1))
                    v(red(SSQ[:, bass.ds(i * 128 + j * 8, 8)], SQP[:, j % 4, :].rearrange("p (h d) -> p h d", h=MH),
                          AX.X, ALU.add), page_used)
                    if j % PSL == PSL - 1:
                        g = j // PSL
                        v(cp(SC[:, bass.ds(i * 128 + g * 64, 64)], PS[:, 4 + g, 0:64]), scores_taken)
            v(tt(SSQ.rearrange("p (n h) -> p n h", h=MH), SSQ.rearrange("p (n h) -> p n h", h=MH),
                 KRS.unsqueeze(2).to_broadcast([P, NS * NPG, MH]), ALU.add), ssq_ready)
            dve.wait_ge(krstd_ready, 1)
            v(tt(SC, SC, SSQ, ALU.mult))
            SC4 = SC.rearrange("p (s g h) -> p s g h", s=NS, g=NPG)
            v(red(MX.rearrange("p (s h) -> p s h", s=NS), SC4.rearrange("p s g h -> p s h g"), AX.X, ALU.max))
            v(tt(MX, MX, NEW, ALU.max), max_ready)
            dve.wait_ge(max_full, 1)
            v(red(MC, PS[0:64, 6, 0:P], AX.X, ALU.max))
            v(ts(DG, ident(64, 64), MC, None, ALU.mult), max_ready)
            dve.wait_ge(max_full, 2)
            v(cp(MX, PS[:, 7, 0:64]))
            v(tt(NEW, NEW, MX, ALU.subtract))
            v(tt(SC4, SC4, MX.rearrange("p (s h) -> p s h", s=NS).unsqueeze(2).to_broadcast([P, NS, NPG, MH]),
                 ALU.subtract), shifted)
            dve.wait_ge(p_exp, 1)
            v(red(LS.rearrange("p (s h) -> p s h", s=NS), SC4.rearrange("p s g h -> p s h g"), AX.X, ALU.add))
            v(tt(LS, LS, NEW, ALU.add), sum_ready)
            dve.wait_ge(sum_full, 1)
            v(nv.reciprocal(RLS, PS[:, 6, 0:64]))
            v(cp(PNB, PS[:, 6, 64:128]))
            v(cp(TS[:, 0:1], EPST[:, :]), acc_taken)
            with v.loop(NS, [(vec_order, 1), (acc_taken, 1)]) as i:
                dve.wait_ge(acc_full, i + 1)
                for r in range(2):
                    v(cp(OL[:, r, bass.ds(i, 1), :].rearrange("p a h -> p (a h)"), PS[:, r, 0:8]),
                      acc_taken if r else None)
            P3 = PNB.rearrange("p (s h) -> p s h", s=NS)
            M3X = MX.rearrange("p (s h) -> p s h", s=NS)
            for r in range(2):
                v(tt(M3X, P3, CKV[:, r, NP:T].unsqueeze(2).to_broadcast([P, NS, MH]), ALU.mult))
                v(tt(OL[:, r, :, :], OL[:, r, :, :], M3X, ALU.add))
                v(tt(OL[:, r, :, :], OL[:, r, :, :], RLS.rearrange("p (s h) -> p s h", s=NS), ALU.mult),
                  olat_ready if r else None)
            dve.wait_ge(osam_full, 1)
            v(cp(B[:, :, NP:T], PS[:, 4, 0:32].rearrange("p (k s) -> p k s", k=4)), attn_ready)
            residual("mout", 64)
            experts(1)


def tiles(w, n):
    k, m = w.shape
    return w.reshape(k // P, P, m // n, n).transpose(2, 1, 0, 3).reshape(m // n, P, k // P * n)


def turned(x):
    return x.T.reshape(x.shape[1] // P, P, x.shape[0]).transpose(1, 0, 2)


def column(w):
    return w.reshape(-1, P).T


def kernel(**inputs):
    import concourse.bacc as bacc
    from concourse.bass_utils import run_bass_kernel_spmd

    w = {k: np.asarray(a) for k, a in inputs.items()}
    const, const2 = constant_tables()
    gw = w["gla_w_in"][0]
    uq = w["mla_w_uq"][0].reshape(QR, MH, QK)
    uq = np.concatenate([uq[:, :, :NOPE].reshape(QR, -1), uq[:, :, NOPE:].reshape(QR, -1)], axis=1)
    dkv = w["kv_w_dkv"]
    dkv = np.concatenate([dkv[:, :KVR]] + [dkv[:, KVR:]] * 4, axis=1)
    uk, uv = w["kv_w_uk"].reshape(KVR, -1), w["kv_w_uv"].reshape(KVR, -1)
    ukv = np.concatenate([tiles(uk, 512)[0], tiles(uv, 512)[0], tiles(np.ascontiguousarray(uk.T), 256)[0]], axis=1)
    vec = np.concatenate(
        [column(w["mix_norm"][l]) for l in range(2)] + [column(w["ffn_norm"][l]) for l in range(2)]
        + [column(w["ada_b"].reshape(-1)), column(w["gla_b_gate"][0]), column(w["gla_out_norm"][0]),
           column(w["kv_in_norm"]), column(w["mla_q_lat_norm"][0]), column(w["kv_lat_norm"])]
        + [np.tile(g[a:b], P // (b - a))[:, None] for g in (w["mla_q_norm"][0], w["kv_k_norm"])
           for a, b in ((0, NOPE), (NOPE, QK))], axis=1)
    cache, cache_kr = w["cache_ckv"], w["cache_krope"]
    npool = cache.shape[0]
    ct = cache.reshape(npool, PAGE, 2, P).transpose(0, 3, 2, 1).reshape(npool, P, KVR)
    arrays = {
        "x": turned(np.concatenate([w["x_prompt"][0], w["x_sample"][:, 0]], axis=0)),
        "c": turned(np.concatenate([w["c_prompt"], w["c_sample"]], axis=0)),
        "const": const, "const2": const2, "vec": vec,
        "ada": np.stack([tiles(w["ada_w"][l], 512) for l in range(2)]).reshape(6, SLOTS, P, 4096),
        "gla": np.concatenate([tiles(gw[:, a:b], 512) for a, b in
                               ((0, 512), (512, 1024), (1024, 2048), (2048, 3072))] + [tiles(w["gla_w_out"][0], 512)]),
        "gate_low": tiles(gw[:, 3072:], GR)[0].reshape(P, KD, GR),
        "gate_up": w["gla_w_gate_up"][0],
        "router": np.stack([tiles(np.concatenate([w["moe_w_group"][l], w["moe_w_router"][l]], axis=1), 20)[0]
                            .reshape(P, KD, 20) for l in range(2)], axis=1),
        "router_b": np.concatenate([w["moe_b_group"], w["moe_b_router"]], axis=1),
        "moe_gu": np.stack([np.stack([tiles(np.concatenate([w["moe_w_gate"][l, e], w["moe_w_up"][l, e]], axis=1),
                                            512)[0] for e in range(NE)]) for l in range(2)])
        .reshape(2, NE // 2, 2, P, 4096),
        "moe_dn": np.stack([np.stack([tiles(w["moe_w_down"][l, e], D)[0] for e in range(NE)]) for l in range(2)])
        .reshape(2, NE // 2, 2, P, 2048),
        "dkv": tiles(dkv, QR)[0], "dq": tiles(w["mla_w_dq"][0], QR)[0], "uq": tiles(uq, MH * QK)[0], "ukv": ukv,
        "mwo": tiles(w["mla_w_out"][0], D)[0],
        "state_in": w["state_gla"][0].transpose(0, 2, 1, 3).reshape(NS, P, GH * DV),
        "cache_t": np.concatenate([ct, cache_kr], axis=2),
        "cache_kr": cache_kr.transpose(0, 2, 1),
        "cache": cache,
        "pages": w["page_table"].reshape(1, -1),
    }
    outs = {"y": (P, KD, T), "state_p": (P, GH * DV), "state_s": (NS, P, GH * DV), "ckv": (P, 2, T), "kr": (ROPE, T)}
    nc = bacc.Bacc("TRN2", target_bir_lowering=False, num_devices=1)
    io, args = {}, {}
    for name, a in arrays.items():
        a = np.ascontiguousarray(a)
        args[f"in_{name}"] = a
        io[name] = nc.dram_tensor(f"in_{name}", a.shape, mybir.dt.from_np(a.dtype), kind="ExternalInput").ap()
    for name, shape in outs.items():
        io[name] = nc.dram_tensor(f"out_{name}", shape, F32, kind="ExternalOutput").ap()
    io["gates"] = nc.dram_tensor("gates", (2, NE, T), F32, kind="Internal").ap()
    io["npool"] = npool
    trunk_program(nc, io)
    got = run_bass_kernel_spmd(nc, [args], core_ids=[0]).results[0]

    def back(a):
        return np.ascontiguousarray(a.transpose(2, 1, 0).reshape(T, -1))

    y, ckv, kr = back(got["out_y"]), back(got["out_ckv"]), np.ascontiguousarray(got["out_kr"].T)
    sp = got["out_state_p"].reshape(P, GH, DV).transpose(1, 0, 2)[None, None]
    ss = got["out_state_s"].reshape(NS, P, GH, DV).transpose(0, 2, 1, 3)[None]
    return (y[None, :NP], y[NP:, None], np.ascontiguousarray(sp), np.ascontiguousarray(ss),
            ckv[None, :NP], kr[None, :NP], ckv[NP:, None], kr[NP:, None])
```

```python
from contextlib import ExitStack, contextmanager

import numpy as np
import concourse.bass as bass
from concourse import mybir

F32 = mybir.dt.float32
I32 = mybir.dt.int32
U32 = mybir.dt.uint32
ALU = mybir.AluOpType
ACT = mybir.ActivationFunctionType
AX = mybir.AxisListType

P = 128
D = 1024
KD = D // P
NP, NS = 512, 8
T = NP + NS
HT = T // 2
QT = NP // P
EPS = 1e-6
GH, DK, DV, GR = 4, 128, 256, 16
C = 64
NC = NP // C
MH, NOPE, ROPE, MV = 8, 64, 32, 64
QK = NOPE + ROPE
QR, KVR = 384, 256
PAST, PAGE = 2048, 128
NPG = PAST // PAGE
PSL = 8
PROW = KVR + ROPE
NE, NG, NEG, FF = 16, 4, 4, 256
BIG = 1.0e30
CAP = 128
NCH = -(-T // CAP)
NOROW = float(1 << 20)
SLOTS = 4

ID, ONE, O1024, O256, O384, TRI, SCAN, RANK = 0, 128, 256, 384, 512, 640, 704, 1216
TRIS, IOTA, TOK = 1220, 1348, 1476
NCONST = 1481
B64, B32, E0, F0, K1, ROT, CAUS, COS, SIN = 0, 128, 256, 512, 768, 896, 1024, 1152, 1672
NCONST2 = 2192
MIXN, FFNN, ADAB, GBIAS, ONORM, KVIN, QLAT, KVLAT, QNN, QNR, KNN, KNR = 0, 16, 32, 128, 132, 134, 142, 145, 147, 148, 149, 150
NVEC = 151


def constant_tables():
    c = np.zeros((P, NCONST), np.float32)
    c[:, ID:ID + P] = np.eye(P)
    c[:, ONE:ONE + P] = 1.0
    c[:, O1024:O1024 + P] = 1.0 / D
    c[:, O256:O256 + P] = 1.0 / 256
    c[:, O384:O384 + P] = 1.0 / QR
    p = np.arange(P)
    c[:, TRI:TRI + C] = np.arange(C)[None, :] >= (p % C)[:, None]
    c[:, SCAN:SCAN + NP] = (np.arange(NP) % C != 0)[None, :]
    c[:, RANK:RANK + 4] = np.array([4.0, 3.0, 2.0, 1.0])
    c[:, TRIS:TRIS + P] = p[:, None] < p[None, :]
    c[:, IOTA:IOTA + P] = p[None, :]
    c[:, TOK:TOK + 5] = p[:, None] + P * np.arange(5)[None, :]
    m = np.zeros((P, NCONST2), np.float32)
    one = np.float32(1.0 / QK)
    half, quarter = p // NOPE, p // ROPE
    m[:, B64:B64 + P] = (half[:, None] == half[None, :]) * one
    m[:, B32:B32 + P] = (quarter[:, None] == quarter[None, :]) * one
    for u in range(2):
        m[:, E0 + u * P:E0 + (u + 1) * P] = (half[:, None] + 2 * u == quarter[None, :]) * one
        m[:, F0 + u * P:F0 + (u + 1) * P] = (quarter[:, None] == half[None, :] + 2 * u) * one
    m[:, K1:K1 + P] = (p < ROPE)[:, None] * one
    for i in range(P):
        j = i + ROPE // 2 if i % ROPE < ROPE // 2 else i - ROPE // 2
        m[j, ROT + i] = -1.0 if i % ROPE < ROPE // 2 else 1.0
    m[:, CAUS:CAUS + P] = np.where(p[None, :] <= p[:, None], 0.0, -BIG)
    inv = (np.float32(10000.0) ** (-np.arange(0, ROPE, 2, dtype=np.float32) / np.float32(ROPE))).astype(np.float32)
    pos = np.concatenate([np.arange(NP), np.full(NS, PAST)]).astype(np.float32)
    ang = (pos[:, None] * inv[None, :]).astype(np.float32)
    ang = np.tile(np.concatenate([ang, ang], axis=1), (1, P // ROPE)).T
    m[:, COS:COS + T] = np.cos(ang)
    m[:, SIN:SIN + T] = np.sin(ang)
    return c, m


STAGES = [("ada", 24), ("norm0", 1), ("qk", 8), ("glow", 1), ("gup", 4), ("v", 5), ("onorm", 4), ("r", 8), ("gout", 8)]
for _l in (0, 1):
    if _l:
        STAGES += [("kvnorm", 1), ("dkv", 3), ("ckvnorm", 1), ("krot", 1), ("norm2", 1), ("dq", 3), ("cqnorm", 1),
                   ("uq", 6), ("qrot", 2), ("qss", 6), ("uk", 4), ("kss", 6), ("uv", 4), ("mout", 8)]
    STAGES += [(f"fnorm{_l}", 1), (f"route{_l}", 1)]
FIRST = {}
_n = 0
for _s, _k in STAGES:
    FIRST[_s] = _n
    _n += _k

RING = {f"ada{j}": (j % SLOTS, j // SLOTS + 1) for j in range(24)}
_use = [6] * SLOTS
for _name, _slot in (("wq", 0), ("wk", 1), ("wv0", 2), ("wv1", 3), ("wr0", 0), ("wr1", 1), ("wo0", 2), ("wo1", 3),
                     ("moe0", None), ("dkv", 0), ("dq", 1), ("uq", 2), ("ukv", 3), ("mwo", 0), ("moe1", None)):
    if _slot is None:
        for _s in range(SLOTS):
            RING[f"{_name}_{_s}"] = (_s, _use[_s] + 1)
            _use[_s] += NE // 2
        continue
    _use[_slot] += 1
    RING[_name] = (_slot, _use[_slot])
LAST_USE = {"ada20": 21, "ada21": 22, "ada22": 23, "ada23": 24}
for _name, _stage, _k in (("wq", "qk", 4), ("wk", "qk", 8), ("wv0", "v", 5), ("wv1", "v", 5), ("wr0", "r", 4),
                          ("wr1", "r", 8), ("wo0", "gout", 4), ("wo1", "gout", 8), ("dkv", "dkv", 3), ("dq", "dq", 3),
                          ("uq", "uq", 6), ("mwo", "mout", 8)):
    LAST_USE[_name] = FIRST[_stage] + _k


class Turn:

    def __init__(self, stage):
        self.n, self.off = FIRST[stage], 0

    def count(self):
        return self.n + 1 + self.off

    def slot(self):
        return self.n % SLOTS


class Order:

    def __init__(self, eng, own):
        self.eng, self.own, self.c, self.open = eng, own, {}, []
        self.i, self.per = None, {}

    def value(self, sem):
        v = self.c[sem.name]
        return v if self.i is None else v + self.i * self.per.get(sem.name, 0)

    def __call__(self, ins, sem=None, hold=True):
        sem = sem or self.own
        self.c[sem.name] = self.c.get(sem.name, 0) + 1
        ins.then_inc(sem, 1)
        if sem not in self.open:
            self.open.append(sem)
        if hold:
            self.settle()

    def settle(self):
        for sem in self.open:
            self.eng.wait_ge(sem, self.value(sem))
        self.open = []

    @contextmanager
    def loop(self, trips, per):
        per = {s.name: k for s, k in per}
        start = dict(self.c)
        with self.eng.Fori(0, trips) as i:
            self.i, self.per = i, per
            yield i
            self.settle()
        self.i = None
        for name in set(self.c) | set(per):
            got = self.c.get(name, 0) - start.get(name, 0)
            assert got == per.get(name, 0), (name, got, per)
            self.c[name] = start.get(name, 0) + trips * got


def trunk_program(nc, io):
    with ExitStack() as ctx:
        def sb(name, shape, dt=F32):
            return ctx.enter_context(nc.sbuf_tensor(name, shape, dt))

        def sem(name):
            return ctx.enter_context(nc.semaphore(name))

        PS = ctx.enter_context(nc.psum_tensor("PS", [P, 8, 512], F32))
        CONST = sb("CONST", [P, NCONST])
        VEC = sb("VEC", [P, NVEC])
        WRT = sb("WRT", [P, 2, KD, NG + NE])
        BRT = sb("BRT", [P, 2, NG + NE])
        PTB = sb("PTB", [1, NS * NPG], I32)
        EPST = sb("EPST", [P, 1])
        CT = sb("CT", [P, KD, 1 + NS])
        IDX = sb("IDX", [P, NCH, NE], U32)
        HOLD = sb("HOLD", [1, 2])
        IDXO = sb("IDXO", [P, 1], U32)
        FLAG = sb("FLAG", [1, 2], I32)
        MOD = sb("MOD", [P, 2 * 6 * KD, 1 + NS])
        AM = sb("AM", [P, KD, 1 + NS])
        TS = sb("TS", [P, 2 * NS])
        RS = sb("RS", [P, 2, T])
        X = sb("X", [P, KD, T])
        H = sb("H", [P, KD, T])
        QB = sb("QB", [P, KD, T])
        O = sb("O", [P, KD, T])
        BE = sb("BE", [P, KD, T])
        VV = sb("VV", [P, 4096])
        VS = sb("VS", [NS, GH * DV])
        AT = sb("AT", [P, 1024])
        SST = sb("SST", [P, 3072])
        WB = sb("WB", [P, SLOTS, 4096])

        def ident(a=P, b=P, p=0, c=0):
            return CONST[p:p + a, ID + c:ID + c + b]

        def const(col, n=P, lo=0, hi=P):
            return CONST[lo:hi, col:col + n]

        def const2(col, n=P, lo=0, hi=P):
            return SST[lo:hi, col:col + n]

        B = BE[:, 0:4, :]
        E = BE[:, 4:8, :]
        EF = E.rearrange("p a b -> p (a b)")
        HF = H[:, :, :].rearrange("p a b -> p (a b)")
        MROW = HF[0:32, 0:2048].rearrange("p (s n) -> p s n", s=SLOTS)
        MTURN = HF[:, 2048:2560].rearrange("p (s n c) -> p s n c", s=SLOTS, n=4)
        V = VV[:, :].rearrange("p (t n) -> p t n", t=4)
        CKV = VV[:, 0:3 * T].rearrange("p (k t) -> p k t", k=3)
        VP = VV[:, 3 * T:3 * T + 2048].rearrange("p (k n) -> p k n", k=4)
        S = SST[:, 0:1024]
        ST = SST[:, 1024:3072].rearrange("p (b n) -> p b n", b=2)
        PG = WB[:, 1, 0:PSL * PROW].rearrange("p (k n) -> p k n", k=PSL)
        KRT = WB[0:ROPE, 2, 0:PSL * PAGE].rearrange("p (k n) -> p k n", k=PSL)
        CN = WB[:, 2, PSL * PAGE:PSL * (PAGE + KVR)].rearrange("p (k n) -> p k n", k=PSL)

        def two(ap):
            return ap.rearrange("p (a b) -> p a b", a=2)

        def halves(s, m=P):
            return PS[0:m, 2 * s:2 * s + 2, 0:HT]

        psum_full, psum_free = sem("psum_full"), sem("psum_free")
        ring_full = [sem(f"ring_full{s}") for s in range(SLOTS)]
        consts_in, x_in, mla_consts_in = sem("consts_in"), sem("x_in"), sem("mla_consts_in")
        gate_up_in, pages_in = sem("gate_up_in"), sem("page_table_in")
        vec_order, act_order = sem("vec_order"), sem("act_order")
        cond_silu, attn_ready = sem("cond_silu"), sem("attn_ready")
        mod_rows, mod_turned = sem("mod_rows"), sem("mod_turned")
        sq_ready, rms_ready, h_ready = sem("sq_ready"), sem("rms_ready"), sem("h_ready")
        glow_ready, softplus_ready, decay_ready, exp_ready = (sem("glow_ready"), sem("softplus_ready"),
                                                              sem("decay_ready"), sem("exp_ready"))
        decayed, prep_full, prep_done = sem("decayed"), sem("prep_full"), sem("prep_done")
        o_full, o_taken, state_ready = sem("gla_o_full"), sem("gla_o_taken"), sem("state_ready")
        ks_full, km_ready, outer_full, snew_ready, os_full = (sem("ks_full"), sem("km_ready"), sem("outer_full"),
                                                              sem("snew_ready"), sem("os_full"))
        st_in = [sem(f"st_in{b}") for b in range(2)]
        st_out = [sem(f"st_out{b}") for b in range(2)]
        y_stored = sem("y_stored")
        stored, silu_ready = sem("stored"), sem("silu_ready")
        route_exp_in, route_exp = sem("route_exp_in"), sem("route_exp")
        tok_full, tok_copied = sem("tok_full"), sem("tok_copied")
        tok_stored = [sem(f"tok_stored{b}") for b in range(2)]
        chosen, pos_full, rows_ready, idx_full, idx_ready = (sem("chosen"), sem("pos_full"), sem("rows_ready"),
                                                             sem("idx_full"), sem("idx_ready"))
        flag_ready = sem("flag_ready")
        xg_in = [sem(f"xg_in{b}") for b in range(2)]
        xt_full, xt_ready, gu_full, act_gated, hid_ready = (sem("xt_full"), sem("xt_ready"), sem("gu_full"),
                                                            sem("act_gated"), sem("hid_ready"))
        ht_full, ht_ready, down_full, y_dve, y_act = (sem("ht_full"), sem("ht_ready"), sem("down_full"),
                                                      sem("y_dve"), sem("y_act"))
        y_out = [sem(f"y_out{b}") for b in range(2)]
        pair_in = [sem(f"pair_in{b}") for b in range(2)]
        weighted = sem("weighted")
        mixed, mixed_full, pair_added = sem("mixed"), sem("mixed_full"), sem("pair_added")
        OVN = ("hold", "table", "table_full", "go", "x_in", "w_in", "xt_full", "xt", "gu_full", "silu", "hid", "ht_full",
               "ht", "down_full", "y", "out")
        more_step = [sem(f"more{l}_step") for l in range(2)]
        ov = [{n: sem(f"more{l}_{n}") for n in OVN} for l in range(2)]
        lat_ready, kr_ready, rope_ready = sem("lat_ready"), sem("kr_ready"), sem("rope_ready")
        sc_full, negmax_ready, exp_done, p_ready = sem("sc_full"), sem("negmax_ready"), sem("exp_done"), sem("p_ready")
        pt_full, pt_ready, pv_full, pv_done = sem("pt_full"), sem("pt_ready"), sem("pv_full"), sem("pv_done")
        qp_ready, ql_full, ql_ready = sem("qp_ready"), sem("ql_full"), sem("ql_ready")
        page_in = [sem(f"page_in{s}") for s in range(PSL)]
        cpage_in = [sem(f"cpage_in{s}") for s in range(PSL)]
        page_used, scores_taken, kn_full, page_sq = (sem("page_used"), sem("scores_taken"), sem("kn_full"),
                                                     sem("page_sq"))
        ssq_ready, krstd_ready, max_ready, max_full, shifted, p_exp = (sem("ssq_ready"), sem("krstd_ready"),
                                                                      sem("max_ready"), sem("max_full"),
                                                                      sem("shifted"), sem("p_exp"))
        sum_ready, sum_full, cpage_used, acc_full, acc_taken = (sem("sum_ready"), sem("sum_full"),
                                                                sem("cpage_used"), sem("acc_full"),
                                                                sem("acc_taken"))
        olat_ready, osam_full, y_ready = sem("olat_ready"), sem("osam_full"), sem("y_ready")

        SQ, n = {}, 0
        for s, k in (("norm0", KD), ("onorm", 1), ("fnorm0", KD), ("kvnorm", KD), ("ckvnorm", 1), ("norm2", KD),
                     ("cqnorm", 1), ("qss", 1), ("kss", 1), ("fnorm1", KD)):
            SQ[s] = n + 1
            n += k
        RMS, n = {}, 0
        for s, k in (("norm0", 1), ("onorm", 4), ("fnorm0", 1), ("kvnorm", 1), ("ckvnorm", 1), ("norm2", 1),
                     ("cqnorm", 1), ("qss", 6), ("kss", 6), ("fnorm1", 1)):
            RMS[s] = n
            n += k
        HR = {s: KD * n for n, s in enumerate(("norm0", "fnorm0", "kvnorm", "norm2", "fnorm1"))}
        SCALE = float(QK) ** -0.5
        LAYERS = ("moe0", "moe1")

        def rows_of(q):
            return P if q < QT else NS

        WGU, WG = AT[0:GR, 0:512], AT[:, 512:640].rearrange("p (k n) -> p k n", k=KD)
        BM, BL, FE = (SST[:, 1024 + 32 * i:1056 + 32 * i].rearrange("p (h c) -> p h c", h=GH) for i in range(3))
        QP, PR = (AT[:, 48 * i:48 * i + 48].rearrange("p (k s) -> p k s", k=6) for i in range(2))
        QL = AT[:, 96:224].rearrange("p (r s h) -> p r s h", r=2, s=NS)
        QRS = AT[0:ROPE, 224:288].rearrange("p (s h) -> p s h", s=NS)
        NEW, KRS, MX, LS, DG = AT[:, 288:352], AT[:, 352:480], AT[:, 480:544], AT[:, 544:608], AT[0:64, 608:672]
        OL = AT[:, 688:816].rearrange("p (r s h) -> p r s h", r=2, s=NS)
        RLS, PNB, MC = AT[:, 816:880], AT[:, 880:944], AT[0:64, 672:673]
        SC, SSQ = HF[:, 0:1024], HF[:, 1024:2048]
        SQP = HF[:, 2048:4096].rearrange("p (b n) -> p b n", b=4)
        ACC = HF[0:MH, 1024:3072].rearrange("p (s r n) -> p s r n", s=NS, r=2)
        LOG = AT[:, 0:100].rearrange("p (q n) -> p q n", q=5)
        GX, OHG, OH1, OH2, LE, TMP = (AT[:, 100 + 20 * i:120 + 20 * i].rearrange("p (q n) -> p q n", q=5)
                                      for i in range(6))
        M1, M2, M3, X2 = (AT[:, 220 + 5 * i:225 + 5 * i] for i in range(4))
        W1, W2 = AT[:, 240:245], AT[:, 245:250]
        PK = [AT[:, 256 + 5 * k:261 + 5 * k] for k in range(2)]
        PC = [AT[:, 266 + 5 * k:271 + 5 * k] for k in range(2)]
        QF = QB[:, :, :].rearrange("p a b -> p (a b)")
        OF = O[:, :, :].rearrange("p a b -> p (a b)")
        BF = BE[:, :, :].rearrange("p a b -> p (a b)")
        OPK = BF[:, 0:1280].rearrange("p (k q n) -> p k q n", k=2, q=5)
        AK = [BF[:, 1280 + 80 * k:1360 + 80 * k].rearrange("p (q e) -> p q e", q=5) for k in range(2)]
        AS, POS = (BF[:, 1440 + 80 * k:1520 + 80 * k].rearrange("p (q e) -> p q e", q=5) for k in range(2))
        RK = [BF[:, 1600 + 160 * k:1760 + 160 * k].rearrange("p (q a e) -> p q a e", q=5, a=2) for k in range(2)]
        ATMP = BF[:, 1920:2000].rearrange("p (q e) -> p q e", q=5)
        SG, HID, HT_ = ([BF[:, 2048 + 512 * a + 256 * b:2304 + 512 * a + 256 * b] for b in range(2)]
                        for a in range(3))
        XG = [QF[:, 1024 * b:1024 * (b + 1)] for b in range(2)]
        XT = [QF[:, 2048 + 1024 * b:3072 + 1024 * b].rearrange("p (k n) -> p k n", k=KD) for b in range(2)]
        YB = [OF[:, 1024 * b:1024 * (b + 1)] for b in range(2)]
        TOKB = [OF[:, 2048 + 1024 * b:3072 + 1024 * b] for b in range(2)]
        PAIR = [[QF[:, 2048 * b + 1024 * k:2048 * b + 1024 * (k + 1)] for k in range(2)] for b in range(2)]
        SEL = AT[:, 336:416].rearrange("p (q g e) -> p q g e", q=5, g=NG)
        NM, LN = TS[:, 0:2], TS[:, 2:4]

        block = ctx.enter_context(nc.Block())

        def load_pages(q, odd):
            mine = range(odd, PSL, 2)

            def number(g, j):
                return q.value_load(PTB[0:1, bass.ds(g * PSL + j, 1)], min_val=0, max_val=io["npool"] - 1)

            def fetch(dst, src, page, landed):
                q.dma_start(dst, io[src][bass.ds(page, 1)].rearrange("a p n -> p (a n)")).then_inc(landed, 16)

            q.wait_ge(psum_full, LAST_USE["uq"])
            with q.Fori(0, NS * NPG // PSL) as g:
                for j in mine:
                    page = number(g, j)
                    q.wait_ge(page_used, g * PSL + (j + 1))
                    fetch(PG[:, j, :], "cache_t", page, page_in[j])
                    fetch(KRT[:, j, :], "cache_kr", page, page_in[j])
            for j in mine:
                fetch(CN[:, j, :], "cache", number(0, j), cpage_in[j])
            with q.Fori(1, NS * NPG // PSL) as g:
                for j in mine:
                    page = number(g, j)
                    q.wait_ge(cpage_used, g * PSL + (j + 1 - PSL))
                    fetch(CN[:, j, :], "cache", page, cpage_in[j])

        @block.sync
        def _(sp):
            sp.dma_start(CT[:, :, :], io["c"]).then_inc(consts_in, 16)
            sp.dma_start(VEC[:, :], io["vec"]).then_inc(consts_in, 16)

            def load(name, src, before=None, part=None):
                slot, use = RING[name]
                dst = WB[:, slot, :] if part is None else WB[:, slot, part[0]:part[1]]
                if before:
                    sp.wait_ge(psum_full, LAST_USE[before])
                sp.dma_start(dst, src).then_inc(ring_full[slot], 16)

            for j in range(SLOTS):
                load(f"ada{j}", io["ada"][0, j])
            sp.dma_start(X[:, :, :], io["x"]).then_inc(x_in, 16)
            sp.dma_start(CONST[:, :], io["const"]).then_inc(x_in, 16)
            sp.dma_start(WRT[:, :, :, :], io["router"]).then_inc(x_in, 16)
            sp.dma_start(BRT[:, :, :], io["router_b"].partition_broadcast(P)).then_inc(x_in, 16)
            sp.dma_start(PTB[:, :], io["pages"]).then_inc(pages_in, 16)
            sp.dma_start(WGU, io["gate_up"]).then_inc(gate_up_in, 16)
            sp.dma_start(WG, io["gate_low"]).then_inc(gate_up_in, 16)
            with sp.Fori(1, 6) as i:
                for s in range(SLOTS):
                    sp.wait_ge(psum_full, i * SLOTS + (s + 1 - SLOTS))
                    sp.dma_start(WB[:, s, :], io["ada"][bass.ds(i, 1), s].rearrange("a p n -> p (a n)"))\
                        .then_inc(ring_full[s], 16)
            for j, (name, before) in enumerate((("wq", "ada20"), ("wk", "ada21"), ("wv0", "ada22"), ("wv1", "ada23"),
                                                ("wr0", "wq"), ("wr1", "wk"), ("wo0", "wv0"), ("wo1", "wv1"))):
                load(name, io["gla"][j], before)

            def moe(l, before):
                gu, dn = io["moe_gu"][l], io["moe_dn"][l]
                for e in range(2):
                    if l:
                        sp.wait_ge(osam_full, 1)
                    sp.wait_ge(psum_full, LAST_USE[before[e]])
                    sp.dma_start(WB[:, e, :], gu[0, e]).then_inc(ring_full[e], 16)
                    if before[2 + e] == "ukv":
                        sp.wait_ge(osam_full, 1)
                    else:
                        sp.wait_ge(psum_full, LAST_USE[before[2 + e]])
                    sp.dma_start(WB[:, 2 + e, 0:2048], dn[0, e]).then_inc(ring_full[2 + e], 16)
                with sp.Fori(1, NE // 2) as i:
                    for e in range(2):
                        sp.wait_ge(gu_full, i * 2 + (NE * l + e - 1))
                        sp.dma_start(WB[:, e, :], gu[bass.ds(i, 1), e].rearrange("a p n -> p (a n)"))\
                            .then_inc(ring_full[e], 16)
                        sp.wait_ge(down_full, i * 2 + (NE * l + e - 1))
                        sp.dma_start(WB[:, 2 + e, 0:2048], dn[bass.ds(i, 1), e].rearrange("a p n -> p (a n)"))\
                            .then_inc(ring_full[2 + e], 16)
                o = ov[l]
                gun, dnn = gu.rearrange("i e p n -> (i e) p n"), dn.rearrange("i e p n -> (i e) p n")
                sp.wait_ge(flag_ready, l + 1)
                most = sp.value_load(FLAG[0:1, l:l + 1], min_val=0, max_val=T)
                with sp.If(most > CAP):
                    with sp.Fori(0, NE) as e:
                        for c in range(NCH - 1):
                            sp.wait_ge(o["go"], e * (NCH - 1) + (c + 1))
                            sp.dma_start(WB[:, 0, :], gun[bass.ds(e, 1)].rearrange("a p n -> p (a n)"))\
                                .then_inc(o["w_in"], 16)
                            sp.dma_start(WB[:, 2, 0:2048], dnn[bass.ds(e, 1)].rearrange("a p n -> p (a n)"))\
                                .then_inc(o["w_in"], 16)
                    sp.wait_ge(o["down_full"], NE * (NCH - 1))
                sp.wait_ge(gu_full, NE * (l + 1))
                sp.wait_ge(down_full, NE * (l + 1))

            moe(0, ("wr0", "wr1", "wo0", "wo1"))
            sp.wait_ge(mixed, 3)
            load("dkv", io["dkv"], part=(0, KD * QR))
            load("dq", io["dq"], part=(0, KD * QR))
            load("uq", io["uq"], part=(0, 3 * MH * QK))
            load("ukv", io["ukv"], part=(0, 3072))
            load("mwo", io["mwo"], "dkv")

            sp.wait_ge(pages_in, 16)
            load_pages(sp, 0)
            moe(1, ("mwo", "dq", "uq", "ukv"))
            sp.wait_ge(y_ready, 1)
            sp.dma_start(io["y"], X[:, :, :]).then_inc(y_stored, 16)
            sp.wait_ge(y_stored, 16)
            sp.wait_ge(stored, 16 * 3)
            for b in range(2):
                sp.wait_ge(st_out[b], 16 * NS // 2)

        @block.gpsimd
        def _(pool):
            pool.wait_ge(exp_ready, 1)
            pool.wait_ge(state_ready, NC)
            for b in range(NS):
                if b >= 2:
                    pool.wait_ge(os_full, b - 1)
                    pool.wait_ge(st_out[b % 2], 16 * (b // 2))
                pool.dma_start(ST[:, b % 2, :], io["state_in"][b]).then_inc(st_in[b % 2], 16)
                if b == 0:
                    pool.dma_start(io["state_p"], S).then_inc(stored, 16)
                if b >= 1:
                    pool.wait_ge(snew_ready, GH * b)
                    pool.dma_start(io["state_s"][b - 1], ST[:, (b - 1) % 2, :]).then_inc(st_out[(b - 1) % 2], 16)
            pool.wait_ge(snew_ready, GH * NS)
            pool.dma_start(io["state_s"][NS - 1], ST[:, 1, :]).then_inc(st_out[1], 16)
            pool.wait_ge(stored, 16)
            for b in range(2):
                pool.wait_ge(st_out[b], 16 * NS // 2)
            pool.wait_ge(os_full, NS)
            pool.dma_start(SST[:, 0:NCONST2], io["const2"]).then_inc(mla_consts_in, 16)

            def experts(l):
                o, h = ov[l], HOLD[:, l:l + 1]

                def hold_wait(name, e, c, k):
                    pool.wait_ge(o["hold"], e * (2 * (NCH - 1)) + (2 * c + k + 1))
                    pool.wait_ge(o[name], e * (NCH - 1) + (c + 1))
                    nc.gpsimd.tensor_tensor(h, h, h, ALU.add).then_inc(o["hold"], 1)

                def gather(e):
                    b = e % 2
                    if e >= 2:
                        pool.wait_ge(xt_full, NE * l + e - 1)
                    pool.indirect_dma_start(XG[b], None, io["rows"], bass.IndirectOffsetOnAxis(IDX[:, 0, e:e + 1], 0),
                                            bounds_check=2 * T - 1, oob_is_err=False).then_inc(xg_in[b], 16)

                pool.wait_ge(idx_ready, l + 1)
                for b in range(2):
                    pool.wait_ge(tok_stored[b], (96, 64)[b] * (l + 1))
                gather(0)
                gather(1)
                for e in range(NE):
                    if e + 2 < NE:
                        gather(e + 2)
                    pool.wait_ge(y_dve, NE * l + e + 1)
                    pool.wait_ge(y_act, NE * l + e + 1)
                    pool.indirect_dma_start(io["outs"], bass.IndirectOffsetOnAxis(IDX[:, 0, e:e + 1], 0), YB[e % 2],
                                            None, bounds_check=2 * T - 1, oob_is_err=False)\
                        .then_inc(y_out[e % 2], 16)
                most = pool.value_load(FLAG[0:1, l:l + 1], min_val=0, max_val=T)
                with pool.If(most > CAP):
                    nc.gpsimd.memset(h, 0.0).then_inc(o["hold"], 1)
                    with pool.Fori(0, NE) as e:
                        for c in range(NCH - 1):
                            hold_wait("go", e, c, 0)
                            pool.indirect_dma_start(XG[0], None, io["rows"], bass.IndirectOffsetOnAxis(IDXO[:, 0:1], 0),
                                                    bounds_check=2 * T - 1, oob_is_err=False)\
                                .then_inc(o["x_in"], 16)
                            hold_wait("y", e, c, 1)
                            pool.indirect_dma_start(io["outs"], bass.IndirectOffsetOnAxis(IDXO[:, 0:1], 0), YB[0],
                                                    None, bounds_check=2 * T - 1, oob_is_err=False)\
                                .then_inc(o["out"], 16)
                    pool.wait_ge(o["out"], 16 * NE * (NCH - 1))
                for b in range(2):
                    pool.wait_ge(y_out[b], 8 * NE * (l + 1))

            experts(0)
            pool.wait_ge(lat_ready, 1)
            pool.dma_start(io["ckv"], CKV[:, 0:2, :]).then_inc(stored, 16)
            pool.wait_ge(kr_ready, 1)
            pool.dma_start(io["kr"], CKV[0:ROPE, 2, :]).then_inc(stored, 16)
            pool.wait_ge(pages_in, 16)
            load_pages(pool, 1)

            experts(1)

        @block.tensor
        def _(pe):
            mm = nc.tensor.matmul

            def slot_for(t):
                pe.wait_ge(psum_free, t.count())
                s = t.slot()
                t.n += 1
                return s

            def product(t, pairs, m=P, ready=None):
                s = slot_for(t)
                for a in range(2):
                    for k, (w, x) in enumerate(pairs):
                        if ready and not a:
                            pe.wait_ge(ready[0], ready[1] + k)
                        last = mm(PS[0:m, 2 * s + a, 0:HT], w, x[:, a * HT:(a + 1) * HT],
                                  start=(k == 0), stop=(k == len(pairs) - 1))
                last.then_inc(psum_full, 1)

            def chunk(name):
                slot, use = RING[name]
                pe.wait_ge(ring_full[slot], 16 * use)
                return slot

            pe.wait_ge(cond_silu, 1)
            with pe.Fori(0, 6) as i:
                for s in range(SLOTS):
                    pe.wait_ge(psum_free, i * SLOTS + (s + 1))
                    pe.wait_ge(ring_full[s], i * 16 + 16)
                    w = WB[:, s, :].rearrange("p (k n) -> p k n", k=KD)
                    for k in range(KD):
                        last = mm(PS[0:1 + NS, 2 * s, :], CT[:, k, :], w[:, k, :], start=(k == 0), stop=(k == KD - 1))
                    last.then_inc(psum_full, 1)

            def mean_square(stage, rows, avg):
                t = Turn(stage)
                if len(rows) == KD:
                    product(t, [(avg, r) for r in rows], ready=(sq_ready, SQ[stage]))
                else:
                    pe.wait_ge(sq_ready, SQ[stage])
                    product(t, [(avg, r) for r in rows])

            def stream(stage, n):
                return None if n else (h_ready, HR[stage] + 1)

            pe.wait_ge(x_in, 64)
            mean_square("norm0", [H[:, k, :] for k in range(KD)], const(O1024))

            t = Turn("qk")
            for name in ("wq", "wk"):
                w = WB[:, chunk(name), :].rearrange("p (k n) -> p k n", k=KD)
                for n in range(4):
                    product(t, [(w[:, k, n * P:(n + 1) * P], H[:, k, :]) for k in range(KD)],
                            ready=stream("norm0", n) if name == "wq" else None)
            pe.wait_ge(gate_up_in, 32)
            product(Turn("glow"), [(WG[:, k, :], H[:, k, :]) for k in range(KD)], m=GR)
            pe.wait_ge(glow_ready, 1)
            t = Turn("gup")
            for n in range(4):
                product(t, [(WGU[:, n * P:(n + 1) * P], EF[0:GR, 0:T])])
            t = Turn("v")
            w = [WB[:, chunk(f"wv{a}"), :].rearrange("p (k n) -> p k n", k=KD) for a in range(2)]
            for q in range(5):
                m = P if q < QT else NS
                s = slot_for(t)
                for a in range(2):
                    for k in range(KD):
                        last = mm(PS[0:m, 2 * s + a, :], H[:, k, q * P:q * P + m], w[a][:, k, :],
                                  start=(k == 0), stop=(k == KD - 1))
                last.then_inc(psum_full, 1)

            pe.wait_ge(decayed, 2)
            for q in range(QT):
                if q >= 2:
                    pe.wait_ge(prep_done, 2 * (q - 1))
                for h in range(GH):
                    nc.tensor.transpose(PS[:, q % 2, h * P:(h + 1) * P], QB[:, 4 + h, q * P:(q + 1) * P], ident())
                    for a in range(2):
                        sl = slice(q * P + a * C, q * P + (a + 1) * C)
                        last = mm(PS[a * C:(a + 1) * C, 2 + q % 2, h * C:(h + 1) * C], QB[:, 4 + h, sl], QB[:, h, sl],
                                  start=True, stop=True)
                last.then_inc(prep_full, 1)
            for c in range(NC):
                q, lo = c // 2, C * (c % 2)
                if c == 0:
                    pe.wait_ge(prep_done, 2 * QT)
                if c >= 2:
                    pe.wait_ge(state_ready, c - 1)
                    pe.wait_ge(o_taken, c - 1)
                for h in range(GH):
                    mm(PS[:, 2 * (c % 2) + h // 2, (h % 2) * DV:(h % 2 + 1) * DV],
                       EF[lo:lo + C, q * 512 + h * DK:q * 512 + (h + 1) * DK],
                       V[lo:lo + C, q, h * DV:(h + 1) * DV], start=True, stop=True)
                if c >= 1:
                    pe.wait_ge(state_ready, c)
                for n in range(2 * GH):
                    h = n // 2
                    out = PS[:, 4 + c % 2, n * C:(n + 1) * C]
                    last = mm(out, V[lo:lo + C, q, n * P:(n + 1) * P],
                              AT[lo:lo + C, q * 256 + h * C:q * 256 + (h + 1) * C], start=True, stop=(c == 0))
                    if c >= 1:
                        last = mm(out, S[:, n * P:(n + 1) * P], QB[:, h, c * C:(c + 1) * C], start=False, stop=True)
                last.then_inc(o_full, 1)
            for h in range(GH):
                last = nc.tensor.transpose(PS[0:NS, 6, h * P:(h + 1) * P], QB[:, 4 + h, NP:T], ident())
            last.then_inc(ks_full, 1)

            def outer(b):
                pe.wait_ge(km_ready, b + 1)
                if b >= 2:
                    pe.wait_ge(snew_ready, GH * (b - 1))
                if b == 0:
                    pe.wait_ge(state_ready, NC)
                for h in range(GH):
                    last = mm(PS[:, 2 * (b % 2) + h // 2, (h % 2) * DV:(h % 2 + 1) * DV],
                              EF[0:NS, 512 * (1 + b % 2) + h * DK:512 * (1 + b % 2) + (h + 1) * DK],
                              VS[:, h * DV:(h + 1) * DV], start=True, stop=True)
                last.then_inc(outer_full, 1)

            outer(0)
            for b in range(NS):
                if b + 1 < NS:
                    outer(b + 1)
                pe.wait_ge(snew_ready, GH * (b + 1))
                for n in range(2 * GH):
                    last = mm(PS[:, 7, b * 8 + n:b * 8 + n + 1], ST[:, b % 2, n * P:(n + 1) * P],
                              QB[:, n // 2, NP + b:NP + b + 1], start=True, stop=True)
                last.then_inc(os_full, 1)

            pe.wait_ge(sq_ready, SQ["onorm"])
            t = Turn("onorm")
            for h in range(GH):
                product(t, [(const(O256), BE[:, 2 * h + a, :]) for a in range(2)])
            t = Turn("r")
            for name in ("wr0", "wr1"):
                w = WB[:, chunk(name), :].rearrange("p (k n) -> p k n", k=KD)
                for n in range(4):
                    product(t, [(w[:, k, n * P:(n + 1) * P], H[:, k, :]) for k in range(KD)])
            pe.wait_ge(psum_free, SLOTS + FIRST["r"] + 8)
            t = Turn("gout")
            for name in ("wo0", "wo1"):
                w = WB[:, chunk(name), :].rearrange("p (k n) -> p k n", k=KD)
                for n in range(4):
                    product(t, [(w[:, k, n * P:(n + 1) * P], O[:, k, :]) for k in range(KD)])

            def experts(l):
                mean_square(f"fnorm{l}", [H[:, k, :] for k in range(KD)], const(O1024))
                t = Turn(f"route{l}")
                s = slot_for(t)
                for q in range(5):
                    m = P if q < QT else NS
                    for k in range(KD):
                        if q == 0:
                            pe.wait_ge(h_ready, HR[f"fnorm{l}"] + k + 1)
                        last = mm(PS[0:m, 2 * s, q * 20:q * 20 + 20], H[:, k, q * P:q * P + m], WRT[:, l, k, :],
                                  start=(k == 0), stop=(k == KD - 1))
                last.then_inc(psum_full, 1)
                for q in range(5):
                    b = 2 * ((s + 1 + q % 2) % SLOTS)
                    if q >= 2:
                        pe.wait_ge(tok_copied, 5 * l + q - 1)
                    for k in range(KD):
                        m = rows_of(q)
                        last = nc.tensor.transpose(PS[0:m, b + k // 4, (k % 4) * P:(k % 4 + 1) * P],
                                                   H[:, k, q * P:q * P + m], ident())
                    last.then_inc(tok_full, 1)
                pe.wait_ge(tok_copied, 5 * l + 5)
                pe.wait_ge(chosen, l + 1)
                for q in range(5):
                    m = rows_of(q)
                    for a in range(q):
                        mm(PS[0:m, 0, q * NE:(q + 1) * NE], const(ONE, m), AS[:, a, :], start=(a == 0), stop=False)
                    mm(PS[0:m, 0, q * NE:(q + 1) * NE], const(TRIS, m, 0, m), AS[0:m, q, :], start=(q == 0), stop=True)
                for q in range(5):
                    m = rows_of(q)
                    last = mm(PS[:, 1, 0:NE], const(ONE, P, 0, m), AS[0:m, q, :], start=(q == 0), stop=(q == QT))
                last.then_inc(pos_full, 1)

                def index_table(bank):
                    for q in range(5):
                        m = rows_of(q)
                        for k in range(2):
                            last = mm(PS[:, bank, 0:2 * NE], OPK[0:m, k, q, :],
                                      RK[k][0:m, q, :, :].rearrange("p a e -> p (a e)"),
                                      start=(q + k == 0), stop=(q + k == QT + 1))
                    return last

                pe.wait_ge(rows_ready, l + 1)
                index_table(2).then_inc(idx_full, 1)

                base, name = NE * l, LAYERS[l]

                def turn_rows(n, b, x_in, count, done):
                    pe.wait_ge(x_in, count)
                    for k in range(KD):
                        last = nc.tensor.transpose(PS[:, k // 4, (k % 4) * P:(k % 4 + 1) * P],
                                                   XG[b][:, k * P:(k + 1) * P], ident())
                    last.then_inc(done, 1)

                def gate_up(b, wslot, ks, bank):
                    w = WB[:, wslot, :].rearrange("p (k n) -> p k n", k=KD)
                    for k in ks:
                        last = mm(PS[:, bank, :], XT[b][:, k, :], w[:, k, :], start=(k == 0), stop=(k == KD - 1))
                    return last

                def turn_hidden(b):
                    for f in range(2):
                        last = nc.tensor.transpose(PS[:, 4, f * P:(f + 1) * P], HID[b][:, f * P:(f + 1) * P], ident())
                    return last

                def down(b, wslot):
                    w = WB[:, wslot, 0:2048].rearrange("p (f n) -> p f n", f=2)
                    for a in range(2):
                        for f in range(2):
                            last = mm(PS[:, 5 + a, :], HT_[b][:, f * P:(f + 1) * P], w[:, f, a * 512:(a + 1) * 512],
                                      start=(f == 0), stop=(f == 1))
                    return last

                def first_half(i, e):
                    if not (isinstance(i, int) and 2 * i + e == 0):
                        pe.wait_ge(xt_ready, i * 2 + (base + e))
                    turn_rows(0, e, xg_in[e], i * 16 + (128 * l + 16), xt_full)
                    pe.wait_ge(xt_ready, i * 2 + (base + e + 1))
                    pe.wait_ge(ring_full[e], i * 16 + 16 * RING[f"{name}_{e}"][1])
                    gate_up(e, e, range(KD // 2), 2 + e)

                def rest(i, e):
                    gate_up(e, e, range(KD // 2, KD), 2 + e).then_inc(gu_full, 1)

                def hidden(i, e):
                    pe.wait_ge(hid_ready, i * 2 + (base + e + 1))
                    turn_hidden(e).then_inc(ht_full, 1)

                def finish(i, e):
                    pe.wait_ge(ht_ready, i * 2 + (base + e + 1))
                    pe.wait_ge(ring_full[2 + e], i * 16 + 16 * RING[f"{name}_{2 + e}"][1])
                    if not (isinstance(i, int) and 2 * i + e == 0):
                        pe.wait_ge(y_dve, i * 2 + (base + e))
                        pe.wait_ge(y_act, i * 2 + (base + e))
                    down(e, 2 + e).then_inc(down_full, 1)

                def step(i, e):
                    first_half(i, e) if e else first_half(i, 0)
                    prev = (i, 0) if e else (i - 1, 1)
                    hidden(*prev)
                    rest(i, e)
                    finish(*prev)

                first_half(0, 0)
                rest(0, 0)
                step(0, 1)
                with pe.Fori(1, NE // 2) as i:
                    step(i, 0)
                    step(i, 1)
                hidden(NE // 2 - 1, 1)
                finish(NE // 2 - 1, 1)

                o = ov[l]
                most = pe.value_load(FLAG[0:1, l:l + 1], min_val=0, max_val=T)
                with pe.If(most > CAP):
                    for c in range(NCH - 1):
                        pe.wait_ge(o["table"], c + 1)
                        index_table(7).then_inc(o["table_full"], 1)
                    with pe.Fori(0, NE) as e:
                        for c in range(NCH - 1):
                            n = e * (NCH - 1) + (c + 1)
                            turn_rows(0, 0, o["x_in"], e * (16 * (NCH - 1)) + 16 * (c + 1), o["xt_full"])
                            pe.wait_ge(o["xt"], n)
                            pe.wait_ge(o["w_in"], e * (32 * (NCH - 1)) + 32 * (c + 1))
                            gate_up(0, 0, range(KD), 2).then_inc(o["gu_full"], 1)
                            pe.wait_ge(o["hid"], n)
                            turn_hidden(0).then_inc(o["ht_full"], 1)
                            pe.wait_ge(o["ht"], n)
                            down(0, 2).then_inc(o["down_full"], 1)

                for q in range(5):
                    m = rows_of(q)
                    b = 2 * (q % 2)
                    if q >= 2:
                        pe.wait_ge(pair_added, 5 * l + q - 1)
                    pe.wait_ge(mixed, 5 * l + q + 1)
                    for k in range(KD):
                        last = nc.tensor.transpose(PS[:, b + k // 4, (k % 4) * P:(k % 4) * P + m],
                                                   PAIR[q % 2][0][0:m, k * P:(k + 1) * P], ident(m, m))
                    last.then_inc(mixed_full, 1)

            experts(0)

            mean_square("kvnorm", [H[:, k, :] for k in range(KD)], const(O1024))
            t = Turn("dkv")
            w = WB[:, chunk("dkv"), 0:KD * QR].rearrange("p (k n) -> p k n", k=KD)
            for n in range(3):
                product(t, [(w[:, k, n * P:(n + 1) * P], H[:, k, :]) for k in range(KD)],
                        ready=stream("kvnorm", n))
            mean_square("ckvnorm", [E[:, k, :] for k in range(2)], const(O256))
            pe.wait_ge(mla_consts_in, 16)
            product(Turn("krot"), [(const2(ROT), CKV[:, 2, :])])

            mean_square("norm2", [H[:, k, :] for k in range(KD)], const(O1024))
            t = Turn("dq")
            w = WB[:, chunk("dq"), 0:KD * QR].rearrange("p (k n) -> p k n", k=KD)
            for n in range(3):
                product(t, [(w[:, k, n * P:(n + 1) * P], H[:, k, :]) for k in range(KD)],
                        ready=stream("norm2", n))
            mean_square("cqnorm", [E[:, k, :] for k in range(3)], const(O384))
            pe.wait_ge(lat_ready, 2)
            t = Turn("uq")
            w = WB[:, chunk("uq"), 0:3 * MH * QK].rearrange("p (k n) -> p k n", k=3)
            for n in range(6):
                product(t, [(w[:, k, n * P:(n + 1) * P], B[:, k, :]) for k in range(3)])
            pe.wait_ge(psum_free, SLOTS + t.n)
            t = Turn("qrot")
            for j in range(2):
                product(t, [(const2(ROT), QB[:, 4 + j, :])])
            pe.wait_ge(sq_ready, SQ["qss"])
            t = Turn("qss")
            for m in range(4):
                product(t, [(const2(B64), H[:, m, :]), (const2(F0 + (m % 2) * P), H[:, 4 + m // 2, :])])
            for j in range(2):
                product(t, [(const2(B32), H[:, 4 + j, :])]
                        + [(const2(E0 + u * P), H[:, 2 * j + u, :]) for u in range(2)])
            chunk("ukv")
            wukv = WB[:, RING["ukv"][0], :]
            t = Turn("uk")
            for n in range(4):
                product(t, [(wukv[:, k * 512 + n * P:k * 512 + (n + 1) * P], CKV[:, k, :]) for k in range(2)])
            pe.wait_ge(sq_ready, SQ["kss"])
            t = Turn("kss")
            for m in range(4):
                product(t, [(const2(B64), H[:, m, :]), (const2(K1), H[:, 4, :])])
            for j in range(2):
                product(t, [(const2(K1), H[:, 4, :])]
                        + [(const2(E0 + u * P), H[:, 2 * j + u, :]) for u in range(2)])
            t = Turn("uv")
            for q in range(QT):
                s = slot_for(t)
                for k in range(2):
                    last = mm(PS[:, 2 * s, :], CKV[:, k, q * P:(q + 1) * P],
                              wukv[:, 1024 + k * 512:1536 + k * 512], start=(k == 0), stop=(k == 1))
                last.then_inc(psum_full, 1)

            pe.wait_ge(psum_free, SLOTS + FIRST["uv"] + 4)
            pe.wait_ge(qp_ready, 2)
            for r in range(2):
                for h in range(MH):
                    lo = NOPE * (h % 2)
                    mm(PS[:, 3 * (h % 2), (r * 4 + h // 2) * 8:(r * 4 + h // 2) * 8 + 8],
                       wukv[lo:lo + NOPE, 2048 + (h // 2) * 256 + r * P:2048 + (h // 2) * 256 + (r + 1) * P],
                       QP[lo:lo + NOPE, h // 2, :], start=True, stop=True)
            for h in range(MH):
                mm(PS[0:ROPE, 1, h * 8:h * 8 + 8], ident(P, ROPE, 0, ROPE * (h % 4)), QP[:, 4 + h // 4, :],
                   start=True, stop=True)
            for h in range(MH):
                mm(PS[0:1, 2, h * 8:h * 8 + 8], const2(B64 + NOPE * (h % 2), 1), PR[:, h // 2, :],
                   start=True, stop=False)
                last = mm(PS[0:1, 2, h * 8:h * 8 + 8], const2(B32 + ROPE * (h % 4), 1), PR[:, 4 + h // 4, :],
                          start=False, stop=True)
            last.then_inc(ql_full, 1)
            pe.wait_ge(ql_ready, 6)

            def scores(n):
                q, h = n // MH, n % MH
                nk = (q + 1) * P
                if n >= 2:
                    pe.wait_ge(exp_done, n - 1)
                lo, lr = NOPE * (h % 2), ROPE * (h % 4)
                mm(PS[:, n % 2, 0:nk], QB[lo:lo + NOPE, h // 2, q * P:(q + 1) * P], O[lo:lo + NOPE, h // 2, 0:nk],
                   start=True, stop=False)
                mm(PS[:, n % 2, 0:nk], QB[lr:lr + ROPE, 4 + h // 4, q * P:(q + 1) * P],
                   O[lr:lr + ROPE, 4 + h // 4, 0:nk], start=False, stop=True).then_inc(sc_full, 1)

            def page_scores(g):
                i, sl = g // NPG, g % PSL
                pe.wait_ge(page_in[sl], 32 * (g // PSL + 1))
                if sl == 0 and g // PSL >= 2:
                    pe.wait_ge(scores_taken, g // PSL - 1)
                if g >= 2:
                    pe.wait_ge(page_sq, g - 1)
                out = PS[:, 3 + 2 * (g // PSL % 2), 8 * sl:8 * sl + 8]
                for r in range(2):
                    mm(out, PG[:, sl, r * P:(r + 1) * P], QL[:, r, i, :], start=(r == 0), stop=False)
                mm(out, KRT[:, sl, :], QRS[:, i, :], start=False, stop=True)
                for r in range(2):
                    last = mm(PS[:, 6 + g % 2, :], PG[:, sl, r * P:(r + 1) * P], wukv[:, r * 512:(r + 1) * 512],
                              start=(r == 0), stop=(r == 1))
                last.then_inc(kn_full, 1)

            scores(0)
            for n in range(QT * MH):
                q, h = n // MH, n % MH
                if n + 1 < QT * MH:
                    scores(n + 1)
                page_scores(4 * n)
                page_scores(4 * n + 1)
                pe.wait_ge(p_ready, n + 1)
                for k in range(q + 1):
                    last = nc.tensor.transpose(PS[:, 2, k * P:(k + 1) * P],
                                               EF[:, 512 * (n % 2) + k * P:512 * (n % 2) + (k + 1) * P], ident())
                last.then_inc(pt_full, 1)
                page_scores(4 * n + 2)
                page_scores(4 * n + 3)
                pe.wait_ge(pt_ready, n + 1)
                if n >= 1:
                    pe.wait_ge(pv_done, n)
                lo = MV * (h % 2)
                for k in range(q + 1):
                    last = mm(PS[lo:lo + MV, 4, 0:P], VP[:, k, h * MV:(h + 1) * MV],
                              EF[:, 1024 + 512 * (n % 2) + k * P:1024 + 512 * (n % 2) + (k + 1) * P],
                              start=(k == 0), stop=(k == q))
                last.then_inc(pv_full, 1)

            pe.wait_ge(max_ready, 1)
            nc.tensor.transpose(PS[0:64, 6, 0:P], MX, ident()).then_inc(max_full, 1)
            pe.wait_ge(max_ready, 2)
            mm(PS[:, 7, 0:64], const(ONE, P, 0, 64), DG, start=True, stop=True).then_inc(max_full, 1)
            pe.wait_ge(sum_ready, 1)
            mm(PS[:, 6, 0:64], const(ONE), LS, start=True, stop=True)
            mm(PS[:, 6, 64:128], const(ONE, P, 0, 1), NEW[0:1, :], start=True, stop=True).then_inc(sum_full, 1)
            for g in range(NS * NPG):
                i, j, sl = g // NPG, g % NPG, g % PSL
                pe.wait_ge(cpage_in[sl], 16 * (g // PSL + 1))
                last = mm(PS[0:MH, i // 2, (i % 2) * KVR:(i % 2 + 1) * KVR], HF[:, g * MH:(g + 1) * MH], CN[:, sl, :],
                          start=(j == 0), stop=(j == NPG - 1))
                last.then_inc(cpage_used, 1)
            for i in range(NS):
                pe.wait_ge(acc_taken, i // 2 + 1)
                for r in range(2):
                    last = nc.tensor.transpose(PS[:, 5, r * 64 + i * MH:r * 64 + (i + 1) * MH], ACC[:, i, r, :],
                                               ident(MH, MH))
            last.then_inc(acc_full, 1)
            pe.wait_ge(olat_ready, 1)
            for h in range(MH):
                lo = MV * (h % 2)
                for r in range(2):
                    last = mm(PS[lo:lo + MV, 4, (h // 2) * 8:(h // 2) * 8 + 8],
                              wukv[:, 1024 + r * 512 + h * MV:1024 + r * 512 + (h + 1) * MV], OL[:, r, :, h],
                              start=(r == 0), stop=(r == 1))
            last.then_inc(osam_full, 1)
            pe.wait_ge(attn_ready, 1)
            t = Turn("mout")
            w = WB[:, chunk("mwo"), :].rearrange("p (k n) -> p k n", k=4)
            for n in range(KD):
                product(t, [(w[:, k, n * P:(n + 1) * P], B[:, k, :]) for k in range(4)])
            experts(1)

        @block.scalar
        def _(act):
            a = Order(act, act_order)
            f = nc.scalar.activation
            act.wait_ge(consts_in, 32)
            a(f(CT[:, :, :], CT[:, :, :], ACT.Silu), cond_silu)
            act.wait_ge(psum_free, SLOTS)
            with a.loop(6, [(mod_rows, SLOTS)]) as i:
                for s in range(SLOTS):
                    act.wait_ge(psum_full, i * SLOTS + (s + 1))
                    a(f(MROW[0:1 + NS, s, :], PS[0:1 + NS, 2 * s, :], ACT.Identity), mod_rows, hold=False)

            def rms(stage, n=1):
                t = Turn(stage)
                for j in range(n):
                    act.wait_ge(psum_full, t.count())
                    if j >= 2:
                        act.wait_ge(psum_free, SLOTS + t.n - 1)
                    r = two(RS[:, (RMS[stage] + j) % 2, :])
                    a(f(r, halves(t.slot()), ACT.Ln, bias=EPST[:, 0:1]))
                    a(f(r, r, ACT.Exp, scale=-0.5), rms_ready)
                    t.n += 1

            rms("norm0")
            act.wait_ge(psum_free, SLOTS + FIRST["gup"] + 4)
            a(f(E, B, ACT.Abs))
            a(f(E, E, ACT.Exp, scale=-1.0))
            a(f(E, E, ACT.Ln, bias=CONST[:, ONE:ONE + 1]), softplus_ready)
            act.wait_ge(decay_ready, 1)
            a(f(B[:, :, NP:T], B[:, :, NP:T], ACT.Exp))
            a(f(FE, FE, ACT.Exp))
            a(f(B[:, :, 0:NP], E[:, :, 0:NP], ACT.Exp), exp_ready)
            a(f(E[:, :, 0:NP], E[:, :, 0:NP], ACT.Exp, scale=-1.0), exp_ready)
            rms("onorm", 4)
            t = Turn("r")
            for n in range(8):
                act.wait_ge(psum_full, t.count())
                a(f(two(QB[:, n, :]), halves(t.slot()), ACT.Silu), silu_ready)
                t.n += 1

            def experts(l):
                rms(f"fnorm{l}")
                for q in range(5):
                    m, b = rows_of(q), q % 2
                    act.wait_ge(tok_full, 5 * l + q + 1)
                    if q >= 2:
                        act.wait_ge(tok_stored[b], (96, 64)[b] * l + 32 * (q // 2))
                    bank = 2 * ((FIRST[f"route{l}"] + 1 + b) % SLOTS)
                    a(f(TOKB[b][0:m, :].rearrange("p (a n) -> p a n", a=2), PS[0:m, bank:bank + 2, :], ACT.Identity),
                      tok_copied)
                    for k in range(2):
                        act.dma_start(io["rows"][k * T + q * P:k * T + q * P + m, :], TOKB[b][0:m, :])\
                            .then_inc(tok_stored[b], 16)
                    if q == 1:
                        act.wait_ge(route_exp_in, 2 * l + 1)
                        a(f(GX, GX, ACT.Exp), route_exp)
                        act.wait_ge(route_exp_in, 2 * l + 2)
                        a(f(X2, X2, ACT.Exp), route_exp)
                a.settle()
                cpy = lambda dst, src: f(dst, src, ACT.Identity)
                base = NE * l

                def hidden(i, e):
                    act.wait_ge(ht_full, i * 2 + (base + e + 1))
                    a(cpy(HT_[e], PS[:, 4, 0:256]), ht_ready, hold=False)

                def gate(i, e):
                    act.wait_ge(gu_full, i * 2 + (base + e + 1))
                    a(f(SG[e], PS[:, 2 + e, 0:FF], ACT.Silu), act_gated, hold=False)

                def output(i, e, first=False):
                    act.wait_ge(down_full, i * 2 + (base + e + 1))
                    if not first:
                        act.wait_ge(y_out[e], i * 16 + (128 * l))
                    a(cpy(YB[e][:, 512:1024], PS[:, 6, :]), y_act, hold=False)

                def step(i, e, first=False):
                    prev = (i, 0) if e else (i - 1, 1)
                    hidden(*prev)
                    gate(i, e)
                    output(*prev, first=first)

                gate(0, 0)
                step(0, 1, True)
                step(1, 0, True)
                step(1, 1)
                with a.loop(NE // 2 - 2, [(ht_ready, 2), (act_gated, 2), (y_act, 2)]) as j:
                    i = j + 2
                    step(i, 0)
                    step(i, 1)
                hidden(NE // 2 - 1, 1)
                output(NE // 2 - 1, 1)
                o = ov[l]
                most = act.value_load(FLAG[0:1, l:l + 1], min_val=0, max_val=T)
                with act.If(most > CAP):
                    with act.Fori(0, NE) as e:
                        for c in range(NCH - 1):
                            act.wait_ge(o["gu_full"], e * (NCH - 1) + (c + 1))
                            f(SG[0], PS[:, 2, 0:FF], ACT.Silu).then_inc(o["silu"], 1)
                            act.wait_ge(o["out"], e * (16 * (NCH - 1)) + 16 * (c + 1))
                for b in range(2):
                    act.wait_ge(y_out[b], 8 * NE * (l + 1))
                act.wait_ge(down_full, NE * (l + 1))

                def fetch_pair(q):
                    m = rows_of(q)
                    for k in range(2):
                        act.dma_start(PAIR[q % 2][k][0:m, :], io["outs"][k * T + q * P:k * T + q * P + m, :])\
                            .then_inc(pair_in[q % 2], 16)

                fetch_pair(0)
                fetch_pair(1)
                for q in range(5):
                    m, b = rows_of(q), q % 2
                    act.wait_ge(pair_in[b], (96, 64)[b] * l + 32 * (q // 2 + 1))
                    a(f(PAIR[b][0][0:m, :], PAIR[b][0][0:m, :], ACT.Identity, scale=W1[0:m, q:q + 1]), weighted,
                      hold=False)
                    if 1 <= q <= 3:
                        act.wait_ge(mixed_full, 5 * l + q)
                        fetch_pair(q + 1)
                a.settle()

            experts(0)
            for stage, n in (("kvnorm", 1), ("ckvnorm", 1), ("norm2", 1), ("cqnorm", 1), ("qss", 6), ("kss", 6)):
                rms(stage, n)
            def probs(n):
                nk = (n // MH + 1) * P
                act.wait_ge(negmax_ready, n + 1)
                if n >= 2:
                    act.wait_ge(pt_full, n - 1)
                a(f(EF[:, 512 * (n % 2):512 * (n % 2) + nk], PS[:, n % 2, 0:nk], ACT.Exp, bias=NM[:, n % 2:n % 2 + 1],
                    scale=SCALE, accum_out=LN[:, n % 2:n % 2 + 1]), exp_done, hold=False)

            def page_squares(g):
                act.wait_ge(kn_full, g + 1)
                act.wait_ge(page_used, g + 5)
                a(f(RS[:, 0, 0:ROPE], PG[:, g % PSL, KVR:PROW], ACT.Square, accum_out=KRS[:, g:g + 1]))
                a(f(SQP[:, g % 4, :], PS[:, 6 + g % 2, :], ACT.Square), page_sq, hold=False)

            probs(0)
            for n in range(QT * MH):
                if n + 1 < QT * MH:
                    probs(n + 1)
                for g in range(4 * n, 4 * n + 4):
                    page_squares(g)
            a.settle()
            act.wait_ge(ssq_ready, 1)
            a(f(SSQ, SSQ, ACT.Ln, bias=EPST[:, 0:1], scale=1.0 / QK))
            a(f(SSQ, SSQ, ACT.Exp, scale=-0.5), krstd_ready)
            act.wait_ge(shifted, 1)
            a(f(NEW, NEW, ACT.Exp))
            a(f(SC, SC, ACT.Exp), p_exp)
            experts(1)

        @block.vector
        def _(dve):
            v = Order(dve, vec_order)
            nv = nc.vector
            tt, ts, stt, cp, red = (nv.tensor_tensor, nv.tensor_scalar, nv.scalar_tensor_tensor, nv.tensor_copy,
                                    nv.tensor_reduce)

            def full(t):
                dve.wait_ge(psum_full, t.count())
                s = t.slot()
                t.n += 1
                return s

            def rows(ap, n):
                return ap.unsqueeze(1).to_broadcast([P, n, T])

            v(nv.memset(MROW, 0.0))
            v(nv.memset(EPST[:, :], EPS), psum_free)
            v(nv.memset(AT[:, 672:688], 0.0), psum_free)
            v(nv.memset(TS[:, 0:NS], 0.0), psum_free)
            v(nv.memset(TS[:, NS:2 * NS], 0.0), psum_free)
            dve.wait_ge(consts_in, 32)
            with v.loop(6, [(psum_free, SLOTS), (mod_turned, 4 * SLOTS)]) as i:
                for s in range(SLOTS):
                    dve.wait_ge(mod_rows, i * SLOTS + (s + 1))
                    src = MROW[:, s, :].bitcast(U32).rearrange("p (n w r) -> p w n r", w=4, r=32)
                    for w in range(4):
                        v(nv.transpose(MTURN[32 * w:32 * w + 32, s].bitcast(U32), src[:, w]), mod_turned, hold=w == 3)
                    v(tt(MOD[:, bass.ds(i * 16 + 4 * s, 4), :], MTURN[:, s, :, 0:1 + NS],
                         VEC[:, bass.ds(i * 16 + (ADAB + 4 * s), 4)].unsqueeze(2).to_broadcast([P, 4, 1 + NS]),
                         ALU.add), psum_free)

            rms_used = [0]

            def normed():
                rms_used[0] += 1
                dve.wait_ge(rms_ready, rms_used[0])
                return RS[:, (rms_used[0] - 1) % 2, :]

            def squares(dst, src):
                v(tt(dst, src, src, ALU.mult), sq_ready)

            def stream_squares():
                for k in range(KD):
                    v(tt(H[:, k, :], X[:, k, :], X[:, k, :], ALU.mult), sq_ready, hold=False)

            def norm_modulate(stage, mod, gain):
                stream_squares()
                v(stt(AM[:, :, :], MOD[:, mod + 8:mod + 16, :], 1.0,
                      VEC[:, gain:gain + KD].unsqueeze(2).to_broadcast([P, KD, 1 + NS]), ALU.add, ALU.mult))
                r = normed()
                full(Turn(stage))
                hs = H[:, :, NP:T]
                v(tt(hs, X[:, :, NP:T], r[:, NP:T].unsqueeze(1).to_broadcast([P, KD, NS]), ALU.mult), psum_free)
                v(tt(hs, hs, AM[:, :, 1:], ALU.mult))
                v(tt(hs, hs, MOD[:, mod:mod + KD, 1:], ALU.add))

                def scaled(k):
                    v(stt(H[:, k, 0:NP], X[:, k, 0:NP], AM[:, k, 0:1], r[:, 0:NP], ALU.mult, ALU.mult), hold=False)

                scaled(0)
                for k in range(KD):
                    if k + 1 < KD:
                        scaled(k + 1)
                    dve.wait_ge(vec_order, v.value(vec_order) - (1 if k + 1 < KD else 0))
                    v(ts(H[:, k, 0:NP], H[:, k, 0:NP], MOD[:, mod + k, 0:1], None, ALU.add), h_ready, hold=False)
                v.settle()

            def residual(stage, mod):
                t = Turn(stage)
                for n in range(KD):
                    s = full(t)
                    g = MOD[:, mod + n, 0:1]
                    v(stt(X[:, n, 0:HT], PS[:, 2 * s, 0:HT], g, X[:, n, 0:HT], ALU.mult, ALU.add), hold=False)
                    v(stt(X[:, n, HT:NP], PS[:, 2 * s + 1, 0:NP - HT], g, X[:, n, HT:NP], ALU.mult, ALU.add),
                      hold=False)
                    v(tt(TS[:, 0:NS], PS[:, 2 * s + 1, NP - HT:HT], MOD[:, mod + n, 1:], ALU.mult))
                    v(tt(X[:, n, NP:T], X[:, n, NP:T], TS[:, 0:NS], ALU.add), psum_free)

            dve.wait_ge(x_in, 64)
            norm_modulate("norm0", 0, MIXN)
            t = Turn("qk")
            for n in range(8):
                s = full(t)
                v(ts(two(QB[:, n, :]), halves(s), float(DK) ** -0.5 if n < 4 else 1.0, None, ALU.mult), psum_free)
            s = full(Turn("glow"))
            v(cp(two(EF[0:GR, 0:T]), halves(s, GR)), psum_free)
            v(cp(TS[:, 0:1], EPST[:, :]), glow_ready)
            t = Turn("gup")
            for n in range(4):
                s = full(t)
                v(ts(two(B[:, n, :]), halves(s), VEC[:, GBIAS + n:GBIAS + n + 1], None, ALU.add), psum_free)
            t = Turn("v")
            for q in range(5):
                s = full(t)
                src = PS[:, 2 * s:2 * s + 2, :] if q < QT else PS[0:NS, 2 * s:2 * s + 2, :]
                dst = V[:, q, :] if q < QT else VS[:, :]
                v(cp(dst.rearrange("p (a b) -> p a b", a=2), src), psum_free)
            dve.wait_ge(softplus_ready, 1)
            v(stt(B, B, 0.0, E, ALU.min, ALU.subtract))
            v(ts(B, B, 1.0 / 16.0, None, ALU.mult))
            for h in range(GH):
                v(nv.tensor_tensor_scan(E[:, h, 0:NP], const(SCAN, NP), B[:, h, 0:NP], 0.0, ALU.mult, ALU.add),
                  hold=False)
            v.settle()
            EC = E[:, :, 0:NP].rearrange("p h (c t) -> p h c t", c=NC)
            v(cp(BM, EC[:, :, :, C // 2 - 1]), hold=False)
            v(cp(BL, EC[:, :, :, C - 1]))
            v(tt(FE, BL, BM, ALU.subtract))
            v(tt(FE[:, :, 0:NC - 1], FE[:, :, 0:NC - 1], BM[:, :, 1:NC], ALU.add))
            v(tt(EC, EC, BM.unsqueeze(3).to_broadcast([P, GH, NC, C]), ALU.subtract), decay_ready)
            dve.wait_ge(exp_ready, 1)
            v(tt(QB[:, 0:4, 0:NP], QB[:, 0:4, 0:NP], B[:, :, 0:NP], ALU.mult), decayed)
            dve.wait_ge(exp_ready, 2)
            v(tt(QB[:, 4:8, 0:NP], QB[:, 4:8, 0:NP], E[:, :, 0:NP], ALU.mult), decayed)
            for q in range(QT):
                dve.wait_ge(prep_full, q + 1)
                v(cp(EF[:, q * 512:(q + 1) * 512], PS[:, q % 2, :]), prep_done, hold=False)
                v(tt(AT[:, q * 256:(q + 1) * 256].rearrange("p (h t) -> p h t", h=GH),
                     PS[:, 2 + q % 2, 0:256].rearrange("p (h t) -> p h t", h=GH),
                     const(TRI, C).unsqueeze(1).to_broadcast([P, GH, C]), ALU.mult), prep_done)
            S4 = S.rearrange("p (h n) -> p h n", h=GH)
            for c in range(NC):
                dve.wait_ge(o_full, c + 1)
                v(cp(O[:, :, c * C:(c + 1) * C], PS[:, 4 + c % 2, :].rearrange("p (n t) -> p n t", n=8)), o_taken)
                kv = PS[:, 2 * (c % 2):2 * (c % 2) + 2, :].rearrange("p a (h n) -> p (a h) n", h=2)
                fe = FE[:, :, c:c + 1].to_broadcast([P, GH, DV])
                if c == 0:
                    v(tt(S4, kv, fe, ALU.mult), state_ready)
                else:
                    v(tt(S4, kv, S4, ALU.add))
                    v(tt(S4, S4, fe, ALU.mult), state_ready)
            dve.wait_ge(ks_full, 1)
            v(cp(EF[0:NS, 0:512], PS[0:NS, 6, :]))

            def key_row(b):
                if b >= 2:
                    dve.wait_ge(outer_full, b - 1)
                v(ts(EF[0:NS, 512 * (1 + b % 2):512 * (2 + b % 2)], EF[0:NS, 0:512], CONST[0:NS, ID + b:ID + b + 1],
                     None, ALU.mult), km_ready)

            key_row(0)
            for b in range(NS):
                if b + 1 < NS:
                    key_row(b + 1)
                dve.wait_ge(outer_full, b + 1)
                dve.wait_ge(st_in[b % 2], 16 * (b // 2 + 1))
                for h in range(GH):
                    st = ST[:, b % 2, h * DV:(h + 1) * DV]
                    v(stt(st, st, B[:, h, NP + b:NP + b + 1],
                          PS[:, 2 * (b % 2) + h // 2, (h % 2) * DV:(h % 2 + 1) * DV], ALU.mult, ALU.add),
                      snew_ready, hold=False)
                v.settle()
            dve.wait_ge(os_full, NS)
            v(cp(O[:, :, NP:T], PS[:, 7, 0:64].rearrange("p (b n) -> p n b", b=NS)))
            squares(BE[:, :, :], O[:, :, :])
            t = Turn("onorm")
            for h in range(GH):
                r = normed()
                full(t)
                v(tt(O[:, 2 * h:2 * h + 2, :], O[:, 2 * h:2 * h + 2, :], rows(r, 2), ALU.mult), psum_free)
            t = Turn("r")
            for n in range(8):
                full(t)
                dve.wait_ge(silu_ready, n + 1)
                v(stt(O[:, n, :], O[:, n, :], VEC[:, ONORM + n % 2:ONORM + n % 2 + 1], QB[:, n, :], ALU.mult,
                      ALU.mult), psum_free)
            residual("gout", 16)

            def first_max(dst, src, top, tmp, top2):
                b = [P, 5, 4]
                v(red(top, src, AX.X, ALU.max))
                v(tt(tmp, src, top.unsqueeze(2).to_broadcast(b), ALU.is_ge))
                v(tt(tmp, tmp, CONST[:, RANK:RANK + 4].unsqueeze(1).to_broadcast(b), ALU.mult))
                v(red(top2, tmp, AX.X, ALU.max))
                v(tt(dst, tmp, top2.unsqueeze(2).to_broadcast(b), ALU.is_equal))

            def experts(l):
                norm_modulate(f"fnorm{l}", l * 48 + 24, FFNN + 8 * l)
                v(nv.memset(LOG, 0.0))
                s = full(Turn(f"route{l}"))
                bias = BRT[:, l, :]
                v(tt(LOG[:, 0:QT, :], PS[:, 2 * s, 0:80].rearrange("p (q n) -> p q n", q=QT),
                     bias.unsqueeze(1).to_broadcast([P, QT, 20]), ALU.add))
                v(tt(LOG[0:NS, QT, :], PS[0:NS, 2 * s, 80:100], bias[0:NS, :], ALU.add), psum_free)
                b = [P, 5, 4]
                first_max(OHG, LOG[:, :, 0:4], M1, TMP, M2)
                v(tt(GX, LOG[:, :, 0:4], M1.unsqueeze(2).to_broadcast(b), ALU.subtract), route_exp_in)
                le = LOG[:, :, 4:20].rearrange("p q (g e) -> p q g e", g=NG)
                v(tt(SEL, le, OHG.unsqueeze(3).to_broadcast([P, 5, 4, 4]), ALU.mult))
                v(red(LE, SEL.rearrange("p q g e -> p q e g"), AX.X, ALU.add))
                first_max(OH1, LE, M1, TMP, M2)
                v(stt(LE, OH1, -BIG, LE, ALU.mult, ALU.add))
                first_max(OH2, LE, M3, TMP, M2)
                v(tt(X2, M3, M1, ALU.subtract), route_exp_in)
                dve.wait_ge(route_exp, 2 * l + 2)
                b16 = [P, 5, NG, NEG]

                def outer(dst, e):
                    v(tt(dst.rearrange("p q (g e) -> p q g e", g=NG), e.unsqueeze(2).to_broadcast(b16),
                         OHG.unsqueeze(3).to_broadcast(b16), ALU.mult))

                outer(AK[0], OH1)
                outer(AK[1], OH2)
                v(tt(AS, AK[0], AK[1], ALU.add), chosen)
                v(red(M1, GX, AX.X, ALU.add))
                v(stt(M2, X2, 1.0, M1, ALU.add, ALU.mult))
                v(nv.reciprocal(W1, M2))
                v(tt(W2, W1, X2, ALU.mult))
                for k in range(2):
                    v(ts(M1, CONST[:, TOK:TOK + 5], float(T * k), None, ALU.add))
                    v(tt(RK[k][:, :, 0, :], AK[k], M1.unsqueeze(2).to_broadcast([P, 5, NE]), ALU.mult))
                    v(cp(RK[k][:, :, 1, :], AK[k]))
                v(nv.memset(POS, 0.0))
                dve.wait_ge(pos_full, l + 1)
                v(cp(POS[:, 0:QT, :], PS[:, 0, 0:QT * NE].rearrange("p (q e) -> p q e", q=QT)), hold=False)
                v(cp(POS[0:NS, QT, :], PS[0:NS, 0, QT * NE:5 * NE]))
                v(red(M1[0:1, 0:1], PS[0:1, 1, 0:NE], AX.X, ALU.max))
                v(cp(FLAG[:, l:l + 1], M1[0:1, 0:1]), flag_ready)
                for k in range(2):
                    v(tt(ATMP, AK[k], POS, ALU.mult))
                    v(red(PK[k], ATMP, AX.X, ALU.add))

                def one_hot_places(c, done):
                    for k in range(2):
                        v(ts(PC[k], PK[k], float(-CAP * c), None, ALU.add))
                        if CAP < P:
                            v(ts(M1, PC[k], float(CAP), 1024.0, ALU.is_ge, ALU.mult))
                            v(tt(PC[k], PC[k], M1, ALU.add))
                        for q in range(5):
                            v(ts(OPK[:, k, q, :], const(IOTA), PC[k][:, q:q + 1], None, ALU.is_equal), hold=False)
                        v.settle()
                    v(cp(TS[:, 0:1], EPST[:, :]), done)

                def index_rows(c, bank, done):
                    v(ts(ATMP[:, 0, :], PS[:, bank, NE:2 * NE], -NOROW, NOROW, ALU.mult, ALU.add))
                    v(tt(IDX[:, c, :], ATMP[:, 0, :], PS[:, bank, 0:NE], ALU.add), done)

                one_hot_places(0, rows_ready)
                dve.wait_ge(idx_full, l + 1)
                index_rows(0, 2, idx_ready)

                base = NE * l

                def turned_rows(i, e):
                    dve.wait_ge(xt_full, i * 2 + (base + e + 1))
                    v(cp(XT[e].rearrange("p (a k) n -> p a (k n)", a=2), PS[:, 0:2, :]), xt_ready, hold=False)

                def hidden(i, e):
                    dve.wait_ge(act_gated, i * 2 + (base + e + 1))
                    v(tt(HID[e], SG[e], PS[:, 2 + e, FF:2 * FF], ALU.mult), hid_ready, hold=False)

                def output(i, e, first=False):
                    dve.wait_ge(down_full, i * 2 + (base + e + 1))
                    if not first:
                        dve.wait_ge(y_out[e], i * 16 + (128 * l))
                    v(cp(YB[e][:, 0:512], PS[:, 5, :]), y_dve, hold=False)

                def step(i, e, first=False):
                    turned_rows(i, e)
                    hidden(i, e)
                    output(*((i, 0) if e else (i - 1, 1)), first=first)

                turned_rows(0, 0)
                hidden(0, 0)
                step(0, 1, True)
                step(1, 0, True)
                step(1, 1)
                with v.loop(NE // 2 - 2, [(xt_ready, 2), (hid_ready, 2), (y_dve, 2)]) as j:
                    i = j + 2
                    step(i, 0)
                    step(i, 1)
                output(NE // 2 - 1, 1)
                v.settle()

                o = ov[l]
                most = dve.value_load(FLAG[0:1, l:l + 1], min_val=0, max_val=T)
                with dve.If(most > CAP):
                    w = Order(dve, o["table"])
                    for c in range(NCH - 1):
                        for k in range(2):
                            w(ts(PC[k], PK[k], float(-CAP * (c + 1)), None, ALU.add), more_step[l])
                            if CAP < P:
                                w(ts(M1, PC[k], float(CAP), 1024.0, ALU.is_ge, ALU.mult), more_step[l])
                                w(tt(PC[k], PC[k], M1, ALU.add), more_step[l])
                            for q in range(5):
                                w(ts(OPK[:, k, q, :], const(IOTA), PC[k][:, q:q + 1], None, ALU.is_equal),
                                  more_step[l])
                        w(cp(TS[:, 0:1], EPST[:, :]), o["table"])
                        dve.wait_ge(o["table_full"], c + 1)
                        w(ts(ATMP[:, 0, :], PS[:, 7, NE:2 * NE], -NOROW, NOROW, ALU.mult, ALU.add), more_step[l])
                        w(tt(IDX[:, c + 1, :], ATMP[:, 0, :], PS[:, 7, 0:NE], ALU.add), more_step[l])
                    for b in range(2):
                        dve.wait_ge(y_out[b], 8 * NE * (l + 1))
                    dve.wait_ge(y_act, NE * (l + 1))
                    with dve.Fori(0, NE) as e:
                        for c in range(NCH - 1):
                            n = e * (NCH - 1) + (c + 1)
                            cp(IDXO[:, :], IDX[:, c + 1, bass.ds(e, 1)]).then_inc(o["go"], 1)
                            dve.wait_ge(o["xt_full"], n)
                            cp(XT[0].rearrange("p (a k) n -> p a (k n)", a=2), PS[:, 0:2, :]).then_inc(o["xt"], 1)
                            dve.wait_ge(o["silu"], n)
                            tt(HID[0], SG[0], PS[:, 2, FF:2 * FF], ALU.mult).then_inc(o["hid"], 1)
                            dve.wait_ge(o["ht_full"], n)
                            cp(HT_[0], PS[:, 4, 0:256]).then_inc(o["ht"], 1)
                            dve.wait_ge(o["down_full"], n)
                            cp(YB[0].rearrange("p (a n) -> p a n", a=2), PS[:, 5:7, :]).then_inc(o["y"], 1)
                            dve.wait_ge(o["out"], e * (16 * (NCH - 1)) + 16 * (c + 1))

                mod = l * 48 + 40
                TMPX = OF[:, 2048:3072].rearrange("p (k n) -> p k n", k=KD)

                def mix(q):
                    m, y = rows_of(q), PAIR[q % 2]
                    dve.wait_ge(weighted, 5 * l + q + 1)
                    v(stt(y[0][0:m, :], y[1][0:m, :], W2[0:m, q:q + 1], y[0][0:m, :], ALU.mult, ALU.add), mixed,
                      hold=False)

                mix(0)
                for q in range(5):
                    m, b = rows_of(q), q % 2
                    if q + 1 < 5:
                        mix(q + 1)
                    dve.wait_ge(mixed_full, 5 * l + q + 1)
                    src = PS[:, 2 * b:2 * b + 2, :].rearrange("p a (k n) -> p (a k) n", k=4)[:, :, 0:m]
                    if q < QT:
                        g = MOD[:, mod:mod + KD, 0:1].to_broadcast([P, KD, m])
                    else:
                        g = MOD[:, mod:mod + KD, 1:]
                    v(tt(TMPX[:, :, 0:m], src, g, ALU.mult), pair_added)
                    x = X[:, :, q * P:q * P + m]
                    v(tt(x, x, TMPX[:, :, 0:m], ALU.add), y_ready if l and q == QT else None)

            experts(0)

            stream_squares()
            r = normed()
            full(Turn("kvnorm"))
            for k in range(KD):
                v(stt(H[:, k, :], X[:, k, :], VEC[:, KVIN + k:KVIN + k + 1], r, ALU.mult, ALU.mult), h_ready, hold=False)
            v(cp(TS[:, 0:1], EPST[:, :]), psum_free)
            t = Turn("dkv")
            for n in range(3):
                s = full(t)
                v(cp(two(CKV[:, n, :]), halves(s)), psum_free)
            squares(E[:, 0:2, :], CKV[:, 0:2, :])
            r = normed()
            full(Turn("ckvnorm"))
            v(tt(CKV[:, 0:2, :], CKV[:, 0:2, :], rows(r, 2), ALU.mult), psum_free)
            v(ts(CKV[:, 0, :], CKV[:, 0, :], VEC[:, KVLAT:KVLAT + 1], None, ALU.mult))
            v(ts(CKV[:, 1, :], CKV[:, 1, :], VEC[:, KVLAT + 1:KVLAT + 2], None, ALU.mult), lat_ready)
            s = full(Turn("krot"))
            v(tt(two(E[:, 3, :]), halves(s), two(const2(SIN, T)), ALU.mult), psum_free)
            v(tt(CKV[:, 2, :], CKV[:, 2, :], const2(COS, T), ALU.mult))
            v(tt(CKV[:, 2, :], CKV[:, 2, :], E[:, 3, :], ALU.add), kr_ready)

            norm_modulate("norm2", 48, MIXN + 8)
            t = Turn("dq")
            for n in range(3):
                s = full(t)
                v(cp(two(B[:, n, :]), halves(s)), psum_free)
            squares(E[:, 0:3, :], B[:, 0:3, :])
            r = normed()
            full(Turn("cqnorm"))
            v(tt(B[:, 0:3, :], B[:, 0:3, :], rows(r, 3), ALU.mult), psum_free)
            for k in range(2):
                v(ts(B[:, k, :], B[:, k, :], VEC[:, QLAT + k:QLAT + k + 1], None, ALU.mult))
            v(ts(B[:, 2, :], B[:, 2, :], VEC[:, QLAT + 2:QLAT + 3], None, ALU.mult), lat_ready)
            t = Turn("uq")
            for n in range(6):
                s = full(t)
                v(cp(two(QB[:, n, :]), halves(s)), psum_free)
            t = Turn("qrot")
            for j in range(2):
                s = full(t)
                v(tt(two(E[:, j, :]), halves(s), two(const2(SIN, T)), ALU.mult), psum_free)
            v(tt(QB[:, 4:6, :], QB[:, 4:6, :], rows(const2(COS, T), 2), ALU.mult))
            v(tt(QB[:, 4:6, :], QB[:, 4:6, :], E[:, 0:2, :], ALU.add))
            squares(H[:, 0:6, :], QB[:, 0:6, :])
            t = Turn("qss")
            for n in range(6):
                r = normed()
                full(t)
                g = QNN if n < 4 else QNR
                v(stt(QB[:, n, :], QB[:, n, :], VEC[:, g:g + 1], r, ALU.mult, ALU.mult), psum_free)
            t = Turn("uk")
            for n in range(4):
                s = full(t)
                v(cp(two(O[:, n, :]), halves(s)), psum_free)
            v(tt(H[:, 0:4, :], O[:, 0:4, :], O[:, 0:4, :], ALU.mult))
            squares(H[:, 4, :], CKV[:, 2, :])
            t = Turn("kss")
            for n in range(6):
                r = normed()
                full(t)
                g, src = (KNN, O[:, n, :]) if n < 4 else (KNR, CKV[:, 2, :])
                v(stt(O[:, n, :], src, VEC[:, g:g + 1], r, ALU.mult, ALU.mult), psum_free)
            t = Turn("uv")
            for q in range(QT):
                s = full(t)
                v(cp(VP[:, q, :], PS[:, 2 * s, :]), psum_free)

            v(ts(QP[:, 0:4, :], QB[:, 0:4, NP:T], VEC[:, KNN:KNN + 1], None, ALU.mult), hold=False)
            v(ts(QP[:, 4:6, :], QB[:, 4:6, NP:T], VEC[:, KNR:KNR + 1], None, ALU.mult), qp_ready)
            v(stt(PR, QB[:, 0:6, NP:T], SCALE * QK, O[:, 0:6, NP:T], ALU.mult, ALU.mult), qp_ready)
            v(nv.memset(NEW, -BIG))
            dve.wait_ge(ql_full, 1)
            for r in range(2):
                for u in range(2):
                    v(ts(QL[:, r, :, u:MH:2], PS[:, 3 * u, r * 32:(r + 1) * 32].rearrange("p (h s) -> p s h", h=4),
                         SCALE, None, ALU.mult), ql_ready)
            v(ts(QRS, PS[0:ROPE, 1, 0:64].rearrange("p (h s) -> p s h", h=MH), SCALE, None, ALU.mult), ql_ready)
            v(cp(NEW[0:1, :].rearrange("p (s h) -> p s h", s=NS), PS[0:1, 2, 0:64].rearrange("p (h s) -> p s h", h=MH)),
              ql_ready)
            for n in range(PSL):
                v(cp(TS[:, n:n + 1], EPST[:, :]), page_used)

            def mask_max(n):
                q, b = n // MH, n % 2
                dve.wait_ge(sc_full, n + 1)
                diag = PS[:, b, q * P:(q + 1) * P]
                v(tt(diag, diag, const2(CAUS), ALU.add))
                v(red(NM[:, b:b + 1], PS[:, b, 0:(q + 1) * P], AX.X, ALU.max))
                v(ts(NM[:, b:b + 1], NM[:, b:b + 1], -SCALE, None, ALU.mult), negmax_ready)

            def page_sums(g):
                dve.wait_ge(page_sq, g + 1)
                v(red(SSQ[:, g * MH:(g + 1) * MH], SQP[:, g % 4, :].rearrange("p (h d) -> p h d", h=MH),
                      AX.X, ALU.add), page_used, hold=False)
                if g % PSL == PSL - 1:
                    m = g // PSL
                    dve.wait_ge(kn_full, g + 1)
                    v(cp(SC[:, m * 64:(m + 1) * 64], PS[:, 3 + 2 * (m % 2), 0:PSL * MH]), scores_taken,
                      hold=False)

            mask_max(0)
            for n in range(QT * MH):
                q, h, b = n // MH, n % MH, n % 2
                nk = (q + 1) * P
                if n + 1 < QT * MH:
                    if n >= 1:
                        dve.wait_ge(exp_done, n)
                    mask_max(n + 1)
                dve.wait_ge(exp_done, n + 1)
                v(nv.reciprocal(LN[:, b:b + 1], LN[:, b:b + 1]))
                pb = EF[:, 512 * b:512 * b + nk]
                v(ts(pb, pb, LN[:, b:b + 1], None, ALU.mult), p_ready)
                page_sums(4 * n)
                dve.wait_ge(pt_full, n + 1)
                if n >= 2:
                    dve.wait_ge(pv_full, n - 1)
                v(cp(EF[:, 1024 + 512 * b:1024 + 512 * b + nk], PS[:, 2, 0:nk]), pt_ready)
                page_sums(4 * n + 1)
                page_sums(4 * n + 2)
                dve.wait_ge(pv_full, n + 1)
                lo = MV * (h % 2)
                v(cp(B[lo:lo + MV, h // 2, q * P:(q + 1) * P], PS[lo:lo + MV, 4, 0:P]), pv_done)
                page_sums(4 * n + 3)
            v.settle()
            v(tt(SSQ.rearrange("p (n h) -> p n h", h=MH), SSQ.rearrange("p (n h) -> p n h", h=MH),
                 KRS.unsqueeze(2).to_broadcast([P, NS * NPG, MH]), ALU.add), ssq_ready)
            dve.wait_ge(krstd_ready, 1)
            v(tt(SC, SC, SSQ, ALU.mult))
            SC4 = SC.rearrange("p (s g h) -> p s g h", s=NS, g=NPG)
            v(red(MX.rearrange("p (s h) -> p s h", s=NS), SC4.rearrange("p s g h -> p s h g"), AX.X, ALU.max))
            v(tt(MX, MX, NEW, ALU.max), max_ready)
            dve.wait_ge(max_full, 1)
            v(red(MC, PS[0:64, 6, 0:P], AX.X, ALU.max))
            v(ts(DG, ident(64, 64), MC, None, ALU.mult), max_ready)
            dve.wait_ge(max_full, 2)
            v(cp(MX, PS[:, 7, 0:64]))
            v(tt(NEW, NEW, MX, ALU.subtract))
            v(tt(SC4, SC4, MX.rearrange("p (s h) -> p s h", s=NS).unsqueeze(2).to_broadcast([P, NS, NPG, MH]),
                 ALU.subtract), shifted)
            dve.wait_ge(p_exp, 1)
            v(red(LS.rearrange("p (s h) -> p s h", s=NS), SC4.rearrange("p s g h -> p s h g"), AX.X, ALU.add))
            v(tt(LS, LS, NEW, ALU.add), sum_ready)
            dve.wait_ge(sum_full, 1)
            v(nv.reciprocal(RLS, PS[:, 6, 0:64]))
            v(cp(PNB, PS[:, 6, 64:128]))
            for i in range(0, NS, 2):
                dve.wait_ge(cpage_used, NPG * (i + 2))
                v(cp(ACC[:, i:i + 2, :, :].rearrange("p s r n -> p (s r n)"), PS[0:MH, i // 2, :]), acc_taken)
            dve.wait_ge(acc_full, 1)
            P3 = PNB.rearrange("p (s h) -> p s h", s=NS)
            M3X = MX.rearrange("p (s h) -> p s h", s=NS)
            for r in range(2):
                v(tt(M3X, P3, CKV[:, r, NP:T].unsqueeze(2).to_broadcast([P, NS, MH]), ALU.mult))
                v(tt(OL[:, r, :, :], PS[:, 5, r * 64:(r + 1) * 64].rearrange("p (s h) -> p s h", s=NS), M3X, ALU.add))
                v(tt(OL[:, r, :, :], OL[:, r, :, :], RLS.rearrange("p (s h) -> p s h", s=NS), ALU.mult),
                  olat_ready if r else None)
            dve.wait_ge(osam_full, 1)
            v(cp(B[:, :, NP:T], PS[:, 4, 0:32].rearrange("p (k s) -> p k s", k=4)), attn_ready)
            residual("mout", 64)
            experts(1)


def tiles(w, n):
    k, m = w.shape
    return w.reshape(k // P, P, m // n, n).transpose(2, 1, 0, 3).reshape(m // n, P, k // P * n)


def turned(x):
    return x.T.reshape(x.shape[1] // P, P, x.shape[0]).transpose(1, 0, 2)


def column(w):
    return w.reshape(-1, P).T


def kernel(**inputs):
    import concourse.bacc as bacc
    from concourse.bass_utils import run_bass_kernel_spmd

    w = {k: np.asarray(a) for k, a in inputs.items()}
    const, const2 = constant_tables()
    gw = w["gla_w_in"][0]
    uq = w["mla_w_uq"][0].reshape(QR, MH, QK)
    uq = np.concatenate([uq[:, :, :NOPE].reshape(QR, -1), uq[:, :, NOPE:].reshape(QR, -1)], axis=1)
    dkv = w["kv_w_dkv"]
    dkv = np.concatenate([dkv[:, :KVR]] + [dkv[:, KVR:]] * 4, axis=1)
    uk, uv = w["kv_w_uk"].reshape(KVR, -1), w["kv_w_uv"].reshape(KVR, -1)
    ukv = np.concatenate([tiles(uk, 512)[0], tiles(uv, 512)[0], tiles(np.ascontiguousarray(uk.T), 256)[0]], axis=1)
    vec = np.concatenate(
        [column(w["mix_norm"][l]) for l in range(2)] + [column(w["ffn_norm"][l]) for l in range(2)]
        + [column(w["ada_b"].reshape(-1)), column(w["gla_b_gate"][0]), column(w["gla_out_norm"][0]),
           column(w["kv_in_norm"]), column(w["mla_q_lat_norm"][0]), column(w["kv_lat_norm"])]
        + [np.tile(g[a:b], P // (b - a))[:, None] for g in (w["mla_q_norm"][0], w["kv_k_norm"])
           for a, b in ((0, NOPE), (NOPE, QK))], axis=1)
    cache, cache_kr = w["cache_ckv"], w["cache_krope"]
    npool = cache.shape[0]
    ct = cache.reshape(npool, PAGE, 2, P).transpose(0, 3, 2, 1).reshape(npool, P, KVR)
    arrays = {
        "x": turned(np.concatenate([w["x_prompt"][0], w["x_sample"][:, 0]], axis=0)),
        "c": turned(np.concatenate([w["c_prompt"], w["c_sample"]], axis=0)),
        "const": const, "const2": const2, "vec": vec,
        "ada": np.stack([tiles(w["ada_w"][l], 512) for l in range(2)]).reshape(6, SLOTS, P, 4096),
        "gla": np.concatenate([tiles(gw[:, a:b], 512) for a, b in
                               ((0, 512), (512, 1024), (1024, 2048), (2048, 3072))] + [tiles(w["gla_w_out"][0], 512)]),
        "gate_low": tiles(gw[:, 3072:], GR)[0].reshape(P, KD, GR),
        "gate_up": w["gla_w_gate_up"][0],
        "router": np.stack([tiles(np.concatenate([w["moe_w_group"][l], w["moe_w_router"][l]], axis=1), 20)[0]
                            .reshape(P, KD, 20) for l in range(2)], axis=1),
        "router_b": np.concatenate([w["moe_b_group"], w["moe_b_router"]], axis=1),
        "moe_gu": np.stack([np.stack([tiles(np.concatenate([w["moe_w_gate"][l, e], w["moe_w_up"][l, e]], axis=1),
                                            512)[0] for e in range(NE)]) for l in range(2)])
        .reshape(2, NE // 2, 2, P, 4096),
        "moe_dn": np.stack([np.stack([tiles(w["moe_w_down"][l, e], D)[0] for e in range(NE)]) for l in range(2)])
        .reshape(2, NE // 2, 2, P, 2048),
        "dkv": tiles(dkv, QR)[0], "dq": tiles(w["mla_w_dq"][0], QR)[0], "uq": tiles(uq, MH * QK)[0], "ukv": ukv,
        "mwo": tiles(w["mla_w_out"][0], D)[0],
        "state_in": w["state_gla"][0].transpose(0, 2, 1, 3).reshape(NS, P, GH * DV),
        "cache_t": np.concatenate([ct, cache_kr], axis=2),
        "cache_kr": cache_kr.transpose(0, 2, 1),
        "cache": cache,
        "pages": w["page_table"].reshape(1, -1),
    }
    outs = {"y": (P, KD, T), "state_p": (P, GH * DV), "state_s": (NS, P, GH * DV), "ckv": (P, 2, T), "kr": (ROPE, T)}
    nc = bacc.Bacc("TRN2", target_bir_lowering=False, num_devices=1)
    io, args = {}, {}
    for name, a in arrays.items():
        a = np.ascontiguousarray(a)
        args[f"in_{name}"] = a
        io[name] = nc.dram_tensor(f"in_{name}", a.shape, mybir.dt.from_np(a.dtype), kind="ExternalInput").ap()
    for name, shape in outs.items():
        io[name] = nc.dram_tensor(f"out_{name}", shape, F32, kind="ExternalOutput").ap()
    io["rows"] = nc.dram_tensor("rows", (2 * T, D), F32, kind="Internal").ap()
    io["outs"] = nc.dram_tensor("outs", (2 * T, D), F32, kind="Internal").ap()
    io["npool"] = npool
    trunk_program(nc, io)
    got = run_bass_kernel_spmd(nc, [args], core_ids=[0]).results[0]

    def back(a):
        return np.ascontiguousarray(a.transpose(2, 1, 0).reshape(T, -1))

    y, ckv, kr = back(got["out_y"]), back(got["out_ckv"]), np.ascontiguousarray(got["out_kr"].T)
    sp = got["out_state_p"].reshape(P, GH, DV).transpose(1, 0, 2)[None, None]
    ss = got["out_state_s"].reshape(NS, P, GH, DV).transpose(0, 2, 1, 3)[None]
    return (y[None, :NP], y[NP:, None], np.ascontiguousarray(sp), np.ascontiguousarray(ss),
            ckv[None, :NP], kr[None, :NP], ckv[NP:, None], kr[NP:, None])
```

```python
from contextlib import ExitStack, contextmanager

import numpy as np
import concourse.bass as bass
from concourse import mybir

F32 = mybir.dt.float32
I32 = mybir.dt.int32
U32 = mybir.dt.uint32
ALU = mybir.AluOpType
ACT = mybir.ActivationFunctionType
AX = mybir.AxisListType

P = 128
D = 1024
KD = D // P
NP, NS = 512, 8
T = NP + NS
HT = T // 2
QT = NP // P
EPS = 1e-6
GH, DK, DV, GR = 4, 128, 256, 16
C = 64
NC = NP // C
MH, NOPE, ROPE, MV = 8, 64, 32, 64
QK = NOPE + ROPE
QR, KVR = 384, 256
PAST, PAGE = 2048, 128
NPG = PAST // PAGE
PSL = 8
PROW = KVR + ROPE
NE, NG, NEG, FF = 16, 4, 4, 256
BIG = 1.0e30
CAP = 128
NCH = -(-T // CAP)
NOROW = float(1 << 20)
SLOTS = 4

ID, ONE, O1024, O256, O384, TRI, SCAN, RANK = 0, 128, 256, 384, 512, 640, 704, 1216
TRIS, IOTA, TOK = 1220, 1348, 1476
NCONST = 1481
B64, B32, E0, F0, K1, ROT, CAUS, COS, SIN = 0, 128, 256, 512, 768, 896, 1024, 1152, 1672
NCONST2 = 2192
MIXN, FFNN, ADAB, GBIAS, ONORM, KVIN, QLAT, KVLAT, QNN, QNR, KNN, KNR = 0, 16, 32, 128, 132, 134, 142, 145, 147, 148, 149, 150
NVEC = 151


def constant_tables():
    c = np.zeros((P, NCONST), np.float32)
    c[:, ID:ID + P] = np.eye(P)
    c[:, ONE:ONE + P] = 1.0
    c[:, O1024:O1024 + P] = 1.0 / D
    c[:, O256:O256 + P] = 1.0 / 256
    c[:, O384:O384 + P] = 1.0 / QR
    p = np.arange(P)
    c[:, TRI:TRI + C] = np.arange(C)[None, :] >= (p % C)[:, None]
    c[:, SCAN:SCAN + NP] = (np.arange(NP) % C != 0)[None, :]
    c[:, RANK:RANK + 4] = np.array([4.0, 3.0, 2.0, 1.0])
    c[:, TRIS:TRIS + P] = p[:, None] < p[None, :]
    c[:, IOTA:IOTA + P] = p[None, :]
    c[:, TOK:TOK + 5] = p[:, None] + P * np.arange(5)[None, :]
    m = np.zeros((P, NCONST2), np.float32)
    one = np.float32(1.0 / QK)
    half, quarter = p // NOPE, p // ROPE
    m[:, B64:B64 + P] = (half[:, None] == half[None, :]) * one
    m[:, B32:B32 + P] = (quarter[:, None] == quarter[None, :]) * one
    for u in range(2):
        m[:, E0 + u * P:E0 + (u + 1) * P] = (half[:, None] + 2 * u == quarter[None, :]) * one
        m[:, F0 + u * P:F0 + (u + 1) * P] = (quarter[:, None] == half[None, :] + 2 * u) * one
    m[:, K1:K1 + P] = (p < ROPE)[:, None] * one
    for i in range(P):
        j = i + ROPE // 2 if i % ROPE < ROPE // 2 else i - ROPE // 2
        m[j, ROT + i] = -1.0 if i % ROPE < ROPE // 2 else 1.0
    m[:, CAUS:CAUS + P] = np.where(p[None, :] <= p[:, None], 0.0, -BIG)
    inv = (np.float32(10000.0) ** (-np.arange(0, ROPE, 2, dtype=np.float32) / np.float32(ROPE))).astype(np.float32)
    pos = np.concatenate([np.arange(NP), np.full(NS, PAST)]).astype(np.float32)
    ang = (pos[:, None] * inv[None, :]).astype(np.float32)
    ang = np.tile(np.concatenate([ang, ang], axis=1), (1, P // ROPE)).T
    m[:, COS:COS + T] = np.cos(ang)
    m[:, SIN:SIN + T] = np.sin(ang)
    return c, m


KADA = 12

STAGES = [("ada", KADA), ("norm0", 1), ("qk", 8), ("glow", 1), ("gup", 4), ("v", 5), ("onorm", 4), ("r", 8), ("gout", 8)]
for _l in (0, 1):
    if _l:
        STAGES += [("kvnorm", 1), ("dkv", 3), ("dq", 3), ("ckvnorm", 1), ("krot", 1), ("cqnorm", 1),
                   ("uq", 6), ("qrot", 2), ("qss", 6), ("uk", 4), ("uv", 4), ("kss", 6), ("mout", 1)]
    STAGES += [(f"fnorm{_l}", 1), (f"route{_l}", 1)]
FIRST = {}
_n = 0
for _s, _k in STAGES:
    FIRST[_s] = _n
    _n += _k

RING = {f"ada{j}": (j % SLOTS, j // SLOTS + 1) for j in range(KADA)}
_use = [KADA // SLOTS] * SLOTS
for _name, _slot in (("wq", 0), ("wk", 1), ("wv0", 2), ("wv1", 3), ("adb0", 0), ("adb1", 1), ("adb2", 2), ("adb3", 3),
                     ("wr0", 0), ("wr1", 1), ("adb4", 2), ("adb5", 3), ("wo0", 2), ("wo1", 3),
                     ("adb6", 0), ("adb7", 1), ("adb8", 2), ("moe0", None), ("adb9", 0), ("adb10", 1), ("adb11", 2),
                     ("dkv", 3), ("dq", 0), ("uq", 2), ("ukv", 3), ("mwo", 0), ("moe1", None)):
    if _slot is None:
        for _s in range(SLOTS):
            RING[f"{_name}_{_s}"] = (_s, _use[_s] + 1)
            _use[_s] += NE // 2
        continue
    _use[_slot] += 1
    RING[_name] = (_slot, _use[_slot])
LAST_USE = {f"ada{j}": j + 1 for j in range(KADA - SLOTS, KADA)}
for _name, _stage, _k in (("wq", "qk", 4), ("wk", "qk", 8), ("wv0", "v", 5), ("wv1", "v", 5), ("wr0", "r", 4),
                          ("wr1", "r", 8), ("wo0", "gout", 4), ("wo1", "gout", 8), ("dkv", "dkv", 3), ("dq", "dq", 3),
                          ("uq", "uq", 6), ("mwo", "mout", 1)):
    LAST_USE[_name] = FIRST[_stage] + _k


class Turn:

    def __init__(self, stage):
        self.n, self.off = FIRST[stage], 0

    def count(self):
        return self.n + 1 + self.off

    def slot(self):
        return self.n % SLOTS


class Order:

    def __init__(self, eng, own):
        self.eng, self.own, self.c, self.open = eng, own, {}, []
        self.i, self.per = None, {}

    def value(self, sem):
        v = self.c[sem.name]
        return v if self.i is None else v + self.i * self.per.get(sem.name, 0)

    def __call__(self, ins, sem=None, hold=True):
        sem = sem or self.own
        self.c[sem.name] = self.c.get(sem.name, 0) + 1
        ins.then_inc(sem, 1)
        if sem not in self.open:
            self.open.append(sem)
        if hold:
            self.settle()

    def settle(self):
        for sem in self.open:
            self.eng.wait_ge(sem, self.value(sem))
        self.open = []

    @contextmanager
    def loop(self, trips, per):
        per = {s.name: k for s, k in per}
        start = dict(self.c)
        with self.eng.Fori(0, trips) as i:
            self.i, self.per = i, per
            yield i
            self.settle()
        self.i = None
        for name in set(self.c) | set(per):
            got = self.c.get(name, 0) - start.get(name, 0)
            assert got == per.get(name, 0), (name, got, per)
            self.c[name] = start.get(name, 0) + trips * got


def trunk_program(nc, io):
    with ExitStack() as ctx:
        def sb(name, shape, dt=F32):
            return ctx.enter_context(nc.sbuf_tensor(name, shape, dt))

        def sem(name):
            return ctx.enter_context(nc.semaphore(name))

        PS = ctx.enter_context(nc.psum_tensor("PS", [P, 8, 512], F32))
        CONST = sb("CONST", [P, NCONST])
        VEC = sb("VEC", [P, NVEC])
        WRT = sb("WRT", [P, 2, KD, NG + NE])
        BRT = sb("BRT", [P, 2, NG + NE])
        PTB = sb("PTB", [1, NS * NPG], I32)
        EPST = sb("EPST", [P, 1])
        CT = sb("CT", [P, KD, 1 + NS])
        IDX = sb("IDX", [P, NCH, NE], U32)
        HOLD = sb("HOLD", [1, 2])
        IDXO = sb("IDXO", [P, 1], U32)
        FLAG = sb("FLAG", [1, 2], I32)
        MOD = sb("MOD", [P, 2 * 6 * KD, 1 + NS])
        AM = sb("AM", [P, KD, 1 + NS])
        TS = sb("TS", [P, 2 * NS])
        RS = sb("RS", [P, 2, T])
        X = sb("X", [P, KD, T])
        H = sb("H", [P, KD, T])
        QB = sb("QB", [P, KD, T])
        O = sb("O", [P, KD, T])
        BE = sb("BE", [P, KD, T])
        VV = sb("VV", [P, 4096])
        VS = sb("VS", [NS, GH * DV])
        AT = sb("AT", [P, 1024])
        SST = sb("SST", [P, 3072])
        WB = sb("WB", [P, SLOTS, 4096])

        def ident(a=P, b=P, p=0, c=0):
            return CONST[p:p + a, ID + c:ID + c + b]

        def const(col, n=P, lo=0, hi=P):
            return CONST[lo:hi, col:col + n]

        def const2(col, n=P, lo=0, hi=P):
            return SST[lo:hi, col:col + n]

        B = BE[:, 0:4, :]
        E = BE[:, 4:8, :]
        EF = E.rearrange("p a b -> p (a b)")
        HF = H[:, :, :].rearrange("p a b -> p (a b)")
        MROW = HF[0:32, 0:2048].rearrange("p (s n) -> p s n", s=SLOTS)
        MTURN = HF[:, 2048:2560].rearrange("p (s n c) -> p s n c", s=SLOTS, n=4)
        LATE = ([(SST[0:32, 1152:2176].rearrange("p (s n) -> p s n", s=2),
                  SST[:, 2176:2432].rearrange("p (s n c) -> p s n c", s=2, n=4))] * 2
                + [(B[0:32, 0:2, 0:512], B[:, 2, 0:256].rearrange("p (s n c) -> p s n c", s=2, n=4))] * 4
                + [(QB[:, :, :].rearrange("p a b -> p (a b)")[0:32, 2048:3072].rearrange("p (s n) -> p s n", s=2),
                    QB[:, :, :].rearrange("p a b -> p (a b)")[:, 3072:3328]
                    .rearrange("p (s n c) -> p s n c", s=2, n=4))] * 3
                + [(HF[0:32, 0:1024].rearrange("p (s n) -> p s n", s=2),
                    HF[:, 2048:2304].rearrange("p (s n c) -> p s n c", s=2, n=4))] * 3)
        LATE_BANK = [6, 7, 4, 5, 4, 5, 6, 7, 6, 7, 4, 7]
        V = VV[:, :].rearrange("p (t n) -> p t n", t=4)
        CKV = VV[:, 0:3 * T].rearrange("p (k t) -> p k t", k=3)
        VP = VV[:, 3 * T:3 * T + 2048].rearrange("p (k n) -> p k n", k=4)
        S = SST[:, 0:1024]
        ST = SST[:, 1024:3072].rearrange("p (b n) -> p b n", b=2)
        PG = WB[:, 1, 0:PSL * PROW].rearrange("p (k n) -> p k n", k=PSL)
        KRT = WB[0:ROPE, 2, 0:PSL * PAGE].rearrange("p (k n) -> p k n", k=PSL)
        CN = WB[:, 2, PSL * PAGE:PSL * (PAGE + KVR)].rearrange("p (k n) -> p k n", k=PSL)

        def two(ap):
            return ap.rearrange("p (a b) -> p a b", a=2)

        def halves(s, m=P):
            return PS[0:m, 2 * s:2 * s + 2, 0:HT]

        psum_full, psum_free = sem("psum_full"), sem("psum_free")
        ring_full = [sem(f"ring_full{s}") for s in range(SLOTS)]
        consts_in, x_in, mla_consts_in = sem("consts_in"), sem("x_in"), sem("mla_consts_in")
        pages_in = sem("page_table_in")
        vec_order, act_order = sem("vec_order"), sem("act_order")
        cond_silu, attn_ready = sem("cond_silu"), sem("attn_ready")
        mod_rows = sem("mod_rows")
        late_rows_clear = sem("late_rows_clear")
        late_mod_full, late_mod_rows, late_mod_ready = (sem("late_mod_full"), sem("late_mod_rows"),
                                                        sem("late_mod_ready"))
        sq_ready, rms_ready, h_ready = sem("sq_ready"), sem("rms_ready"), sem("h_ready")
        glow_ready, softplus_ready, decay_ready, exp_ready = (sem("glow_ready"), sem("softplus_ready"),
                                                              sem("decay_ready"), sem("exp_ready"))
        decayed, prep_full, prep_done = sem("decayed"), sem("prep_full"), sem("prep_done")
        o_full, o_taken, state_ready = sem("gla_o_full"), sem("gla_o_taken"), sem("state_ready")
        ks_full, km_ready, outer_full, snew_ready, os_full = (sem("ks_full"), sem("km_ready"), sem("outer_full"),
                                                              sem("snew_ready"), sem("os_full"))
        st_in = [sem(f"st_in{b}") for b in range(2)]
        st_out = [sem(f"st_out{b}") for b in range(2)]
        y_stored = sem("y_stored")
        stored, silu_ready = sem("stored"), sem("silu_ready")
        route_exp_in, route_exp = sem("route_exp_in"), sem("route_exp")
        tok_full, tok_copied = sem("tok_full"), sem("tok_copied")
        tok_stored = [sem(f"tok_stored{b}") for b in range(2)]
        routing_step, routing_full, rows_ready, idx_full, idx_ready = (sem("routing_step"), sem("routing_full"),
                                                             sem("rows_ready"),
                                                             sem("idx_full"), sem("idx_ready"))
        flag_ready = sem("flag_ready")
        xg_in = [sem(f"xg_in{b}") for b in range(2)]
        xt_full, xt_ready, gu_full, act_gated, hid_ready = (sem("xt_full"), sem("xt_ready"), sem("gu_full"),
                                                            sem("act_gated"), sem("hid_ready"))
        ht_full, ht_ready, down_full, y_dve, y_act = (sem("ht_full"), sem("ht_ready"), sem("down_full"),
                                                      sem("y_dve"), sem("y_act"))
        y_out = [sem(f"y_out{b}") for b in range(2)]
        pair_in = [sem(f"pair_in{b}") for b in range(2)]
        weighted = sem("weighted")
        mixed, mixed_full, pair_added = sem("mixed"), sem("mixed_full"), sem("pair_added")
        OVN = ("hold", "table", "table_full", "go", "x_in", "w_in", "xt_full", "xt", "gu_full", "silu", "hid", "ht_full",
               "ht", "down_full", "y", "out")
        more_step = [sem(f"more{l}_step") for l in range(2)]
        ov = [{n: sem(f"more{l}_{n}") for n in OVN} for l in range(2)]
        lat_ready, kr_ready = sem("lat_ready"), sem("kr_ready")
        sc_full, negmax_ready, exp_done, p_ready = sem("sc_full"), sem("negmax_ready"), sem("exp_done"), sem("p_ready")
        pt_full, pt_ready, pv_full, pv_done = sem("pt_full"), sem("pt_ready"), sem("pv_full"), sem("pv_done")
        qp_ready, ql_full, ql_ready = sem("qp_ready"), sem("ql_full"), sem("ql_ready")
        page_in = [sem(f"page_in{s}") for s in range(PSL)]
        cpage_in = [sem(f"cpage_in{s}") for s in range(PSL)]
        page_used, scores_taken, kn_full, page_sq = (sem("page_used"), sem("scores_taken"), sem("kn_full"),
                                                     sem("page_sq"))
        ssq_ready, krstd_ready, stat_ready, stat_full, shifted, p_exp = (sem("ssq_ready"), sem("krstd_ready"),
                                                                      sem("stat_ready"), sem("stat_full"),
                                                                      sem("shifted"), sem("p_exp"))
        cpage_used, acc_full, acc_taken = sem("cpage_used"), sem("acc_full"), sem("acc_taken")
        mout_full, mout_taken = sem("mout_full"), sem("mout_taken")
        olat_ready, osam_full, y_ready = sem("olat_ready"), sem("osam_full"), sem("y_ready")

        SQ, n = {}, 0
        for s, k in (("norm0", KD), ("onorm", 1), ("fnorm0", KD), ("kvnorm", KD), ("ckvnorm", 1),
                     ("cqnorm", 1), ("qss", 1), ("kss", 1), ("fnorm1", KD)):
            SQ[s] = n + 1
            n += k
        RMS, n = {}, 0
        for s, k in (("norm0", 1), ("onorm", 4), ("fnorm0", 1), ("kvnorm", 1), ("ckvnorm", 1),
                     ("cqnorm", 1), ("qss", 6), ("kss", 6), ("fnorm1", 1)):
            RMS[s] = n
            n += k
        HR = {s: KD * n for n, s in enumerate(("norm0", "fnorm0", "kvnorm", "norm2", "fnorm1"))}
        PAIRED = ("qss", "kss")

        def rms_buffer(stage, j):
            if stage in PAIRED:
                return E[:, 2 + j % 2, :] if j // 2 % 2 else RS[:, j % 2, :]
            return RS[:, (RMS[stage] + j) % 2, :]

        SCALE = float(QK) ** -0.5
        LAYERS = ("moe0", "moe1")

        def rows_of(q):
            return P if q < QT else NS

        WGU, WG = AT[0:GR, 0:512], AT[:, 512:640].rearrange("p (k n) -> p k n", k=KD)
        BM, BL, FE = (SST[:, 1024 + 32 * i:1056 + 32 * i].rearrange("p (h c) -> p h c", h=GH) for i in range(3))
        QP, PR = (AT[:, 48 * i:48 * i + 48].rearrange("p (k s) -> p k s", k=6) for i in range(2))
        QL = AT[:, 96:224].rearrange("p (r s h) -> p r s h", r=2, s=NS)
        QRS = AT[0:ROPE, 224:288].rearrange("p (s h) -> p s h", s=NS)
        NEW, KRS, MX, LS, DG = AT[:, 288:352], AT[:, 352:480], AT[:, 480:544], AT[:, 544:608], AT[0:64, 608:672]
        OL = AT[:, 688:816].rearrange("p (r s h) -> p r s h", r=2, s=NS)
        RLS, PNB, MC = AT[:, 816:880], AT[:, 880:944], AT[0:64, 672:673]
        SC, SSQ = HF[:, 0:1024], HF[:, 1024:2048]
        SQP = HF[:, 2048:4096].rearrange("p (b n) -> p b n", b=4)
        ACC = HF[0:MH, 1024:3072].rearrange("p (s r n) -> p s r n", s=NS, r=2)
        LOG = AT[:, 0:100].rearrange("p (q n) -> p q n", q=5)
        GX, OHG, OH1, OH2, LE, TMP = (AT[:, 100 + 20 * i:120 + 20 * i].rearrange("p (q n) -> p q n", q=5)
                                      for i in range(6))
        M1, M2, M3, X2 = (AT[:, 220 + 5 * i:225 + 5 * i] for i in range(4))
        W1, W2 = AT[:, 240:245], AT[:, 245:250]
        PK = [AT[:, 256 + 5 * k:261 + 5 * k] for k in range(2)]
        PC = [AT[:, 266 + 5 * k:271 + 5 * k] for k in range(2)]
        QF = QB[:, :, :].rearrange("p a b -> p (a b)")
        OF = O[:, :, :].rearrange("p a b -> p (a b)")
        BF = BE[:, :, :].rearrange("p a b -> p (a b)")
        OPK = BF[:, 0:1280].rearrange("p (k q n) -> p k q n", k=2, q=5)
        AK = [BF[:, 1280 + 80 * k:1360 + 80 * k].rearrange("p (q e) -> p q e", q=5) for k in range(2)]
        AS, AC = (BF[:, 1440 + 80 * k:1520 + 80 * k].rearrange("p (q e) -> p q e", q=5) for k in range(2))
        RK = [BF[:, 1600 + 160 * k:1760 + 160 * k].rearrange("p (q a e) -> p q a e", q=5, a=2) for k in range(2)]
        ATMP = BF[:, 1920:2000].rearrange("p (q e) -> p q e", q=5)
        SG, HID, HT_ = ([BF[:, 2048 + 512 * a + 256 * b:2304 + 512 * a + 256 * b] for b in range(2)]
                        for a in range(3))
        XG = [QF[:, 1024 * b:1024 * (b + 1)] for b in range(2)]
        XT = [QF[:, 2048 + 1024 * b:3072 + 1024 * b].rearrange("p (k n) -> p k n", k=KD) for b in range(2)]
        YB = [OF[:, 1024 * b:1024 * (b + 1)] for b in range(2)]
        TOKB = [OF[:, 2048 + 1024 * b:3072 + 1024 * b] for b in range(2)]
        PAIR = [[QF[:, 2048 * b + 1024 * k:2048 * b + 1024 * (k + 1)] for k in range(2)] for b in range(2)]
        LOGT = BF[0:NG + NE, 3584:3584 + T]
        SEL = AT[:, 336:416].rearrange("p (q g e) -> p q g e", q=5, g=NG)
        NM, LN = TS[:, 0:2], TS[:, 2:4]

        block = ctx.enter_context(nc.Block())

        def load_pages(q, odd):
            mine = range(odd, PSL, 2)

            def number(g, j):
                return q.value_load(PTB[0:1, bass.ds(g * PSL + j, 1)], min_val=0, max_val=io["npool"] - 1)

            def fetch(dst, src, page, landed):
                q.dma_start(dst, io[src][bass.ds(page, 1)].rearrange("a p n -> p (a n)")).then_inc(landed, 16)

            q.wait_ge(psum_full, LAST_USE["uq"])
            with q.Fori(0, NS * NPG // PSL) as g:
                for j in mine:
                    page = number(g, j)
                    q.wait_ge(page_used, g * PSL + (j + 1))
                    fetch(PG[:, j, :], "cache_t", page, page_in[j])
                    fetch(KRT[:, j, :], "cache_kr", page, page_in[j])
            for j in mine:
                fetch(CN[:, j, :], "cache", number(0, j), cpage_in[j])
            with q.Fori(1, NS * NPG // PSL) as g:
                for j in mine:
                    page = number(g, j)
                    q.wait_ge(cpage_used, g * PSL + (j + 1 - PSL))
                    fetch(CN[:, j, :], "cache", page, cpage_in[j])

        @block.sync
        def _(sp):
            sp.dma_start(CT[:, :, :], io["c"]).then_inc(consts_in, 16)
            sp.dma_start(VEC[:, :], io["vec"]).then_inc(consts_in, 16)

            def used(chunk):
                if chunk.startswith("adb"):
                    sp.wait_ge(late_mod_full, int(chunk[3:]) + 1)
                else:
                    sp.wait_ge(psum_full, LAST_USE[chunk])

            def load(name, src, before=None, part=None):
                slot, use = RING[name]
                dst = WB[:, slot, :] if part is None else WB[:, slot, part[0]:part[1]]
                if before:
                    used(before)
                sp.dma_start(dst, src).then_inc(ring_full[slot], 16)

            for j in range(SLOTS):
                load(f"ada{j}", io["ada"][0, j])
            sp.dma_start(X[:, :, :], io["x"]).then_inc(x_in, 16)
            sp.dma_start(CONST[:, :], io["const"]).then_inc(x_in, 16)
            sp.dma_start(WRT[:, :, :, :], io["router"]).then_inc(x_in, 16)
            sp.dma_start(BRT[:, :, :], io["router_b"].partition_broadcast(P)).then_inc(x_in, 16)
            sp.dma_start(PTB[:, :], io["pages"]).then_inc(pages_in, 16)
            sp.dma_start(WGU, io["gate_up"]).then_inc(x_in, 16)
            sp.dma_start(WG, io["gate_low"]).then_inc(x_in, 16)
            with sp.Fori(1, KADA // SLOTS) as i:
                for s in range(SLOTS):
                    sp.wait_ge(psum_full, i * SLOTS + (s + 1 - SLOTS))
                    sp.dma_start(WB[:, s, :], io["ada"][bass.ds(i, 1), s].rearrange("a p n -> p (a n)"))\
                        .then_inc(ring_full[s], 16)
            def late(n, before=None):
                load(f"adb{n}", io["ada"][(KADA + n) // SLOTS, (KADA + n) % SLOTS], before)

            for j, (name, before) in enumerate((("wq", "ada8"), ("wk", "ada9"), ("wv0", "ada10"), ("wv1", "ada11"))):
                load(name, io["gla"][j], before)
            for n, before in enumerate(("wq", "wk", "wv0", "wv1")):
                late(n, before)
            load("wr0", io["gla"][4], "adb0")
            load("wr1", io["gla"][5], "adb1")
            late(4, "adb2")
            late(5, "adb3")
            load("wo0", io["gla"][6], "adb4")
            load("wo1", io["gla"][7], "adb5")
            late(6, "wr0")
            late(7, "wr1")
            late(8, "wo0")

            def moe(l, before):
                gu, dn = io["moe_gu"][l], io["moe_dn"][l]
                for e in range(2):
                    if l:
                        sp.wait_ge(osam_full, 1)
                    if before[e]:
                        used(before[e])
                    sp.dma_start(WB[:, e, :], gu[0, e]).then_inc(ring_full[e], 16)
                    if before[2 + e]:
                        used(before[2 + e])
                    sp.dma_start(WB[:, 2 + e, 0:2048], dn[0, e]).then_inc(ring_full[2 + e], 16)
                with sp.Fori(1, NE // 2) as i:
                    for e in range(2):
                        sp.wait_ge(gu_full, i * 2 + (NE * l + e - 1))
                        sp.dma_start(WB[:, e, :], gu[bass.ds(i, 1), e].rearrange("a p n -> p (a n)"))\
                            .then_inc(ring_full[e], 16)
                        sp.wait_ge(down_full, i * 2 + (NE * l + e - 1))
                        sp.dma_start(WB[:, 2 + e, 0:2048], dn[bass.ds(i, 1), e].rearrange("a p n -> p (a n)"))\
                            .then_inc(ring_full[2 + e], 16)
                o = ov[l]
                gun, dnn = gu.rearrange("i e p n -> (i e) p n"), dn.rearrange("i e p n -> (i e) p n")
                sp.wait_ge(flag_ready, l + 1)
                most = sp.value_load(FLAG[0:1, l:l + 1], min_val=0, max_val=T)
                with sp.If(most > CAP):
                    with sp.Fori(0, NE) as e:
                        for c in range(NCH - 1):
                            sp.wait_ge(o["go"], e * (NCH - 1) + (c + 1))
                            sp.dma_start(WB[:, 0, :], gun[bass.ds(e, 1)].rearrange("a p n -> p (a n)"))\
                                .then_inc(o["w_in"], 16)
                            sp.dma_start(WB[:, 2, 0:2048], dnn[bass.ds(e, 1)].rearrange("a p n -> p (a n)"))\
                                .then_inc(o["w_in"], 16)
                    sp.wait_ge(o["down_full"], NE * (NCH - 1))

            moe(0, ("adb6", "adb7", "adb8", "wo1"))
            sp.wait_ge(gu_full, NE - 1)
            late(9)
            sp.wait_ge(gu_full, NE)
            late(10)
            sp.wait_ge(down_full, NE - 1)
            late(11)
            sp.wait_ge(down_full, NE)
            sp.wait_ge(mixed, 3)
            load("dkv", io["dkv"], part=(0, KD * QR))
            load("dq", io["dq"], "adb9", part=(0, KD * QR))
            load("uq", io["uq"], "adb11", part=(0, 3 * MH * QK))
            load("ukv", io["ukv"], "dkv", part=(0, 3072))
            load("mwo", io["mwo"], "dq")

            sp.wait_ge(pages_in, 16)
            load_pages(sp, 0)
            moe(1, ("mwo", None, None, None))
            for q in range(5):
                sp.wait_ge(y_ready, q + 1)
                m = rows_of(q)
                sp.dma_start(io["y"][:, :, q * P:q * P + m], X[:, :, q * P:q * P + m]).then_inc(y_stored, 16)
            sp.wait_ge(y_stored, 16 * 5)
            sp.wait_ge(stored, 16 * 3)
            for b in range(2):
                sp.wait_ge(st_out[b], 16 * NS // 2)

        @block.gpsimd
        def _(pool):
            pool.wait_ge(exp_ready, 1)
            pool.wait_ge(state_ready, NC)
            for b in range(NS):
                if b >= 2:
                    pool.wait_ge(os_full, b - 1)
                    pool.wait_ge(st_out[b % 2], 16 * (b // 2))
                pool.dma_start(ST[:, b % 2, :], io["state_in"][b]).then_inc(st_in[b % 2], 16)
                if b == 0:
                    pool.dma_start(io["state_p"], S).then_inc(stored, 16)
                if b >= 1:
                    pool.wait_ge(snew_ready, GH * b)
                    pool.dma_start(io["state_s"][b - 1], ST[:, (b - 1) % 2, :]).then_inc(st_out[(b - 1) % 2], 16)
            pool.wait_ge(snew_ready, GH * NS)
            pool.dma_start(io["state_s"][NS - 1], ST[:, 1, :]).then_inc(st_out[1], 16)
            pool.wait_ge(stored, 16)
            for b in range(2):
                pool.wait_ge(st_out[b], 16 * NS // 2)
            pool.wait_ge(os_full, NS)
            pool.dma_start(SST[:, 0:NCONST2], io["const2"]).then_inc(mla_consts_in, 16)

            def experts(l):
                o, h = ov[l], HOLD[:, l:l + 1]

                def hold_wait(name, e, c, k):
                    pool.wait_ge(o["hold"], e * (2 * (NCH - 1)) + (2 * c + k + 1))
                    pool.wait_ge(o[name], e * (NCH - 1) + (c + 1))
                    nc.gpsimd.tensor_tensor(h, h, h, ALU.add).then_inc(o["hold"], 1)

                def gather(e):
                    b = e % 2
                    if e >= 2:
                        pool.wait_ge(xt_full, NE * l + e - 1)
                    pool.indirect_dma_start(XG[b], None, io["rows"], bass.IndirectOffsetOnAxis(IDX[:, 0, e:e + 1], 0),
                                            bounds_check=2 * T - 1, oob_is_err=False).then_inc(xg_in[b], 16)

                pool.wait_ge(idx_ready, l + 1)
                for b in range(2):
                    pool.wait_ge(tok_stored[b], (96, 64)[b] * (l + 1))
                gather(0)
                gather(1)
                for e in range(NE):
                    if e + 2 < NE:
                        gather(e + 2)
                    pool.wait_ge(y_dve, NE * l + e + 1)
                    pool.wait_ge(y_act, NE * l + e + 1)
                    pool.indirect_dma_start(io["outs"], bass.IndirectOffsetOnAxis(IDX[:, 0, e:e + 1], 0), YB[e % 2],
                                            None, bounds_check=2 * T - 1, oob_is_err=False)\
                        .then_inc(y_out[e % 2], 16)
                pool.wait_ge(flag_ready, l + 1)
                most = pool.value_load(FLAG[0:1, l:l + 1], min_val=0, max_val=T)
                with pool.If(most > CAP):
                    nc.gpsimd.memset(h, 0.0).then_inc(o["hold"], 1)
                    with pool.Fori(0, NE) as e:
                        for c in range(NCH - 1):
                            hold_wait("go", e, c, 0)
                            pool.indirect_dma_start(XG[0], None, io["rows"], bass.IndirectOffsetOnAxis(IDXO[:, 0:1], 0),
                                                    bounds_check=2 * T - 1, oob_is_err=False)\
                                .then_inc(o["x_in"], 16)
                            hold_wait("y", e, c, 1)
                            pool.indirect_dma_start(io["outs"], bass.IndirectOffsetOnAxis(IDXO[:, 0:1], 0), YB[0],
                                                    None, bounds_check=2 * T - 1, oob_is_err=False)\
                                .then_inc(o["out"], 16)
                    pool.wait_ge(o["out"], 16 * NE * (NCH - 1))
                for b in range(2):
                    pool.wait_ge(y_out[b], 8 * NE * (l + 1))

            experts(0)
            pool.wait_ge(lat_ready, 2)
            pool.dma_start(io["ckv"], CKV[:, 0:2, :]).then_inc(stored, 16)
            pool.wait_ge(kr_ready, 1)
            pool.dma_start(io["kr"], CKV[0:ROPE, 2, :]).then_inc(stored, 16)
            pool.wait_ge(pages_in, 16)
            load_pages(pool, 1)

            experts(1)

        @block.tensor
        def _(pe):
            mm = nc.tensor.matmul

            def slot_for(t):
                pe.wait_ge(psum_free, t.count())
                s = t.slot()
                t.n += 1
                return s

            def product(t, pairs, m=P, ready=None):
                s = slot_for(t)
                for a in range(2):
                    for k, (w, x) in enumerate(pairs):
                        if ready and not a:
                            pe.wait_ge(ready[0], ready[1] + k)
                        last = mm(PS[0:m, 2 * s + a, 0:HT], w, x[:, a * HT:(a + 1) * HT],
                                  start=(k == 0), stop=(k == len(pairs) - 1))
                last.then_inc(psum_full, 1)

            def chunk(name):
                slot, use = RING[name]
                pe.wait_ge(ring_full[slot], 16 * use)
                return slot

            pe.wait_ge(cond_silu, 1)
            with pe.Fori(0, KADA // SLOTS) as i:
                for s in range(SLOTS):
                    pe.wait_ge(psum_free, i * SLOTS + (s + 1))
                    pe.wait_ge(ring_full[s], i * 16 + 16)
                    w = WB[:, s, :].rearrange("p (k n) -> p k n", k=KD)
                    for k in range(KD):
                        last = mm(PS[0:1 + NS, 2 * s, :], CT[:, k, :], w[:, k, :], start=(k == 0), stop=(k == KD - 1))
                    last.then_inc(psum_full, 1)

            def late_modulation(n):
                w = WB[:, chunk(f"adb{n}"), :].rearrange("p (k n) -> p k n", k=KD)
                if n >= 2:
                    pe.wait_ge(late_mod_ready, n - 1)
                for k in range(KD):
                    last = mm(PS[0:1 + NS, LATE_BANK[n], :], CT[:, k, :], w[:, k, :], start=(k == 0), stop=(k == KD - 1))
                last.then_inc(late_mod_full, 1)

            def mean_square(stage, rows, avg):
                t = Turn(stage)
                if len(rows) == KD:
                    product(t, [(avg, r) for r in rows], ready=(sq_ready, SQ[stage]))
                else:
                    pe.wait_ge(sq_ready, SQ[stage])
                    product(t, [(avg, r) for r in rows])

            def stream(stage, n):
                return None if n else (h_ready, HR[stage] + 1)

            pe.wait_ge(x_in, 96)
            mean_square("norm0", [H[:, k, :] for k in range(KD)], const(O1024))

            t = Turn("qk")
            for name in ("wq", "wk"):
                w = WB[:, chunk(name), :].rearrange("p (k n) -> p k n", k=KD)
                for n in range(4):
                    product(t, [(w[:, k, n * P:(n + 1) * P], H[:, k, :]) for k in range(KD)],
                            ready=stream("norm0", n) if name == "wq" else None)
            product(Turn("glow"), [(WG[:, k, :], H[:, k, :]) for k in range(KD)], m=GR)
            pe.wait_ge(glow_ready, 1)
            t = Turn("gup")
            for n in range(4):
                product(t, [(WGU[:, n * P:(n + 1) * P], EF[0:GR, 0:T])])
            t = Turn("v")
            w = [WB[:, chunk(f"wv{a}"), :].rearrange("p (k n) -> p k n", k=KD) for a in range(2)]

            def values(q):
                m = rows_of(q)
                s = slot_for(t)
                for a in range(2):
                    for k in range(KD):
                        last = mm(PS[0:m, 2 * s + a, :], H[:, k, q * P:q * P + m], w[a][:, k, :],
                                  start=(k == 0), stop=(k == KD - 1))
                last.then_inc(psum_full, 1)

            for q in range(QT):
                values(q)

            pe.wait_ge(psum_free, SLOTS + FIRST["v"] + 2)
            late_modulation(0)
            late_modulation(1)
            values(QT)

            pe.wait_ge(decayed, 2)
            for q in range(QT):
                if q >= 2:
                    pe.wait_ge(prep_done, 2 * (q - 1))
                for h in range(GH):
                    nc.tensor.transpose(PS[:, q % 2, h * P:(h + 1) * P], QB[:, 4 + h, q * P:(q + 1) * P], ident())
                    for a in range(2):
                        sl = slice(q * P + a * C, q * P + (a + 1) * C)
                        last = mm(PS[a * C:(a + 1) * C, 2 + q % 2, h * C:(h + 1) * C], QB[:, 4 + h, sl], QB[:, h, sl],
                                  start=True, stop=True)
                last.then_inc(prep_full, 1)
            for c in range(NC):
                q, lo = c // 2, C * (c % 2)
                if c == 0:
                    pe.wait_ge(prep_done, 2 * QT)
                if c >= 2:
                    pe.wait_ge(state_ready, c - 1)
                    pe.wait_ge(o_taken, c - 1)
                for h in range(GH):
                    mm(PS[:, 2 * (c % 2) + h // 2, (h % 2) * DV:(h % 2 + 1) * DV],
                       EF[lo:lo + C, q * 512 + h * DK:q * 512 + (h + 1) * DK],
                       V[lo:lo + C, q, h * DV:(h + 1) * DV], start=True, stop=True)
                for n in range(2 * GH):
                    last = mm(PS[:, 4 + c % 2, n * C:(n + 1) * C], V[lo:lo + C, q, n * P:(n + 1) * P],
                              AT[lo:lo + C, q * 256 + n // 2 * C:q * 256 + (n // 2 + 1) * C], start=(n == 0),
                              stop=(c == 0), skip_group_check=True)
                if c >= 1:
                    pe.wait_ge(state_ready, c)
                    for n in range(2 * GH):
                        last = mm(PS[:, 4 + c % 2, n * C:(n + 1) * C], S[:, n * P:(n + 1) * P],
                                  QB[:, n // 2, c * C:(c + 1) * C], start=False, stop=True, skip_group_check=True)
                last.then_inc(o_full, 1)
            for h in range(GH):
                last = nc.tensor.transpose(PS[0:NS, 6, h * P:(h + 1) * P], QB[:, 4 + h, NP:T], ident())
            last.then_inc(ks_full, 1)

            def outer(b):
                pe.wait_ge(km_ready, b + 1)
                if b >= 2:
                    pe.wait_ge(snew_ready, GH * (b - 1))
                if b == 0:
                    pe.wait_ge(state_ready, NC)
                for h in range(GH):
                    last = mm(PS[:, 2 * (b % 2) + h // 2, (h % 2) * DV:(h % 2 + 1) * DV],
                              EF[0:NS, 512 * (1 + b % 2) + h * DK:512 * (1 + b % 2) + (h + 1) * DK],
                              VS[:, h * DV:(h + 1) * DV], start=True, stop=True)
                last.then_inc(outer_full, 1)

            outer(0)
            for b in range(NS):
                if b + 1 < NS:
                    outer(b + 1)
                pe.wait_ge(snew_ready, GH * (b + 1))
                for n in range(2 * GH):
                    last = mm(PS[:, 7, b * 8 + n:b * 8 + n + 1], ST[:, b % 2, n * P:(n + 1) * P],
                              QB[:, n // 2, NP + b:NP + b + 1], start=True, stop=True)
                last.then_inc(os_full, 1)
                if b % 2 == 0:
                    if b == 0:
                        pe.wait_ge(o_taken, NC)
                    late_modulation(2 + b // 2)

            pe.wait_ge(sq_ready, SQ["onorm"])
            t = Turn("onorm")
            for h in range(GH):
                product(t, [(const(O256), BE[:, 2 * h + a, :]) for a in range(2)])
            t = Turn("r")
            for name in ("wr0", "wr1"):
                w = WB[:, chunk(name), :].rearrange("p (k n) -> p k n", k=KD)
                for n in range(4):
                    product(t, [(w[:, k, n * P:(n + 1) * P], H[:, k, :]) for k in range(KD)])
            pe.wait_ge(psum_free, SLOTS + FIRST["r"] + 8)
            t = Turn("gout")
            for name in ("wo0", "wo1"):
                w = WB[:, chunk(name), :].rearrange("p (k n) -> p k n", k=KD)
                for n in range(4):
                    product(t, [(w[:, k, n * P:(n + 1) * P], O[:, k, :]) for k in range(KD)])

            def experts(l):
                mean_square(f"fnorm{l}", [H[:, k, :] for k in range(KD)], const(O1024))
                s = slot_for(Turn(f"route{l}"))
                for k in range(KD):
                    pe.wait_ge(h_ready, HR[f"fnorm{l}"] + k + 1)
                    for a in range(2):
                        last = mm(PS[0:NG + NE, 2 * s + a, 0:HT], WRT[:, l, k, :], H[:, k, a * HT:(a + 1) * HT],
                                  start=(k == 0), stop=(k == KD - 1))
                last.then_inc(psum_full, 1)

                def turn_stream(q):
                    b = 2 * ((s + 1 + q % 2) % SLOTS)
                    if q >= 2:
                        pe.wait_ge(tok_copied, 5 * l + q - 1)
                    m = rows_of(q)
                    for k in range(KD):
                        last = nc.tensor.transpose(PS[0:m, b + k // 4, (k % 4) * P:(k % 4 + 1) * P],
                                                   H[:, k, q * P:q * P + m], ident())
                    last.then_inc(tok_full, 1)

                turn_stream(0)
                pe.wait_ge(routing_step, 2 * l + 1)
                for q in range(5):
                    m = rows_of(q)
                    last = nc.tensor.transpose(PS[0:m, 2 * s, q * 20:q * 20 + 20], LOGT[:, q * P:q * P + m],
                                               ident(NG + NE, NG + NE))
                last.then_inc(routing_full, 1)
                if l == 0:
                    late_modulation(6)
                for q in range(1, QT):
                    turn_stream(q)
                pe.wait_ge(routing_step, 2 * l + 2)
                mm(PS[:, 2 * s, 0:5 * NE], const(TRIS), AS.rearrange("p q e -> p (q e)"), start=True, stop=False)
                last = mm(PS[:, 2 * s, 0:5 * NE], const(ONE), AC.rearrange("p q e -> p (q e)"), start=False, stop=True)
                last.then_inc(routing_full, 1)
                for q in range(5):
                    m = rows_of(q)
                    last = mm(PS[:, 2 * s + 1, 0:NE], const(ONE, P, 0, m), AS[0:m, q, :], start=(q == 0),
                              stop=(q == QT))
                last.then_inc(routing_full, 1)
                turn_stream(QT)

                def index_table(bank):
                    for q in range(5):
                        m = rows_of(q)
                        for k in range(2):
                            last = mm(PS[:, bank, 0:2 * NE], OPK[0:m, k, q, :],
                                      RK[k][0:m, q, :, :].rearrange("p a e -> p (a e)"),
                                      start=(q + k == 0), stop=(q + k == QT + 1))
                    return last

                if l == 0:
                    late_modulation(7)
                pe.wait_ge(rows_ready, l + 1)
                index_table(2 * s).then_inc(idx_full, 1)
                if l == 0:
                    late_modulation(8)

                base, name = NE * l, LAYERS[l]

                def turn_rows(n, b, x_in, count, done):
                    pe.wait_ge(x_in, count)
                    for k in range(KD):
                        last = nc.tensor.transpose(PS[:, k // 4, (k % 4) * P:(k % 4 + 1) * P],
                                                   XG[b][:, k * P:(k + 1) * P], ident())
                    last.then_inc(done, 1)

                def gate_up(b, wslot, ks, bank):
                    w = WB[:, wslot, :].rearrange("p (k n) -> p k n", k=KD)
                    for k in ks:
                        last = mm(PS[:, bank, :], XT[b][:, k, :], w[:, k, :], start=(k == 0), stop=(k == KD - 1))
                    return last

                def turn_hidden(b):
                    for f in range(2):
                        last = nc.tensor.transpose(PS[:, 4, f * P:(f + 1) * P], HID[b][:, f * P:(f + 1) * P], ident())
                    return last

                def down(b, wslot):
                    w = WB[:, wslot, 0:2048].rearrange("p (f n) -> p f n", f=2)
                    for a in range(2):
                        for f in range(2):
                            last = mm(PS[:, 5 + a, :], HT_[b][:, f * P:(f + 1) * P], w[:, f, a * 512:(a + 1) * 512],
                                      start=(f == 0), stop=(f == 1))
                    return last

                def first_half(i, e):
                    if not (isinstance(i, int) and 2 * i + e == 0):
                        pe.wait_ge(xt_ready, i * 2 + (base + e))
                    turn_rows(0, e, xg_in[e], i * 16 + (128 * l + 16), xt_full)
                    pe.wait_ge(xt_ready, i * 2 + (base + e + 1))
                    pe.wait_ge(ring_full[e], i * 16 + 16 * RING[f"{name}_{e}"][1])
                    gate_up(e, e, range(KD // 2), 2 + e)

                def rest(i, e):
                    gate_up(e, e, range(KD // 2, KD), 2 + e).then_inc(gu_full, 1)

                def hidden(i, e):
                    pe.wait_ge(hid_ready, i * 2 + (base + e + 1))
                    turn_hidden(e).then_inc(ht_full, 1)

                def finish(i, e):
                    pe.wait_ge(ht_ready, i * 2 + (base + e + 1))
                    pe.wait_ge(ring_full[2 + e], i * 16 + 16 * RING[f"{name}_{2 + e}"][1])
                    if not (isinstance(i, int) and 2 * i + e == 0):
                        pe.wait_ge(y_dve, i * 2 + (base + e))
                        pe.wait_ge(y_act, i * 2 + (base + e))
                    down(e, 2 + e).then_inc(down_full, 1)

                def step(i, e):
                    first_half(i, e) if e else first_half(i, 0)
                    prev = (i, 0) if e else (i - 1, 1)
                    hidden(*prev)
                    rest(i, e)
                    finish(*prev)

                first_half(0, 0)
                rest(0, 0)
                step(0, 1)
                with pe.Fori(1, NE // 2) as i:
                    step(i, 0)
                    step(i, 1)
                hidden(NE // 2 - 1, 1)
                finish(NE // 2 - 1, 1)

                o = ov[l]
                pe.wait_ge(flag_ready, l + 1)
                most = pe.value_load(FLAG[0:1, l:l + 1], min_val=0, max_val=T)
                with pe.If(most > CAP):
                    for c in range(NCH - 1):
                        pe.wait_ge(o["table"], c + 1)
                        index_table(7).then_inc(o["table_full"], 1)
                    with pe.Fori(0, NE) as e:
                        for c in range(NCH - 1):
                            n = e * (NCH - 1) + (c + 1)
                            turn_rows(0, 0, o["x_in"], e * (16 * (NCH - 1)) + 16 * (c + 1), o["xt_full"])
                            pe.wait_ge(o["xt"], n)
                            pe.wait_ge(o["w_in"], e * (32 * (NCH - 1)) + 32 * (c + 1))
                            gate_up(0, 0, range(KD), 2).then_inc(o["gu_full"], 1)
                            pe.wait_ge(o["hid"], n)
                            turn_hidden(0).then_inc(o["ht_full"], 1)
                            pe.wait_ge(o["ht"], n)
                            down(0, 2).then_inc(o["down_full"], 1)

                if l == 0:
                    for n in (9, 10, 11):
                        late_modulation(n)
                for q in range(5):
                    m = rows_of(q)
                    b = 2 * (q % 2)
                    if q >= 2:
                        pe.wait_ge(pair_added, 5 * l + q - 1)
                    pe.wait_ge(mixed, 5 * l + q + 1)
                    for k in range(KD):
                        last = nc.tensor.transpose(PS[:, b + k // 4, (k % 4) * P:(k % 4) * P + m],
                                                   PAIR[q % 2][0][0:m, k * P:(k + 1) * P], ident(m, m))
                    last.then_inc(mixed_full, 1)

            experts(0)

            mean_square("kvnorm", [H[:, k, :] for k in range(KD)], const(O1024))
            t = Turn("dkv")
            w = WB[:, chunk("dkv"), 0:KD * QR].rearrange("p (k n) -> p k n", k=KD)
            for n in range(3):
                product(t, [(w[:, k, n * P:(n + 1) * P], H[:, k, :]) for k in range(KD)],
                        ready=stream("kvnorm", n))
            t = Turn("dq")
            w = WB[:, chunk("dq"), 0:KD * QR].rearrange("p (k n) -> p k n", k=KD)
            for n in range(3):
                product(t, [(w[:, k, n * P:(n + 1) * P], QB[:, k, :]) for k in range(KD)], ready=stream("norm2", n))
            mean_square("ckvnorm", [E[:, k, :] for k in range(2)], const(O256))
            pe.wait_ge(mla_consts_in, 16)
            product(Turn("krot"), [(const2(ROT), CKV[:, 2, :])])
            mean_square("cqnorm", [H[:, k, :] for k in range(3)], const(O384))
            pe.wait_ge(lat_ready, 1)
            t = Turn("uq")
            w = WB[:, chunk("uq"), 0:3 * MH * QK].rearrange("p (k n) -> p k n", k=3)
            for n in range(6):
                product(t, [(w[:, k, n * P:(n + 1) * P], B[:, k, :]) for k in range(3)])
            pe.wait_ge(psum_free, SLOTS + t.n)
            t = Turn("qrot")
            for j in range(2):
                product(t, [(const2(ROT), QB[:, 4 + j, :])])
            pe.wait_ge(sq_ready, SQ["qss"])
            t = Turn("qss")
            for m in range(4):
                product(t, [(const2(B64), H[:, m, :]), (const2(F0 + (m % 2) * P), H[:, 4 + m // 2, :])])
            for j in range(2):
                product(t, [(const2(B32), H[:, 4 + j, :])]
                        + [(const2(E0 + u * P), H[:, 2 * j + u, :]) for u in range(2)])
            chunk("ukv")
            wukv = WB[:, RING["ukv"][0], :]
            t = Turn("uk")
            for n in range(4):
                product(t, [(wukv[:, k * 512 + n * P:k * 512 + (n + 1) * P], CKV[:, k, :]) for k in range(2)])
            t = Turn("uv")
            for q in range(QT):
                s = slot_for(t)
                for k in range(2):
                    last = mm(PS[:, 2 * s, :], CKV[:, k, q * P:(q + 1) * P],
                              wukv[:, 1024 + k * 512:1536 + k * 512], start=(k == 0), stop=(k == 1))
                last.then_inc(psum_full, 1)
            pe.wait_ge(sq_ready, SQ["kss"])
            t = Turn("kss")
            for m in range(4):
                product(t, [(const2(B64), H[:, m, :]), (const2(K1), H[:, 4, :])])
            for j in range(2):
                product(t, [(const2(K1), H[:, 4, :])]
                        + [(const2(E0 + u * P), H[:, 2 * j + u, :]) for u in range(2)])

            pe.wait_ge(psum_free, SLOTS + FIRST["kss"] + 6)
            pe.wait_ge(qp_ready, 2)
            for r in range(2):
                for h in range(MH):
                    lo = NOPE * (h % 2)
                    mm(PS[:, 3 * (h % 2), (r * 4 + h // 2) * 8:(r * 4 + h // 2) * 8 + 8],
                       wukv[lo:lo + NOPE, 2048 + (h // 2) * 256 + r * P:2048 + (h // 2) * 256 + (r + 1) * P],
                       QP[lo:lo + NOPE, h // 2, :], start=True, stop=True)
            for h in range(MH):
                mm(PS[0:ROPE, 1, h * 8:h * 8 + 8], ident(P, ROPE, 0, ROPE * (h % 4)), QP[:, 4 + h // 4, :],
                   start=True, stop=True)
            for h in range(MH):
                mm(PS[0:1, 2, h * 8:h * 8 + 8], const2(B64 + NOPE * (h % 2), 1), PR[:, h // 2, :],
                   start=True, stop=False)
                last = mm(PS[0:1, 2, h * 8:h * 8 + 8], const2(B32 + ROPE * (h % 4), 1), PR[:, 4 + h // 4, :],
                          start=False, stop=True)
            last.then_inc(ql_full, 1)
            pe.wait_ge(ql_ready, 6)

            def scores(n):
                q, h = n // MH, n % MH
                nk = (q + 1) * P
                if n >= 2:
                    pe.wait_ge(exp_done, n - 1)
                lo, lr = NOPE * (h % 2), ROPE * (h % 4)
                mm(PS[:, n % 2, 0:nk], QB[lo:lo + NOPE, h // 2, q * P:(q + 1) * P], O[lo:lo + NOPE, h // 2, 0:nk],
                   start=True, stop=False)
                mm(PS[:, n % 2, 0:nk], QB[lr:lr + ROPE, 4 + h // 4, q * P:(q + 1) * P],
                   O[lr:lr + ROPE, 4 + h // 4, 0:nk], start=False, stop=True).then_inc(sc_full, 1)

            def page_scores(g):
                i, sl = g // NPG, g % PSL
                pe.wait_ge(page_in[sl], 32 * (g // PSL + 1))
                if sl == 0 and g // PSL >= 2:
                    pe.wait_ge(scores_taken, g // PSL - 1)
                if g >= 2:
                    pe.wait_ge(page_sq, g - 1)
                out = PS[:, 3 + 2 * (g // PSL % 2), 8 * sl:8 * sl + 8]
                for r in range(2):
                    mm(out, PG[:, sl, r * P:(r + 1) * P], QL[:, r, i, :], start=(r == 0), stop=False)
                mm(out, KRT[:, sl, :], QRS[:, i, :], start=False, stop=True)
                for r in range(2):
                    last = mm(PS[:, 6 + g % 2, :], PG[:, sl, r * P:(r + 1) * P], wukv[:, r * 512:(r + 1) * 512],
                              start=(r == 0), stop=(r == 1))
                last.then_inc(kn_full, 1)

            scores(0)
            for n in range(QT * MH):
                q, h = n // MH, n % MH
                if n + 1 < QT * MH:
                    scores(n + 1)
                page_scores(4 * n)
                page_scores(4 * n + 1)
                pe.wait_ge(p_ready, n + 1)
                for k in range(q + 1):
                    last = nc.tensor.transpose(PS[:, 2, k * P:(k + 1) * P],
                                               EF[:, 512 * (n % 2) + k * P:512 * (n % 2) + (k + 1) * P], ident())
                last.then_inc(pt_full, 1)
                page_scores(4 * n + 2)
                page_scores(4 * n + 3)
                pe.wait_ge(pt_ready, n + 1)
                if n >= 1:
                    pe.wait_ge(pv_done, n)
                lo = MV * (h % 2)
                for k in range(q + 1):
                    last = mm(PS[lo:lo + MV, 4, 0:P], VP[:, k, h * MV:(h + 1) * MV],
                              EF[:, 1024 + 512 * (n % 2) + k * P:1024 + 512 * (n % 2) + (k + 1) * P],
                              start=(k == 0), stop=(k == q))
                last.then_inc(pv_full, 1)

            wmo = WB[:, chunk("mwo"), :].rearrange("p (k n) -> p k n", k=4)

            def prompt_out(n):
                if n >= 2:
                    pe.wait_ge(mout_taken, n - 1)
                for k in range(4):
                    last = mm(PS[:, 4 + n % 2, :], wmo[:, k, n * P:(n + 1) * P], B[:, k, 0:NP], start=(k == 0),
                              stop=(k == 3))
                last.then_inc(mout_full, 1)

            pe.wait_ge(pv_done, QT * MH)
            pe.wait_ge(scores_taken, NS * NPG // PSL)
            prompt_out(0)
            prompt_out(1)

            pe.wait_ge(stat_ready, 1)
            nc.tensor.transpose(PS[0:64, 6, 0:P], MX, ident()).then_inc(stat_full, 1)
            pe.wait_ge(stat_ready, 2)
            mm(PS[:, 7, 0:64], const(ONE, P, 0, 64), DG, start=True, stop=True).then_inc(stat_full, 1)
            pe.wait_ge(stat_ready, 3)
            mm(PS[:, 6, 0:64], const(ONE), LS, start=True, stop=True)
            mm(PS[:, 6, 64:128], const(ONE, P, 0, 1), NEW[0:1, :], start=True, stop=True).then_inc(stat_full, 1)
            for g in range(NS * NPG):
                i, j, sl = g // NPG, g % NPG, g % PSL
                pe.wait_ge(cpage_in[sl], 16 * (g // PSL + 1))
                last = mm(PS[0:MH, i // 2, (i % 2) * KVR:(i % 2 + 1) * KVR], HF[:, g * MH:(g + 1) * MH], CN[:, sl, :],
                          start=(j == 0), stop=(j == NPG - 1))
                last.then_inc(cpage_used, 1)
                if j == NPG - 1 and i + 2 < KD:
                    prompt_out(i + 2)
            pe.wait_ge(mout_taken, KD)
            for i in range(NS):
                pe.wait_ge(acc_taken, i // 2 + 1)
                for r in range(2):
                    last = nc.tensor.transpose(PS[:, 5, r * 64 + i * MH:r * 64 + (i + 1) * MH], ACC[:, i, r, :],
                                               ident(MH, MH))
            last.then_inc(acc_full, 1)
            pe.wait_ge(olat_ready, 1)
            for h in range(MH):
                lo = MV * (h % 2)
                for r in range(2):
                    last = mm(PS[lo:lo + MV, 4, (h // 2) * 8:(h // 2) * 8 + 8],
                              wukv[:, 1024 + r * 512 + h * MV:1024 + r * 512 + (h + 1) * MV], OL[:, r, :, h],
                              start=(r == 0), stop=(r == 1))
            last.then_inc(osam_full, 1)
            pe.wait_ge(attn_ready, 1)
            s = slot_for(Turn("mout"))
            for n in range(KD):
                for k in range(4):
                    last = mm(PS[:, 2 * s, n * NS:(n + 1) * NS], wmo[:, k, n * P:(n + 1) * P], B[:, k, NP:T],
                              start=(k == 0), stop=(k == 3))
            last.then_inc(psum_full, 1)
            experts(1)

        @block.scalar
        def _(act):
            a = Order(act, act_order)
            f = nc.scalar.activation
            act.wait_ge(consts_in, 32)
            a(f(CT[:, :, :], CT[:, :, :], ACT.Silu), cond_silu)
            act.wait_ge(psum_free, SLOTS)
            with a.loop(KADA // SLOTS, [(mod_rows, SLOTS)]) as i:
                for s in range(SLOTS):
                    act.wait_ge(psum_full, i * SLOTS + (s + 1))
                    a(f(MROW[0:1 + NS, s, :], PS[0:1 + NS, 2 * s, :], ACT.Identity), mod_rows, hold=False)

            def late_modulation(n):
                act.wait_ge(late_mod_full, n + 1)
                if n >= 2:
                    act.wait_ge(late_mod_ready, n - 1)
                a(f(LATE[n][0][0:1 + NS, n % 2, :], PS[0:1 + NS, LATE_BANK[n], :], ACT.Identity), late_mod_rows,
                  hold=False)

            def rms(stage, n=1):
                t = Turn(stage)
                for j in range(n):
                    act.wait_ge(psum_full, t.count())
                    if j >= 2:
                        act.wait_ge(psum_free, SLOTS + t.n - 1)
                    r = two(rms_buffer(stage, j))
                    a(f(r, halves(t.slot()), ACT.Ln, bias=EPST[:, 0:1]))
                    a(f(r, r, ACT.Exp, scale=-0.5), rms_ready)
                    t.n += 1

            def paired_rms(stage):
                t = Turn(stage)
                for j in range(0, 6, 2):
                    r = [two(rms_buffer(stage, j + i)) for i in range(2)]
                    for i in range(2):
                        act.wait_ge(psum_full, t.count())
                        if j + i >= 4:
                            act.wait_ge(psum_free, SLOTS + t.n - 3)
                        a(f(r[i], halves(t.slot()), ACT.Ln, bias=EPST[:, 0:1]), hold=False)
                        t.n += 1
                    a.settle()
                    for i in range(2):
                        a(f(r[i], r[i], ACT.Exp, scale=-0.5), rms_ready, hold=False)
                    a.settle()

            rms("norm0")
            act.wait_ge(psum_free, SLOTS + FIRST["gup"] + 4)
            a(f(E, B, ACT.Abs))
            a(f(E, E, ACT.Exp, scale=-1.0))
            a(f(E, E, ACT.Ln, bias=CONST[:, ONE:ONE + 1]), softplus_ready)
            act.wait_ge(late_rows_clear, 1)
            late_modulation(0)
            late_modulation(1)
            act.wait_ge(decay_ready, 1)
            a(f(B[:, :, NP:T], B[:, :, NP:T], ACT.Exp))
            a(f(FE, FE, ACT.Exp))
            a(f(B[:, :, 0:NP], E[:, :, 0:NP], ACT.Exp), exp_ready)
            a(f(E[:, :, 0:NP], E[:, :, 0:NP], ACT.Exp, scale=-1.0), exp_ready)
            act.wait_ge(late_rows_clear, 2)
            for n in range(2, 6):
                late_modulation(n)
            rms("onorm", 4)
            t = Turn("r")
            for n in range(8):
                act.wait_ge(psum_full, t.count())
                a(f(two(QB[:, n, :]), halves(t.slot()), ACT.Silu), silu_ready)
                t.n += 1

            def experts(l):
                rms(f"fnorm{l}")
                if l == 0:
                    act.wait_ge(late_rows_clear, 3)
                    late_modulation(6)
                for q in range(5):
                    m, b = rows_of(q), q % 2
                    act.wait_ge(tok_full, 5 * l + q + 1)
                    if q >= 2:
                        act.wait_ge(tok_stored[b], (96, 64)[b] * l + 32 * (q // 2))
                    bank = 2 * ((FIRST[f"route{l}"] + 1 + b) % SLOTS)
                    a(f(TOKB[b][0:m, :].rearrange("p (a n) -> p a n", a=2), PS[0:m, bank:bank + 2, :], ACT.Identity),
                      tok_copied)
                    for k in range(2):
                        act.dma_start(io["rows"][k * T + q * P:k * T + q * P + m, :], TOKB[b][0:m, :])\
                            .then_inc(tok_stored[b], 16)
                    if q == 1:
                        act.wait_ge(route_exp_in, 2 * l + 1)
                        a(f(GX, GX, ACT.Exp), route_exp)
                        act.wait_ge(route_exp_in, 2 * l + 2)
                        a(f(X2, X2, ACT.Exp), route_exp)
                if l == 0:
                    late_modulation(7)
                    late_modulation(8)
                a.settle()
                cpy = lambda dst, src: f(dst, src, ACT.Identity)
                base = NE * l

                def hidden(i, e):
                    act.wait_ge(ht_full, i * 2 + (base + e + 1))
                    a(cpy(HT_[e], PS[:, 4, 0:256]), ht_ready, hold=False)

                def gate(i, e):
                    act.wait_ge(gu_full, i * 2 + (base + e + 1))
                    a(f(SG[e], PS[:, 2 + e, 0:FF], ACT.Silu), act_gated, hold=False)

                def output(i, e, first=False):
                    act.wait_ge(down_full, i * 2 + (base + e + 1))
                    if not first:
                        act.wait_ge(y_out[e], i * 16 + (128 * l))
                    a(cpy(YB[e][:, 512:1024], PS[:, 6, :]), y_act, hold=False)

                def step(i, e, first=False):
                    prev = (i, 0) if e else (i - 1, 1)
                    hidden(*prev)
                    gate(i, e)
                    output(*prev, first=first)

                gate(0, 0)
                step(0, 1, True)
                step(1, 0, True)
                step(1, 1)
                with a.loop(NE // 2 - 2, [(ht_ready, 2), (act_gated, 2), (y_act, 2)]) as j:
                    i = j + 2
                    step(i, 0)
                    step(i, 1)
                hidden(NE // 2 - 1, 1)
                output(NE // 2 - 1, 1)
                o = ov[l]
                act.wait_ge(flag_ready, l + 1)
                most = act.value_load(FLAG[0:1, l:l + 1], min_val=0, max_val=T)
                with act.If(most > CAP):
                    with act.Fori(0, NE) as e:
                        for c in range(NCH - 1):
                            act.wait_ge(o["gu_full"], e * (NCH - 1) + (c + 1))
                            f(SG[0], PS[:, 2, 0:FF], ACT.Silu).then_inc(o["silu"], 1)
                            act.wait_ge(o["out"], e * (16 * (NCH - 1)) + 16 * (c + 1))
                if l == 0:
                    act.wait_ge(late_rows_clear, 4)
                    late_modulation(9)
                    late_modulation(10)
                for b in range(2):
                    act.wait_ge(y_out[b], 8 * NE * (l + 1))
                act.wait_ge(down_full, NE * (l + 1))

                def fetch_pair(q):
                    m = rows_of(q)
                    for k in range(2):
                        act.dma_start(PAIR[q % 2][k][0:m, :], io["outs"][k * T + q * P:k * T + q * P + m, :])\
                            .then_inc(pair_in[q % 2], 16)

                fetch_pair(0)
                fetch_pair(1)
                if l == 0:
                    late_modulation(11)
                for q in range(5):
                    m, b = rows_of(q), q % 2
                    act.wait_ge(pair_in[b], (96, 64)[b] * l + 32 * (q // 2 + 1))
                    a(f(PAIR[b][0][0:m, :], PAIR[b][0][0:m, :], ACT.Identity, scale=W1[0:m, q:q + 1]), weighted,
                      hold=False)
                    if 1 <= q <= 3:
                        act.wait_ge(mixed_full, 5 * l + q)
                        fetch_pair(q + 1)
                a.settle()

            experts(0)
            for stage, n in (("kvnorm", 1), ("ckvnorm", 1), ("cqnorm", 1)):
                rms(stage, n)
            paired_rms("qss")
            paired_rms("kss")
            def probs(n):
                nk = (n // MH + 1) * P
                act.wait_ge(negmax_ready, n + 1)
                if n >= 2:
                    act.wait_ge(pt_full, n - 1)
                a(f(EF[:, 512 * (n % 2):512 * (n % 2) + nk], PS[:, n % 2, 0:nk], ACT.Exp, bias=NM[:, n % 2:n % 2 + 1],
                    scale=SCALE, accum_out=LN[:, n % 2:n % 2 + 1]), exp_done, hold=False)

            def page_squares(g):
                act.wait_ge(kn_full, g + 1)
                act.wait_ge(page_used, g + 5)
                a(f(RS[:, 0, 0:ROPE], PG[:, g % PSL, KVR:PROW], ACT.Square, accum_out=KRS[:, g:g + 1]))
                a(f(SQP[:, g % 4, :], PS[:, 6 + g % 2, :], ACT.Square), page_sq, hold=False)

            probs(0)
            for n in range(QT * MH):
                if n + 1 < QT * MH:
                    probs(n + 1)
                for g in range(4 * n, 4 * n + 4):
                    page_squares(g)
            a.settle()
            act.wait_ge(ssq_ready, 1)
            a(f(SSQ, SSQ, ACT.Ln, bias=EPST[:, 0:1], scale=1.0 / QK))
            a(f(SSQ, SSQ, ACT.Exp, scale=-0.5), krstd_ready)
            act.wait_ge(shifted, 1)
            a(f(NEW, NEW, ACT.Exp))
            a(f(SC, SC, ACT.Exp), p_exp)
            experts(1)

        @block.vector
        def _(dve):
            v = Order(dve, vec_order)
            nv = nc.vector
            tt, ts, stt, cp, red = (nv.tensor_tensor, nv.tensor_scalar, nv.scalar_tensor_tensor, nv.tensor_copy,
                                    nv.tensor_reduce)

            def full(t):
                dve.wait_ge(psum_full, t.count())
                s = t.slot()
                t.n += 1
                return s

            def rows(ap, n):
                return ap.unsqueeze(1).to_broadcast([P, n, T])

            v(nv.memset(MROW, 0.0))
            v(nv.memset(EPST[:, :], EPS), psum_free)
            v(nv.memset(AT[:, 672:688], 0.0), psum_free)
            v(nv.memset(TS[:, 0:NS], 0.0), psum_free)
            v(nv.memset(TS[:, NS:2 * NS], 0.0), psum_free)
            dve.wait_ge(consts_in, 32)
            with v.loop(KADA // SLOTS, [(psum_free, SLOTS), (vec_order, 4 * SLOTS)]) as i:
                for s in range(SLOTS):
                    dve.wait_ge(mod_rows, i * SLOTS + (s + 1))
                    src = MROW[:, s, :].bitcast(U32).rearrange("p (n w r) -> p w n r", w=4, r=32)
                    for w in range(4):
                        v(nv.transpose(MTURN[32 * w:32 * w + 32, s].bitcast(U32), src[:, w]), hold=w == 3)
                    v(tt(MOD[:, bass.ds(i * 16 + 4 * s, 4), :], MTURN[:, s, :, 0:1 + NS],
                         VEC[:, bass.ds(i * 16 + (ADAB + 4 * s), 4)].unsqueeze(2).to_broadcast([P, 4, 1 + NS]),
                         ALU.add), psum_free)

            def clear_late_rows(n):
                v(nv.memset(LATE[n][0], 0.0), late_rows_clear)

            def late_modulation(n):
                rows_in, turned_out = LATE[n]
                dve.wait_ge(late_mod_rows, n + 1)
                src = rows_in[:, n % 2, :].bitcast(U32).rearrange("p (n w r) -> p w n r", w=4, r=32)
                for w in range(4):
                    v(nv.transpose(turned_out[32 * w:32 * w + 32, n % 2].bitcast(U32), src[:, w]), hold=w == 3)
                lo = 4 * (KADA + n)
                v(tt(MOD[:, lo:lo + 4, :], turned_out[:, n % 2, :, 0:1 + NS],
                     VEC[:, ADAB + lo:ADAB + lo + 4].unsqueeze(2).to_broadcast([P, 4, 1 + NS]), ALU.add),
                  late_mod_ready)

            clear_late_rows(0)
            rms_used = [0]

            def normed(stage, j=0):
                rms_used[0] += 1
                dve.wait_ge(rms_ready, rms_used[0])
                return rms_buffer(stage, j)

            def squares(dst, src):
                v(tt(dst, src, src, ALU.mult), sq_ready)

            def stream_squares():
                for k in range(KD):
                    v(tt(H[:, k, :], X[:, k, :], X[:, k, :], ALU.mult), sq_ready, hold=False)

            def norm_modulate(stage, mod, gain, dst=H, r=None):
                if r is None:
                    stream_squares()
                v(stt(AM[:, :, :], MOD[:, mod + 8:mod + 16, :], 1.0,
                      VEC[:, gain:gain + KD].unsqueeze(2).to_broadcast([P, KD, 1 + NS]), ALU.add, ALU.mult))
                known = r is not None
                if not known:
                    r = normed(stage)
                    full(Turn(stage))
                hs = dst[:, :, NP:T]
                v(tt(hs, X[:, :, NP:T], r[:, NP:T].unsqueeze(1).to_broadcast([P, KD, NS]), ALU.mult),
                  None if known else psum_free)
                v(tt(hs, hs, AM[:, :, 1:], ALU.mult))
                v(tt(hs, hs, MOD[:, mod:mod + KD, 1:], ALU.add))

                def scaled(k):
                    v(stt(dst[:, k, 0:NP], X[:, k, 0:NP], AM[:, k, 0:1], r[:, 0:NP], ALU.mult, ALU.mult), hold=False)

                scaled(0)
                for k in range(KD):
                    if k + 1 < KD:
                        scaled(k + 1)
                    dve.wait_ge(vec_order, v.value(vec_order) - (1 if k + 1 < KD else 0))
                    v(ts(dst[:, k, 0:NP], dst[:, k, 0:NP], MOD[:, mod + k, 0:1], None, ALU.add), h_ready, hold=False)
                v.settle()

            def residual(stage, mod):
                t = Turn(stage)
                for n in range(KD):
                    s = full(t)
                    g = MOD[:, mod + n, 0:1]
                    v(stt(X[:, n, 0:HT], PS[:, 2 * s, 0:HT], g, X[:, n, 0:HT], ALU.mult, ALU.add), hold=False)
                    v(stt(X[:, n, HT:NP], PS[:, 2 * s + 1, 0:NP - HT], g, X[:, n, HT:NP], ALU.mult, ALU.add),
                      hold=False)
                    v(tt(TS[:, 0:NS], PS[:, 2 * s + 1, NP - HT:HT], MOD[:, mod + n, 1:], ALU.mult))
                    v(tt(X[:, n, NP:T], X[:, n, NP:T], TS[:, 0:NS], ALU.add), psum_free)

            dve.wait_ge(x_in, 96)
            norm_modulate("norm0", 0, MIXN)
            t = Turn("qk")
            for n in range(8):
                s = full(t)
                v(ts(two(QB[:, n, :]), halves(s), float(DK) ** -0.5 if n < 4 else 1.0, None, ALU.mult), psum_free)
            s = full(Turn("glow"))
            v(cp(two(EF[0:GR, 0:T]), halves(s, GR)), psum_free)
            v(cp(TS[:, 0:1], EPST[:, :]), glow_ready)
            t = Turn("gup")
            for n in range(4):
                s = full(t)
                v(ts(two(B[:, n, :]), halves(s), VEC[:, GBIAS + n:GBIAS + n + 1], None, ALU.add), psum_free)
            t = Turn("v")
            for q in range(QT):
                s = full(t)
                v(cp(V[:, q, :].rearrange("p (a b) -> p a b", a=2), PS[:, 2 * s:2 * s + 2, :]), psum_free)
            dve.wait_ge(softplus_ready, 1)
            v(stt(B, B, 0.0, E, ALU.min, ALU.subtract))
            v(ts(B, B, 1.0 / 16.0, None, ALU.mult))
            for h in range(GH):
                v(nv.tensor_tensor_scan(E[:, h, 0:NP], const(SCAN, NP), B[:, h, 0:NP], 0.0, ALU.mult, ALU.add),
                  hold=False)
            v.settle()
            EC = E[:, :, 0:NP].rearrange("p h (c t) -> p h c t", c=NC)
            v(cp(BM, EC[:, :, :, C // 2 - 1]), hold=False)
            v(cp(BL, EC[:, :, :, C - 1]))
            v(tt(FE, BL, BM, ALU.subtract))
            v(tt(FE[:, :, 0:NC - 1], FE[:, :, 0:NC - 1], BM[:, :, 1:NC], ALU.add))
            v(tt(EC, EC, BM.unsqueeze(3).to_broadcast([P, GH, NC, C]), ALU.subtract), decay_ready)
            dve.wait_ge(exp_ready, 1)
            v(tt(QB[:, 0:4, 0:NP], QB[:, 0:4, 0:NP], B[:, :, 0:NP], ALU.mult), decayed)
            dve.wait_ge(exp_ready, 2)
            v(tt(QB[:, 4:8, 0:NP], QB[:, 4:8, 0:NP], E[:, :, 0:NP], ALU.mult), decayed)
            late_modulation(0)
            late_modulation(1)
            clear_late_rows(2)
            t = Turn("v")
            t.n += QT
            s = full(t)
            v(cp(VS[:, :].rearrange("p (a b) -> p a b", a=2), PS[0:NS, 2 * s:2 * s + 2, :]), psum_free)
            for q in range(QT):
                dve.wait_ge(prep_full, q + 1)
                v(cp(EF[:, q * 512:(q + 1) * 512], PS[:, q % 2, :]), prep_done, hold=False)
                v(tt(AT[:, q * 256:(q + 1) * 256].rearrange("p (h t) -> p h t", h=GH),
                     PS[:, 2 + q % 2, 0:256].rearrange("p (h t) -> p h t", h=GH),
                     const(TRI, C).unsqueeze(1).to_broadcast([P, GH, C]), ALU.mult), prep_done)
            S4 = S.rearrange("p (h n) -> p h n", h=GH)
            for c in range(NC):
                dve.wait_ge(o_full, c + 1)
                kv = PS[:, 2 * (c % 2):2 * (c % 2) + 2, :].rearrange("p a (h n) -> p (a h) n", h=2)
                fe = FE[:, :, c:c + 1].to_broadcast([P, GH, DV])
                if c == 0:
                    v(tt(S4, kv, fe, ALU.mult), state_ready)
                else:
                    v(tt(S4, kv, S4, ALU.add))
                    v(tt(S4, S4, fe, ALU.mult), state_ready)
                v(cp(O[:, :, c * C:(c + 1) * C], PS[:, 4 + c % 2, :].rearrange("p (n t) -> p n t", n=8)), o_taken)
            dve.wait_ge(ks_full, 1)
            v(cp(EF[0:NS, 0:512], PS[0:NS, 6, :]))

            def key_row(b):
                if b >= 2:
                    dve.wait_ge(outer_full, b - 1)
                v(ts(EF[0:NS, 512 * (1 + b % 2):512 * (2 + b % 2)], EF[0:NS, 0:512], CONST[0:NS, ID + b:ID + b + 1],
                     None, ALU.mult), km_ready)

            key_row(0)
            for b in range(NS):
                if b + 1 < NS:
                    key_row(b + 1)
                dve.wait_ge(outer_full, b + 1)
                dve.wait_ge(st_in[b % 2], 16 * (b // 2 + 1))
                for h in range(GH):
                    st = ST[:, b % 2, h * DV:(h + 1) * DV]
                    v(stt(st, st, B[:, h, NP + b:NP + b + 1],
                          PS[:, 2 * (b % 2) + h // 2, (h % 2) * DV:(h % 2 + 1) * DV], ALU.mult, ALU.add),
                      snew_ready, hold=False)
                v.settle()
                if b % 2:
                    late_modulation(2 + b // 2)
            dve.wait_ge(os_full, NS)
            v(cp(O[:, :, NP:T], PS[:, 7, 0:64].rearrange("p (b n) -> p n b", b=NS)))
            squares(BE[:, :, :], O[:, :, :])
            t = Turn("onorm")
            for h in range(GH):
                r = normed("onorm", h)
                full(t)
                v(tt(O[:, 2 * h:2 * h + 2, :], O[:, 2 * h:2 * h + 2, :], rows(r, 2), ALU.mult), psum_free)
            t = Turn("r")
            for n in range(8):
                full(t)
                dve.wait_ge(silu_ready, n + 1)
                v(stt(O[:, n, :], O[:, n, :], VEC[:, ONORM + n % 2:ONORM + n % 2 + 1], QB[:, n, :], ALU.mult,
                      ALU.mult), psum_free)
            clear_late_rows(6)
            residual("gout", 16)

            def first_max(dst, src, top, tmp, top2):
                b = [P, 5, 4]
                v(red(top, src, AX.X, ALU.max))
                v(tt(tmp, src, top.unsqueeze(2).to_broadcast(b), ALU.is_ge))
                v(tt(tmp, tmp, CONST[:, RANK:RANK + 4].unsqueeze(1).to_broadcast(b), ALU.mult))
                v(red(top2, tmp, AX.X, ALU.max))
                v(tt(dst, tmp, top2.unsqueeze(2).to_broadcast(b), ALU.is_equal))

            def experts(l):
                norm_modulate(f"fnorm{l}", l * 48 + 24, FFNN + 8 * l)
                v(nv.memset(LOG, 0.0))
                s = full(Turn(f"route{l}"))
                v(cp(two(LOGT), halves(s, NG + NE)), routing_step)
                v(nv.memset(AC[:, 0, :], 0.0))
                dve.wait_ge(routing_full, 3 * l + 1)
                bias = BRT[:, l, :]
                v(tt(LOG[:, 0:QT, :], PS[:, 2 * s, 0:80].rearrange("p (q n) -> p q n", q=QT),
                     bias.unsqueeze(1).to_broadcast([P, QT, 20]), ALU.add))
                v(tt(LOG[0:NS, QT, :], PS[0:NS, 2 * s, 80:100], bias[0:NS, :], ALU.add), psum_free)
                b = [P, 5, 4]
                first_max(OHG, LOG[:, :, 0:4], M1, TMP, M2)
                v(tt(GX, LOG[:, :, 0:4], M1.unsqueeze(2).to_broadcast(b), ALU.subtract), route_exp_in)
                le = LOG[:, :, 4:20].rearrange("p q (g e) -> p q g e", g=NG)
                v(tt(SEL, le, OHG.unsqueeze(3).to_broadcast([P, 5, 4, 4]), ALU.mult))
                v(red(LE, SEL.rearrange("p q g e -> p q e g"), AX.X, ALU.add))
                first_max(OH1, LE, M1, TMP, M2)
                v(stt(LE, OH1, -BIG, LE, ALU.mult, ALU.add))
                first_max(OH2, LE, M3, TMP, M2)
                v(tt(X2, M3, M1, ALU.subtract), route_exp_in)
                if l == 0:
                    late_modulation(6)
                dve.wait_ge(route_exp, 2 * l + 2)
                b16 = [P, 5, NG, NEG]

                def outer(dst, e):
                    v(tt(dst.rearrange("p q (g e) -> p q g e", g=NG), e.unsqueeze(2).to_broadcast(b16),
                         OHG.unsqueeze(3).to_broadcast(b16), ALU.mult))

                outer(AK[0], OH1)
                outer(AK[1], OH2)
                v(tt(AS, AK[0], AK[1], ALU.add))
                for q in range(1, 5):
                    v(tt(AC[:, q, :], AC[:, q - 1, :], AS[:, q - 1, :], ALU.add), routing_step if q == QT else None)
                v(red(M1, GX, AX.X, ALU.add))
                v(stt(M2, X2, 1.0, M1, ALU.add, ALU.mult))
                v(nv.reciprocal(W1, M2))
                v(tt(W2, W1, X2, ALU.mult))
                for k in range(2):
                    v(ts(M1, CONST[:, TOK:TOK + 5], float(T * k), None, ALU.add))
                    v(tt(RK[k][:, :, 0, :], AK[k], M1.unsqueeze(2).to_broadcast([P, 5, NE]), ALU.mult))
                    v(cp(RK[k][:, :, 1, :], AK[k]))
                dve.wait_ge(routing_full, 3 * l + 2)
                pos = PS[:, 2 * s, 0:5 * NE].rearrange("p (q e) -> p q e", q=5)
                for k in range(2):
                    v(tt(ATMP, AK[k], pos, ALU.mult))
                    v(red(PK[k], ATMP, AX.X, ALU.add))

                def one_hot_places(c, done):
                    for k in range(2):
                        v(ts(PC[k], PK[k], float(-CAP * c), None, ALU.add))
                        if CAP < P:
                            v(ts(M1, PC[k], float(CAP), 1024.0, ALU.is_ge, ALU.mult))
                            v(tt(PC[k], PC[k], M1, ALU.add))
                        for q in range(5):
                            v(ts(OPK[:, k, q, :], const(IOTA), PC[k][:, q:q + 1], None, ALU.is_equal), hold=False)
                        v.settle()
                    v(cp(TS[:, 0:1], EPST[:, :]), done)

                def index_rows(c, bank, done):
                    v(ts(ATMP[:, 0, :], PS[:, bank, NE:2 * NE], -NOROW, NOROW, ALU.mult, ALU.add))
                    v(tt(IDX[:, c, :], ATMP[:, 0, :], PS[:, bank, 0:NE], ALU.add), done)

                one_hot_places(0, rows_ready)
                dve.wait_ge(routing_full, 3 * l + 3)
                v(red(M1[0:1, 0:1], PS[0:1, 2 * s + 1, 0:NE], AX.X, ALU.max))
                v(cp(FLAG[:, l:l + 1], M1[0:1, 0:1]), flag_ready)
                if l == 0:
                    late_modulation(7)
                dve.wait_ge(idx_full, l + 1)
                index_rows(0, 2 * s, idx_ready)
                if l == 0:
                    late_modulation(8)

                base = NE * l

                def turned_rows(i, e):
                    dve.wait_ge(xt_full, i * 2 + (base + e + 1))
                    v(cp(XT[e].rearrange("p (a k) n -> p a (k n)", a=2), PS[:, 0:2, :]), xt_ready, hold=False)

                def hidden(i, e):
                    dve.wait_ge(act_gated, i * 2 + (base + e + 1))
                    v(tt(HID[e], SG[e], PS[:, 2 + e, FF:2 * FF], ALU.mult), hid_ready, hold=False)

                def output(i, e, first=False):
                    dve.wait_ge(down_full, i * 2 + (base + e + 1))
                    if not first:
                        dve.wait_ge(y_out[e], i * 16 + (128 * l))
                    v(cp(YB[e][:, 0:512], PS[:, 5, :]), y_dve, hold=False)

                def step(i, e, first=False):
                    turned_rows(i, e)
                    hidden(i, e)
                    output(*((i, 0) if e else (i - 1, 1)), first=first)

                turned_rows(0, 0)
                hidden(0, 0)
                step(0, 1, True)
                step(1, 0, True)
                step(1, 1)
                with v.loop(NE // 2 - 2, [(xt_ready, 2), (hid_ready, 2), (y_dve, 2)]) as j:
                    i = j + 2
                    step(i, 0)
                    step(i, 1)
                output(NE // 2 - 1, 1)
                v.settle()

                o = ov[l]
                most = dve.value_load(FLAG[0:1, l:l + 1], min_val=0, max_val=T)
                with dve.If(most > CAP):
                    w = Order(dve, o["table"])
                    for c in range(NCH - 1):
                        for k in range(2):
                            w(ts(PC[k], PK[k], float(-CAP * (c + 1)), None, ALU.add), more_step[l])
                            if CAP < P:
                                w(ts(M1, PC[k], float(CAP), 1024.0, ALU.is_ge, ALU.mult), more_step[l])
                                w(tt(PC[k], PC[k], M1, ALU.add), more_step[l])
                            for q in range(5):
                                w(ts(OPK[:, k, q, :], const(IOTA), PC[k][:, q:q + 1], None, ALU.is_equal),
                                  more_step[l])
                        w(cp(TS[:, 0:1], EPST[:, :]), o["table"])
                        dve.wait_ge(o["table_full"], c + 1)
                        w(ts(ATMP[:, 0, :], PS[:, 7, NE:2 * NE], -NOROW, NOROW, ALU.mult, ALU.add), more_step[l])
                        w(tt(IDX[:, c + 1, :], ATMP[:, 0, :], PS[:, 7, 0:NE], ALU.add), more_step[l])
                    for b in range(2):
                        dve.wait_ge(y_out[b], 8 * NE * (l + 1))
                    dve.wait_ge(y_act, NE * (l + 1))
                    with dve.Fori(0, NE) as e:
                        for c in range(NCH - 1):
                            n = e * (NCH - 1) + (c + 1)
                            cp(IDXO[:, :], IDX[:, c + 1, bass.ds(e, 1)]).then_inc(o["go"], 1)
                            dve.wait_ge(o["xt_full"], n)
                            cp(XT[0].rearrange("p (a k) n -> p a (k n)", a=2), PS[:, 0:2, :]).then_inc(o["xt"], 1)
                            dve.wait_ge(o["silu"], n)
                            tt(HID[0], SG[0], PS[:, 2, FF:2 * FF], ALU.mult).then_inc(o["hid"], 1)
                            dve.wait_ge(o["ht_full"], n)
                            cp(HT_[0], PS[:, 4, 0:256]).then_inc(o["ht"], 1)
                            dve.wait_ge(o["down_full"], n)
                            cp(YB[0].rearrange("p (a n) -> p a n", a=2), PS[:, 5:7, :]).then_inc(o["y"], 1)
                            dve.wait_ge(o["out"], e * (16 * (NCH - 1)) + 16 * (c + 1))

                mod = l * 48 + 40
                TMPX = OF[:, 2048:3072].rearrange("p (k n) -> p k n", k=KD)

                def mix(q):
                    m, y = rows_of(q), PAIR[q % 2]
                    dve.wait_ge(weighted, 5 * l + q + 1)
                    v(stt(y[0][0:m, :], y[1][0:m, :], W2[0:m, q:q + 1], y[0][0:m, :], ALU.mult, ALU.add), mixed,
                      hold=False)

                if l == 0:
                    clear_late_rows(9)
                    for n in (9, 10, 11):
                        late_modulation(n)
                mix(0)
                for q in range(5):
                    m, b = rows_of(q), q % 2
                    if q + 1 < 5:
                        mix(q + 1)
                    dve.wait_ge(mixed_full, 5 * l + q + 1)
                    src = PS[:, 2 * b:2 * b + 2, :].rearrange("p a (k n) -> p (a k) n", k=4)[:, :, 0:m]
                    if q < QT:
                        g = MOD[:, mod:mod + KD, 0:1].to_broadcast([P, KD, m])
                    else:
                        g = MOD[:, mod:mod + KD, 1:]
                    v(tt(TMPX[:, :, 0:m], src, g, ALU.mult), pair_added)
                    x = X[:, :, q * P:q * P + m]
                    v(tt(x, x, TMPX[:, :, 0:m], ALU.add), y_ready if l else None)

            experts(0)

            stream_squares()
            r = normed("kvnorm")
            full(Turn("kvnorm"))
            for k in range(KD):
                v(stt(H[:, k, :], X[:, k, :], VEC[:, KVIN + k:KVIN + k + 1], r, ALU.mult, ALU.mult), h_ready, hold=False)
            v(cp(TS[:, 0:1], EPST[:, :]), psum_free)
            norm_modulate(None, 48, MIXN + 8, QB, r)
            t = Turn("dkv")
            for n in range(3):
                s = full(t)
                v(cp(two(CKV[:, n, :]), halves(s)), psum_free)
            squares(E[:, 0:2, :], CKV[:, 0:2, :])
            t = Turn("dq")
            for n in range(3):
                s = full(t)
                v(cp(two(B[:, n, :]), halves(s)), psum_free)
            squares(H[:, 0:3, :], B[:, 0:3, :])
            r = normed("ckvnorm")
            full(Turn("ckvnorm"))
            v(tt(CKV[:, 0:2, :], CKV[:, 0:2, :], rows(r, 2), ALU.mult), psum_free)
            s = full(Turn("krot"))
            v(tt(two(E[:, 3, :]), halves(s), two(const2(SIN, T)), ALU.mult), psum_free)
            r = normed("cqnorm")
            full(Turn("cqnorm"))
            v(tt(B[:, 0:3, :], B[:, 0:3, :], rows(r, 3), ALU.mult), psum_free)
            for k in range(2):
                v(ts(B[:, k, :], B[:, k, :], VEC[:, QLAT + k:QLAT + k + 1], None, ALU.mult), hold=False)
            v(ts(B[:, 2, :], B[:, 2, :], VEC[:, QLAT + 2:QLAT + 3], None, ALU.mult), lat_ready)
            v(ts(CKV[:, 0, :], CKV[:, 0, :], VEC[:, KVLAT:KVLAT + 1], None, ALU.mult), hold=False)
            v(ts(CKV[:, 1, :], CKV[:, 1, :], VEC[:, KVLAT + 1:KVLAT + 2], None, ALU.mult), lat_ready)
            v(tt(CKV[:, 2, :], CKV[:, 2, :], const2(COS, T), ALU.mult))
            v(tt(CKV[:, 2, :], CKV[:, 2, :], E[:, 3, :], ALU.add), kr_ready)
            t = Turn("uq")
            for n in range(6):
                s = full(t)
                v(cp(two(QB[:, n, :]), halves(s)), psum_free)
            t = Turn("qrot")
            for j in range(2):
                s = full(t)
                v(tt(two(E[:, j, :]), halves(s), two(const2(SIN, T)), ALU.mult), psum_free)
            v(tt(QB[:, 4:6, :], QB[:, 4:6, :], rows(const2(COS, T), 2), ALU.mult))
            v(tt(QB[:, 4:6, :], QB[:, 4:6, :], E[:, 0:2, :], ALU.add))
            squares(H[:, 0:6, :], QB[:, 0:6, :])
            t = Turn("qss")
            for n in range(6):
                r = normed("qss", n)
                full(t)
                g = QNN if n < 4 else QNR
                v(stt(QB[:, n, :], QB[:, n, :], VEC[:, g:g + 1], r, ALU.mult, ALU.mult), psum_free)
            t = Turn("uk")
            for n in range(4):
                s = full(t)
                v(cp(two(O[:, n, :]), halves(s)), psum_free)
            v(tt(H[:, 0:4, :], O[:, 0:4, :], O[:, 0:4, :], ALU.mult))
            squares(H[:, 4, :], CKV[:, 2, :])
            t = Turn("uv")
            for q in range(QT):
                s = full(t)
                v(cp(VP[:, q, :], PS[:, 2 * s, :]), psum_free)
            t = Turn("kss")
            for n in range(6):
                r = normed("kss", n)
                full(t)
                g, src = (KNN, O[:, n, :]) if n < 4 else (KNR, CKV[:, 2, :])
                v(stt(O[:, n, :], src, VEC[:, g:g + 1], r, ALU.mult, ALU.mult), psum_free)
            v(ts(QP[:, 0:4, :], QB[:, 0:4, NP:T], VEC[:, KNN:KNN + 1], None, ALU.mult), hold=False)
            v(ts(QP[:, 4:6, :], QB[:, 4:6, NP:T], VEC[:, KNR:KNR + 1], None, ALU.mult), qp_ready)
            v(stt(PR, QB[:, 0:6, NP:T], SCALE * QK, O[:, 0:6, NP:T], ALU.mult, ALU.mult), qp_ready)
            v(nv.memset(NEW, -BIG))
            dve.wait_ge(ql_full, 1)
            for r in range(2):
                for u in range(2):
                    v(ts(QL[:, r, :, u:MH:2], PS[:, 3 * u, r * 32:(r + 1) * 32].rearrange("p (h s) -> p s h", h=4),
                         SCALE, None, ALU.mult), ql_ready)
            v(ts(QRS, PS[0:ROPE, 1, 0:64].rearrange("p (h s) -> p s h", h=MH), SCALE, None, ALU.mult), ql_ready)
            v(cp(NEW[0:1, :].rearrange("p (s h) -> p s h", s=NS), PS[0:1, 2, 0:64].rearrange("p (h s) -> p s h", h=MH)),
              ql_ready)
            for n in range(PSL):
                v(cp(TS[:, n:n + 1], EPST[:, :]), page_used)

            def mask_max(n):
                q, b = n // MH, n % 2
                dve.wait_ge(sc_full, n + 1)
                diag = PS[:, b, q * P:(q + 1) * P]
                v(tt(diag, diag, const2(CAUS), ALU.add))
                v(red(NM[:, b:b + 1], PS[:, b, 0:(q + 1) * P], AX.X, ALU.max))
                v(ts(NM[:, b:b + 1], NM[:, b:b + 1], -SCALE, None, ALU.mult), negmax_ready)

            def page_sums(g):
                dve.wait_ge(page_sq, g + 1)
                v(red(SSQ[:, g * MH:(g + 1) * MH], SQP[:, g % 4, :].rearrange("p (h d) -> p h d", h=MH),
                      AX.X, ALU.add), page_used, hold=False)
                if g % PSL == PSL - 1:
                    m = g // PSL
                    dve.wait_ge(kn_full, g + 1)
                    v(cp(SC[:, m * 64:(m + 1) * 64], PS[:, 3 + 2 * (m % 2), 0:PSL * MH]), scores_taken,
                      hold=False)

            mask_max(0)
            for n in range(QT * MH):
                q, h, b = n // MH, n % MH, n % 2
                nk = (q + 1) * P
                if n + 1 < QT * MH:
                    if n >= 1:
                        dve.wait_ge(exp_done, n)
                    mask_max(n + 1)
                dve.wait_ge(exp_done, n + 1)
                v(nv.reciprocal(LN[:, b:b + 1], LN[:, b:b + 1]))
                pb = EF[:, 512 * b:512 * b + nk]
                v(ts(pb, pb, LN[:, b:b + 1], None, ALU.mult), p_ready)
                page_sums(4 * n)
                dve.wait_ge(pt_full, n + 1)
                if n >= 2:
                    dve.wait_ge(pv_full, n - 1)
                v(cp(EF[:, 1024 + 512 * b:1024 + 512 * b + nk], PS[:, 2, 0:nk]), pt_ready)
                page_sums(4 * n + 1)
                page_sums(4 * n + 2)
                dve.wait_ge(pv_full, n + 1)
                lo = MV * (h % 2)
                v(cp(B[lo:lo + MV, h // 2, q * P:(q + 1) * P], PS[lo:lo + MV, 4, 0:P]), pv_done)
                page_sums(4 * n + 3)
            v.settle()
            v(tt(SSQ.rearrange("p (n h) -> p n h", h=MH), SSQ.rearrange("p (n h) -> p n h", h=MH),
                 KRS.unsqueeze(2).to_broadcast([P, NS * NPG, MH]), ALU.add), ssq_ready)
            dve.wait_ge(krstd_ready, 1)
            v(tt(SC, SC, SSQ, ALU.mult))
            SC4 = SC.rearrange("p (s g h) -> p s g h", s=NS, g=NPG)
            v(red(MX.rearrange("p (s h) -> p s h", s=NS), SC4.rearrange("p s g h -> p s h g"), AX.X, ALU.max))
            v(tt(MX, MX, NEW, ALU.max), stat_ready)
            dve.wait_ge(stat_full, 1)
            v(red(MC, PS[0:64, 6, 0:P], AX.X, ALU.max))
            v(ts(DG, ident(64, 64), MC, None, ALU.mult), stat_ready)
            dve.wait_ge(stat_full, 2)
            v(cp(MX, PS[:, 7, 0:64]))
            v(tt(NEW, NEW, MX, ALU.subtract))
            v(tt(SC4, SC4, MX.rearrange("p (s h) -> p s h", s=NS).unsqueeze(2).to_broadcast([P, NS, NPG, MH]),
                 ALU.subtract), shifted)
            dve.wait_ge(p_exp, 1)
            v(red(LS.rearrange("p (s h) -> p s h", s=NS), SC4.rearrange("p s g h -> p s h g"), AX.X, ALU.add))
            v(tt(LS, LS, NEW, ALU.add), stat_ready)
            dve.wait_ge(stat_full, 3)
            v(nv.reciprocal(RLS, PS[:, 6, 0:64]))
            v(cp(PNB, PS[:, 6, 64:128]))

            def prompt_residual(n):
                dve.wait_ge(mout_full, n + 1)
                v(stt(X[:, n, 0:NP], PS[:, 4 + n % 2, :], MOD[:, 64 + n, 0:1], X[:, n, 0:NP], ALU.mult, ALU.add),
                  mout_taken, hold=False)

            prompt_residual(0)
            prompt_residual(1)
            for i in range(0, NS, 2):
                dve.wait_ge(cpage_used, NPG * (i + 2))
                v(cp(ACC[:, i:i + 2, :, :].rearrange("p s r n -> p (s r n)"), PS[0:MH, i // 2, :]), acc_taken)
                for n in (i + 2, i + 3):
                    if n < KD:
                        prompt_residual(n)
            v.settle()
            dve.wait_ge(acc_full, 1)
            P3 = PNB.rearrange("p (s h) -> p s h", s=NS)
            M3X = MX.rearrange("p (s h) -> p s h", s=NS)
            for r in range(2):
                v(tt(M3X, P3, CKV[:, r, NP:T].unsqueeze(2).to_broadcast([P, NS, MH]), ALU.mult))
                v(tt(OL[:, r, :, :], PS[:, 5, r * 64:(r + 1) * 64].rearrange("p (s h) -> p s h", s=NS), M3X, ALU.add))
                v(tt(OL[:, r, :, :], OL[:, r, :, :], RLS.rearrange("p (s h) -> p s h", s=NS), ALU.mult),
                  olat_ready if r else None)
            dve.wait_ge(osam_full, 1)
            v(cp(B[:, :, NP:T], PS[:, 4, 0:32].rearrange("p (k s) -> p k s", k=4)), attn_ready)
            s = full(Turn("mout"))
            xs, ts8 = X[:, :, NP:T], AT[:, 0:KD * NS].rearrange("p (n s) -> p n s", n=KD)
            v(tt(ts8, PS[:, 2 * s, 0:KD * NS].rearrange("p (n s) -> p n s", n=KD), MOD[:, 64:64 + KD, 1:], ALU.mult),
              psum_free)
            v(tt(xs, xs, ts8, ALU.add))
            experts(1)


def tiles(w, n):
    k, m = w.shape
    return w.reshape(k // P, P, m // n, n).transpose(2, 1, 0, 3).reshape(m // n, P, k // P * n)


def turned(x):
    return x.T.reshape(x.shape[1] // P, P, x.shape[0]).transpose(1, 0, 2)


def column(w):
    return w.reshape(-1, P).T


def kernel(**inputs):
    import concourse.bacc as bacc
    from concourse.bass_utils import run_bass_kernel_spmd

    w = {k: np.asarray(a) for k, a in inputs.items()}
    const, const2 = constant_tables()
    gw = w["gla_w_in"][0]
    uq = w["mla_w_uq"][0].reshape(QR, MH, QK)
    uq = np.concatenate([uq[:, :, :NOPE].reshape(QR, -1), uq[:, :, NOPE:].reshape(QR, -1)], axis=1)
    dkv = w["kv_w_dkv"]
    dkv = np.concatenate([dkv[:, :KVR]] + [dkv[:, KVR:]] * 4, axis=1)
    uk, uv = w["kv_w_uk"].reshape(KVR, -1), w["kv_w_uv"].reshape(KVR, -1)
    ukv = np.concatenate([tiles(uk, 512)[0], tiles(uv, 512)[0], tiles(np.ascontiguousarray(uk.T), 256)[0]], axis=1)
    vec = np.concatenate(
        [column(w["mix_norm"][l]) for l in range(2)] + [column(w["ffn_norm"][l]) for l in range(2)]
        + [column(w["ada_b"].reshape(-1)), column(w["gla_b_gate"][0]), column(w["gla_out_norm"][0]),
           column(w["kv_in_norm"]), column(w["mla_q_lat_norm"][0]), column(w["kv_lat_norm"])]
        + [np.tile(g[a:b], P // (b - a))[:, None] for g in (w["mla_q_norm"][0], w["kv_k_norm"])
           for a, b in ((0, NOPE), (NOPE, QK))], axis=1)
    cache, cache_kr = w["cache_ckv"], w["cache_krope"]
    npool = cache.shape[0]
    ct = cache.reshape(npool, PAGE, 2, P).transpose(0, 3, 2, 1).reshape(npool, P, KVR)
    arrays = {
        "x": turned(np.concatenate([w["x_prompt"][0], w["x_sample"][:, 0]], axis=0)),
        "c": turned(np.concatenate([w["c_prompt"], w["c_sample"]], axis=0)),
        "const": const, "const2": const2, "vec": vec,
        "ada": np.stack([tiles(w["ada_w"][l], 512) for l in range(2)]).reshape(6, SLOTS, P, 4096),
        "gla": np.concatenate([tiles(gw[:, a:b], 512) for a, b in
                               ((0, 512), (512, 1024), (1024, 2048), (2048, 3072))] + [tiles(w["gla_w_out"][0], 512)]),
        "gate_low": tiles(gw[:, 3072:], GR)[0].reshape(P, KD, GR),
        "gate_up": w["gla_w_gate_up"][0],
        "router": np.stack([tiles(np.concatenate([w["moe_w_group"][l], w["moe_w_router"][l]], axis=1), 20)[0]
                            .reshape(P, KD, 20) for l in range(2)], axis=1),
        "router_b": np.concatenate([w["moe_b_group"], w["moe_b_router"]], axis=1),
        "moe_gu": np.stack([np.stack([tiles(np.concatenate([w["moe_w_gate"][l, e], w["moe_w_up"][l, e]], axis=1),
                                            512)[0] for e in range(NE)]) for l in range(2)])
        .reshape(2, NE // 2, 2, P, 4096),
        "moe_dn": np.stack([np.stack([tiles(w["moe_w_down"][l, e], D)[0] for e in range(NE)]) for l in range(2)])
        .reshape(2, NE // 2, 2, P, 2048),
        "dkv": tiles(dkv, QR)[0], "dq": tiles(w["mla_w_dq"][0], QR)[0], "uq": tiles(uq, MH * QK)[0], "ukv": ukv,
        "mwo": tiles(w["mla_w_out"][0], D)[0],
        "state_in": w["state_gla"][0].transpose(0, 2, 1, 3).reshape(NS, P, GH * DV),
        "cache_t": np.concatenate([ct, cache_kr], axis=2),
        "cache_kr": cache_kr.transpose(0, 2, 1),
        "cache": cache,
        "pages": w["page_table"].reshape(1, -1),
    }
    outs = {"y": (P, KD, T), "state_p": (P, GH * DV), "state_s": (NS, P, GH * DV), "ckv": (P, 2, T), "kr": (ROPE, T)}
    nc = bacc.Bacc("TRN2", target_bir_lowering=False, num_devices=1)
    io, args = {}, {}
    for name, a in arrays.items():
        a = np.ascontiguousarray(a)
        args[f"in_{name}"] = a
        io[name] = nc.dram_tensor(f"in_{name}", a.shape, mybir.dt.from_np(a.dtype), kind="ExternalInput").ap()
    for name, shape in outs.items():
        io[name] = nc.dram_tensor(f"out_{name}", shape, F32, kind="ExternalOutput").ap()
    io["rows"] = nc.dram_tensor("rows", (2 * T, D), F32, kind="Internal").ap()
    io["outs"] = nc.dram_tensor("outs", (2 * T, D), F32, kind="Internal").ap()
    io["npool"] = npool
    trunk_program(nc, io)
    got = run_bass_kernel_spmd(nc, [args], core_ids=[0]).results[0]

    def back(a):
        return np.ascontiguousarray(a.transpose(2, 1, 0).reshape(T, -1))

    y, ckv, kr = back(got["out_y"]), back(got["out_ckv"]), np.ascontiguousarray(got["out_kr"].T)
    sp = got["out_state_p"].reshape(P, GH, DV).transpose(1, 0, 2)[None, None]
    ss = got["out_state_s"].reshape(NS, P, GH, DV).transpose(0, 2, 1, 3)[None]
    return (y[None, :NP], y[NP:, None], np.ascontiguousarray(sp), np.ascontiguousarray(ss),
            ckv[None, :NP], kr[None, :NP], ckv[NP:, None], kr[NP:, None])
```
